# Optimizing a Trainium2 kernel written in Bass

```python
import jax, jax.numpy as jnp
from jax import lax
import numpy as np
import math

D_MODEL = 2048
BATCH = 1
SEQ = 256
DEPTH = 1

FOX_HEAD_DIM = 128
FOX_WIDTH = D_MODEL // 2
FOX_HEADS = FOX_WIDTH // FOX_HEAD_DIM
RWKV_HEAD_DIM = 64
RWKV_WIDTH = D_MODEL // 2
RWKV_HEADS = RWKV_WIDTH // RWKV_HEAD_DIM
DECAY_LORA = max(32, int(round(D_MODEL ** 0.5 * 1.8 / 32)) * 32)
AAA_LORA = max(32, int(round(D_MODEL ** 0.5 * 1.8 / 32)) * 32)
Q_BLOCK = 128
RMS_EPS = 1e-6
GN_EPS = 64e-5
L2_EPS = 1e-12

FOX_SIZES = (FOX_WIDTH, FOX_WIDTH, FOX_WIDTH, FOX_WIDTH, FOX_HEADS)
RWKV_SIZES = (RWKV_WIDTH, RWKV_WIDTH, RWKV_WIDTH, RWKV_WIDTH, DECAY_LORA, AAA_LORA)
FOX_COLS = sum(FOX_SIZES)
RWKV_COLS = sum(RWKV_SIZES)
IN_COLS = FOX_COLS + RWKV_COLS + 2 * D_MODEL


def _split(u, sizes):
    idx = [int(i) for i in np.cumsum(sizes)[:-1]]
    return jnp.split(u, idx, axis=-1)

def _rmsnorm(x, g):
    xf = x.astype(jnp.float32)
    y = xf * lax.rsqrt(jnp.mean(xf * xf, axis=-1, keepdims=True) + RMS_EPS)
    return (y * g.astype(jnp.float32)).astype(x.dtype)

def _token_shift(u, mu):
    prev = jnp.pad(u, ((0, 0), (1, 0), (0, 0)))[:, :-1]
    return u + (prev - u) * mu

def _fox_attention(q, k, v, log_f):
    c = jnp.cumsum(log_f, axis=-1)
    T = q.shape[2]
    scale = FOX_HEAD_DIM ** -0.5
    outs = []
    for i in range(T // Q_BLOCK):
        s0, e = i * Q_BLOCK, (i + 1) * Q_BLOCK
        qb, kb, vb = q[:, :, s0:e], k[:, :, :e], v[:, :, :e]
        logits = (jnp.einsum('bhqd,bhkd->bhqk', qb, kb) * scale
                  + c[:, :, s0:e, None] - c[:, :, None, :e])
        causal = jnp.arange(e)[None, :] <= jnp.arange(s0, e)[:, None]
        logits = jnp.where(causal, logits, -jnp.inf)
        p = jax.nn.softmax(logits, axis=-1)
        outs.append(jnp.einsum('bhqk,bhkd->bhqd', p, vb))
    return jnp.concatenate(outs, axis=2)

def _rwkv7_scan(r, decay, k, v, kk, b):
    B, T, H, N = r.shape
    S0 = jnp.zeros((B, H, N, N), jnp.float32)
    xs = tuple(jnp.moveaxis(t, 1, 0) for t in (r, decay, k, v, kk, b))

    def step(S, inp):
        r_t, w_t, k_t, v_t, kk_t, b_t = inp
        sa = jnp.einsum('bhvk,bhk->bhv', S, -kk_t)
        S = (S * w_t[:, :, None, :] + sa[..., None] * b_t[:, :, None, :]
             + v_t[..., None] * k_t[:, :, None, :])
        y = jnp.einsum('bhvk,bhk->bhv', S, r_t)
        return S, y

    _, ys = lax.scan(step, S0, xs)
    return jnp.moveaxis(ys, 0, 1)

def _hybrid_layer(x, norm_gain, w_in, fox_forget_bias, rwkv_shift_mix, rwkv_w0, rwkv_w2,
                  rwkv_a0, rwkv_a2, rwkv_k_k, rwkv_k_a, rwkv_r_k, rwkv_ln_w, rwkv_ln_b,
                  w_proj_fox, w_proj_rwkv, w_out):
    B, T, _ = x.shape
    f32 = jnp.float32
    h = _rmsnorm(x, norm_gain)
    u = h @ w_in
    u_fox, u_rwkv, g_a, g_b = _split(u, (FOX_COLS, RWKV_COLS, D_MODEL, D_MODEL))

    q, k, v, z_a, f_logit = _split(u_fox.astype(f32), FOX_SIZES)
    to_heads = lambda t: t.reshape(B, T, FOX_HEADS, FOX_HEAD_DIM).transpose(0, 2, 1, 3)
    log_f = jax.nn.log_sigmoid(f_logit + fox_forget_bias.astype(f32)).transpose(0, 2, 1)
    o_a = _fox_attention(to_heads(q), to_heads(k), to_heads(v), log_f)
    o_a = o_a.transpose(0, 2, 1, 3).reshape(B, T, FOX_WIDTH) * jax.nn.silu(z_a)

    u_rwkv = _token_shift(u_rwkv.astype(f32), rwkv_shift_mix.astype(f32))
    r, kr, vr, z_b, w_down, a_down = _split(u_rwkv, RWKV_SIZES)
    w = -jax.nn.softplus(-(rwkv_w0.astype(f32) + jnp.tanh(w_down) @ rwkv_w2.astype(f32))) - 0.5
    decay = jnp.exp(-jnp.exp(w))
    a = jax.nn.sigmoid(rwkv_a0.astype(f32) + a_down @ rwkv_a2.astype(f32))
    heads = lambda t: t.reshape(B, T, RWKV_HEADS, RWKV_HEAD_DIM)
    kk = heads(kr * rwkv_k_k.astype(f32))
    kk = kk / jnp.maximum(jnp.sqrt(jnp.sum(kk * kk, axis=-1, keepdims=True)), L2_EPS)
    kr = kr * (1.0 + (a - 1.0) * rwkv_k_a.astype(f32))
    rh, kh, vh, ah = heads(r), heads(kr), heads(vr), heads(a)
    y = _rwkv7_scan(rh, heads(decay), kh, vh, kk, kk * ah)
    mu = jnp.mean(y, axis=-1, keepdims=True)
    var = jnp.mean(jnp.square(y - mu), axis=-1, keepdims=True)
    y = ((y - mu) * lax.rsqrt(var + GN_EPS)).reshape(B, T, RWKV_WIDTH)
    y = y * rwkv_ln_w.astype(f32) + rwkv_ln_b.astype(f32)
    bonus = jnp.sum(rh * kh * rwkv_r_k.astype(f32), axis=-1, keepdims=True) * vh
    o_b = (y + bonus.reshape(B, T, RWKV_WIDTH)) * jax.nn.silu(z_b)

    o_a = o_a.astype(x.dtype) @ w_proj_fox
    o_b = o_b.astype(x.dtype) @ w_proj_rwkv
    m = jax.nn.sigmoid(g_a) * o_a + jax.nn.sigmoid(g_b) * o_b
    return x + m @ w_out

def first_inputs(seed: int = 0) -> dict:
    key = jax.random.key(seed)
    ks = jax.random.split(key, 20)
    n = jax.random.normal
    L, D = DEPTH, D_MODEL
    return {
        "x": n(ks[0], (BATCH, SEQ, D), jnp.float32),
        "norm_gain": 1.0 + 0.05 * n(ks[1], (L, D), jnp.float32),
        "w_in": n(ks[2], (L, D, IN_COLS), jnp.float32) * D ** -0.5,
        "fox_forget_bias": 3.0 + 0.5 * n(ks[3], (L, FOX_HEADS), jnp.float32),
        "rwkv_shift_mix": jax.random.uniform(ks[4], (L, RWKV_COLS), jnp.float32),
        "rwkv_w0": jax.random.uniform(ks[5], (L, RWKV_WIDTH), jnp.float32, -6.5, -1.5),
        "rwkv_w2": n(ks[6], (L, DECAY_LORA, RWKV_WIDTH), jnp.float32) * 0.5 * DECAY_LORA ** -0.5,
        "rwkv_a0": 0.1 * n(ks[7], (L, RWKV_WIDTH), jnp.float32),
        "rwkv_a2": n(ks[8], (L, AAA_LORA, RWKV_WIDTH), jnp.float32) * AAA_LORA ** -0.5,
        "rwkv_k_k": 0.85 + 0.05 * n(ks[9], (L, RWKV_WIDTH), jnp.float32),
        "rwkv_k_a": 1.0 + 0.05 * n(ks[10], (L, RWKV_WIDTH), jnp.float32),
        "rwkv_r_k": -0.04 + 0.02 * n(ks[11], (L, RWKV_HEADS, RWKV_HEAD_DIM), jnp.float32),
        "rwkv_ln_w": 1.0 + 0.05 * n(ks[12], (L, RWKV_WIDTH), jnp.float32),
        "rwkv_ln_b": 0.02 * n(ks[13], (L, RWKV_WIDTH), jnp.float32),
        "w_proj_fox": n(ks[14], (L, FOX_WIDTH, D), jnp.float32) * FOX_WIDTH ** -0.5,
        "w_proj_rwkv": n(ks[15], (L, RWKV_WIDTH, D), jnp.float32) * RWKV_WIDTH ** -0.5,
        "w_out": n(ks[16], (L, D, D), jnp.float32) * D ** -0.5,
        "final_norm_gain": 1.0 + 0.05 * n(ks[17], (D,), jnp.float32),
    }

def first_block(x, norm_gain, w_in, fox_forget_bias, rwkv_shift_mix, rwkv_w0, rwkv_w2,
              rwkv_a0, rwkv_a2, rwkv_k_k, rwkv_k_a, rwkv_r_k, rwkv_ln_w, rwkv_ln_b,
              w_proj_fox, w_proj_rwkv, w_out, final_norm_gain):
    h = x
    for l in range(DEPTH):
        h = _hybrid_layer(h, norm_gain[l], w_in[l], fox_forget_bias[l], rwkv_shift_mix[l],
                          rwkv_w0[l], rwkv_w2[l], rwkv_a0[l], rwkv_a2[l], rwkv_k_k[l],
                          rwkv_k_a[l], rwkv_r_k[l], rwkv_ln_w[l], rwkv_ln_b[l],
                          w_proj_fox[l], w_proj_rwkv[l], w_out[l])
    return _rmsnorm(h, final_norm_gain)


MLA_NOPE = 128
MLA_ROPE = 64
MLA_V = 128
MLA_HEADS = D_MODEL // MLA_V
MLA_Q_RANK = 768
MLA_KV_RANK = 512
MLA_QK = MLA_NOPE + MLA_ROPE
ROPE_THETA = 10000.0
SWA_HEAD_DIM = 64
SWA_HEADS = D_MODEL // SWA_HEAD_DIM
SWA_KV_HEADS = 4
SWA_GROUP = SWA_HEADS // SWA_KV_HEADS
WINDOW = 128
BLOCK = 128
REL_BUCKETS = 32
REL_MAX_DIST = 128
D_FF = 5632
CONV_WIDTH = 3
EPS = 1e-6
NEG = -1e30

MLA_IN = MLA_Q_RANK + MLA_KV_RANK + MLA_ROPE
SWA_Q = SWA_HEADS * SWA_HEAD_DIM
SWA_KV = SWA_KV_HEADS * SWA_HEAD_DIM
N_BRANCH = 2
IN_COLS_2 = MLA_IN + SWA_Q + 2 * SWA_KV + N_BRANCH * D_MODEL


def rms_norm(x, g):
    xf = x.astype(jnp.float32)
    y = xf * lax.rsqrt(jnp.mean(xf * xf, axis=-1, keepdims=True) + EPS)
    return (y * g.astype(jnp.float32)).astype(x.dtype)

def rope_tables(seq):
    pos = jnp.arange(seq, dtype=jnp.float32)
    inv = ROPE_THETA ** (-jnp.arange(0, MLA_ROPE, 2, dtype=jnp.float32) / MLA_ROPE)
    ang = pos[:, None] * inv[None, :]
    ang = jnp.concatenate([ang, ang], axis=-1)
    return jnp.cos(ang), jnp.sin(ang)

def apply_rope(x, cos, sin):
    half = x.shape[-1] // 2
    x1, x2 = x[..., :half], x[..., half:]
    rot = jnp.concatenate([-x2, x1], axis=-1)
    return x * cos.astype(x.dtype) + rot * sin.astype(x.dtype)

def t5_bucket(dist):
    max_exact = REL_BUCKETS // 2
    n = jnp.maximum(dist, 0)
    large = max_exact + (jnp.log(jnp.maximum(n, 1).astype(jnp.float32) / max_exact)
                         / math.log(REL_MAX_DIST / max_exact)
                         * (REL_BUCKETS - max_exact)).astype(jnp.int32)
    large = jnp.minimum(large, REL_BUCKETS - 1)
    return jnp.where(n < max_exact, n, large)

def mla_branch(cq, ckv, k_rope, g_q, w_uq, g_kv, w_ukv):
    B, S, _ = cq.shape
    nb = S // BLOCK
    cos, sin = rope_tables(S)
    q = (rms_norm(cq, g_q) @ w_uq).reshape(B, S, MLA_HEADS, MLA_QK)
    q_nope = q[..., :MLA_NOPE]
    q_rope = apply_rope(q[..., MLA_NOPE:], cos[:, None, :], sin[:, None, :])
    kv = (rms_norm(ckv, g_kv) @ w_ukv).reshape(B, S, MLA_HEADS, MLA_NOPE + MLA_V)
    k_nope, v = kv[..., :MLA_NOPE], kv[..., MLA_NOPE:]
    k_rope = apply_rope(k_rope, cos, sin)
    scale = MLA_QK ** -0.5
    qn_blocks = q_nope.reshape(B, nb, BLOCK, MLA_HEADS, MLA_NOPE).transpose(1, 0, 2, 3, 4)
    qr_blocks = q_rope.reshape(B, nb, BLOCK, MLA_HEADS, MLA_ROPE).transpose(1, 0, 2, 3, 4)
    kpos = jnp.arange(S)

    def one_block(args):
        qn, qr, i = args
        s = (jnp.einsum('bqhd,bkhd->bhqk', qn, k_nope)
             + jnp.einsum('bqhd,bkd->bhqk', qr, k_rope)).astype(jnp.float32) * scale
        qpos = i * BLOCK + jnp.arange(BLOCK)
        s = jnp.where(kpos[None, :] <= qpos[:, None], s, NEG)
        p = jax.nn.softmax(s, axis=-1).astype(v.dtype)
        return jnp.einsum('bhqk,bkhd->bqhd', p, v)

    out = lax.map(one_block, (qn_blocks, qr_blocks, jnp.arange(nb)))
    return out.transpose(1, 0, 2, 3, 4).reshape(B, S, MLA_HEADS * MLA_V)

def swa_branch(q, k, v, rel_bias, sinks):
    B, S, _ = q.shape
    nb = S // BLOCK
    q = q.reshape(B, nb, BLOCK, SWA_KV_HEADS, SWA_GROUP, SWA_HEAD_DIM)

    def band(t):
        t = t.reshape(B, S, SWA_KV_HEADS, SWA_HEAD_DIM)
        t = jnp.pad(t, ((0, 0), (BLOCK, 0), (0, 0), (0, 0)))
        t = t.reshape(B, nb + 1, BLOCK, SWA_KV_HEADS, SWA_HEAD_DIM)
        return jnp.concatenate([t[:, :-1], t[:, 1:]], axis=2)

    kb, vb = band(k), band(v)
    s = jnp.einsum('bnqhgd,bnshd->bhgnqs', q, kb).astype(jnp.float32) * (SWA_HEAD_DIM ** -0.5)
    a = jnp.arange(BLOCK)
    bidx = jnp.arange(2 * BLOCK)
    dist = BLOCK + a[:, None] - bidx[None, :]
    bias = rel_bias[t5_bucket(dist)].astype(jnp.float32)
    bias = bias.transpose(2, 0, 1).reshape(SWA_KV_HEADS, SWA_GROUP, 1, BLOCK, 2 * BLOCK)
    kpos = jnp.arange(nb)[:, None, None] * BLOCK - BLOCK + bidx[None, None, :]
    mask = (dist >= 0)[None] & (dist < WINDOW)[None] & (kpos >= 0)
    s = jnp.where(mask, s + bias, NEG)
    sink = sinks.astype(jnp.float32).reshape(SWA_KV_HEADS, SWA_GROUP, 1, 1, 1)
    m = jnp.maximum(jnp.max(s, axis=-1, keepdims=True), sink)
    e = jnp.exp(s - m)
    p = e / (jnp.sum(e, axis=-1, keepdims=True) + jnp.exp(sink - m))
    o = jnp.einsum('bhgnqs,bnshd->bnqhgd', p.astype(vb.dtype), vb)
    return o.reshape(B, S, SWA_Q)

def causal_dwconv(u, w, b):
    S = u.shape[1]
    up = jnp.pad(u, ((0, 0), (CONV_WIDTH - 1, 0), (0, 0)))
    y = b
    for j in range(CONV_WIDTH):
        y = y + w[j] * up[:, j:j + S]
    return y

def second_inputs(seed: int = 0) -> dict:
    key = jax.random.key(seed)
    ks = jax.random.split(key, 24)
    f32 = jnp.float32
    D, L = D_MODEL, DEPTH

    def nrm(k, shape, scale):
        return jax.random.normal(k, shape, f32) * scale

    def gain(k, shape):
        return 1.0 + 0.1 * jax.random.normal(k, shape, f32)

    return {
        "x": nrm(ks[0], (BATCH, SEQ, D), 1.0),
        "c": nrm(ks[1], (BATCH, D), 1.0),
        "w_ada": nrm(ks[2], (L, D, 6 * D), 0.5 * D ** -0.5),
        "b_ada": nrm(ks[3], (L, 6 * D), 0.02),
        "g_pre_mix": gain(ks[4], (L, D)),
        "g_post_mix": gain(ks[5], (L, D)),
        "w_in": nrm(ks[6], (L, D, IN_COLS_2), D ** -0.5),
        "g_q_lat": gain(ks[7], (L, MLA_Q_RANK)),
        "w_uq": nrm(ks[8], (L, MLA_Q_RANK, MLA_HEADS * MLA_QK), MLA_Q_RANK ** -0.5),
        "g_kv_lat": gain(ks[9], (L, MLA_KV_RANK)),
        "w_ukv": nrm(ks[10], (L, MLA_KV_RANK, MLA_HEADS * (MLA_NOPE + MLA_V)), MLA_KV_RANK ** -0.5),
        "rel_bias": nrm(ks[11], (REL_BUCKETS, SWA_HEADS), 0.5),
        "sinks": nrm(ks[12], (L, SWA_HEADS), 1.0),
        "w_o": nrm(ks[13], (L, D, D), D ** -0.5),
        "g_pre_ffn": gain(ks[14], (L, D)),
        "g_post_ffn": gain(ks[15], (L, D)),
        "w_up": nrm(ks[16], (L, D, 2 * D_FF), D ** -0.5),
        "conv_w": nrm(ks[17], (L, CONV_WIDTH, 2 * D_FF), CONV_WIDTH ** -0.5),
        "conv_b": nrm(ks[18], (L, 2 * D_FF), 0.02),
        "w_down": nrm(ks[19], (L, D_FF, D), D_FF ** -0.5),
    }

def second_block(x, c, w_ada, b_ada, g_pre_mix, g_post_mix, w_in, g_q_lat, w_uq, g_kv_lat,
              w_ukv, rel_bias, sinks, w_o, g_pre_ffn, g_post_ffn, w_up, conv_w, conv_b, w_down):
    D = D_MODEL
    c_act = jax.nn.silu(c)
    for l in range(DEPTH):
        mod = (c_act @ w_ada[l] + b_ada[l])[:, None, :]
        sh1, sc1, gt1, sh2, sc2, gt2 = jnp.split(mod, 6, axis=-1)

        h = rms_norm(x, g_pre_mix[l]) * (1.0 + sc1) + sh1
        z = h @ w_in[l]
        o0 = 0
        cq = z[..., o0:o0 + MLA_Q_RANK]; o0 += MLA_Q_RANK
        ckv = z[..., o0:o0 + MLA_KV_RANK]; o0 += MLA_KV_RANK
        kr = z[..., o0:o0 + MLA_ROPE]; o0 += MLA_ROPE
        qs = z[..., o0:o0 + SWA_Q]; o0 += SWA_Q
        ks_ = z[..., o0:o0 + SWA_KV]; o0 += SWA_KV
        vs = z[..., o0:o0 + SWA_KV]; o0 += SWA_KV
        gates = jax.nn.sigmoid(z[..., o0:o0 + N_BRANCH * D])
        g_a, g_b = gates[..., :D], gates[..., D:]

        o_a = mla_branch(cq, ckv, kr, g_q_lat[l], w_uq[l], g_kv_lat[l], w_ukv[l])
        o_b = swa_branch(qs, ks_, vs, rel_bias, sinks[l])
        mix = (g_a * o_a + g_b * o_b) @ w_o[l]
        x = x + gt1 * rms_norm(mix, g_post_mix[l])

        h = rms_norm(x, g_pre_ffn[l]) * (1.0 + sc2) + sh2
        u = causal_dwconv(h @ w_up[l], conv_w[l], conv_b[l])
        y = (jax.nn.silu(u[..., :D_FF]) * u[..., D_FF:]) @ w_down[l]
        x = x + gt2 * rms_norm(y, g_post_ffn[l])
    return x


def setup_inputs(seed=0):
    out = dict(first_inputs(seed))
    for name, value in second_inputs(seed + 1).items():
        if name != "x":
            out[name + "_2"] = value
    return out


def reference(
    x, norm_gain, w_in, fox_forget_bias, rwkv_shift_mix, rwkv_w0, rwkv_w2, rwkv_a0, rwkv_a2,
    rwkv_k_k, rwkv_k_a, rwkv_r_k, rwkv_ln_w, rwkv_ln_b, w_proj_fox, w_proj_rwkv, w_out,
    final_norm_gain, c_2, w_ada_2, b_ada_2, g_pre_mix_2, g_post_mix_2, w_in_2, g_q_lat_2,
    w_uq_2, g_kv_lat_2, w_ukv_2, rel_bias_2, sinks_2, w_o_2, g_pre_ffn_2, g_post_ffn_2, w_up_2,
    conv_w_2, conv_b_2, w_down_2,
):
    x = first_block(
        x, norm_gain, w_in, fox_forget_bias, rwkv_shift_mix, rwkv_w0, rwkv_w2, rwkv_a0, rwkv_a2,
        rwkv_k_k, rwkv_k_a, rwkv_r_k, rwkv_ln_w, rwkv_ln_b, w_proj_fox, w_proj_rwkv, w_out,
        final_norm_gain,
    )
    return second_block(
        x, c_2, w_ada_2, b_ada_2, g_pre_mix_2, g_post_mix_2, w_in_2, g_q_lat_2, w_uq_2,
        g_kv_lat_2, w_ukv_2, rel_bias_2, sinks_2, w_o_2, g_pre_ffn_2, g_post_ffn_2, w_up_2,
        conv_w_2, conv_b_2, w_down_2,
    )


_drawn_inputs = setup_inputs


def setup_inputs(seed=0):
    import zlib

    import numpy as np

    out = dict(_drawn_inputs(seed))
    spreads = {}
    factors = {'rwkv_w2': 8.0,
     'rwkv_a0': 5.82,
     'rwkv_k_k': 5.3,
     'rwkv_k_a': 3.909,
     'rwkv_r_k': 4.783,
     'rwkv_ln_w': 4.603,
     'rwkv_ln_b': 8.0,
     'g_q_lat_2': 6.059,
     'g_kv_lat_2': 2.793,
     'sinks_2': 20.349,
     'conv_b_2': 7.499,
     'rel_bias_2': 5.973}
    for name, (base, spread) in spreads.items():
        noise = np.random.default_rng([zlib.crc32(name.encode()), seed]).standard_normal(out[name].shape)
        drawn = base * np.exp(spread * noise) if base else spread * noise
        out[name] = __import__('jax').numpy.asarray(drawn.astype(out[name].dtype))
    for name, factor in factors.items():
        out[name] = (out[name] * factor).astype(out[name].dtype)
    return out
```

```python
from contextlib import ExitStack

import numpy as np

import concourse.bass as bass
from concourse import mybir

F32 = mybir.dt.float32
F32R = mybir.dt.float32r
ALU = mybir.AluOpType
ACT = mybir.ActivationFunctionType
AX = mybir.AxisListType

P = 128
D = 2048
T = 256
DT = D // P
TT = T // P
FOX_HEADS = 8
FOX_SCALE = float(P) ** -0.5
W1 = D // 2
WT = W1 // P
LORA = 96
RWKV_HD = 64
CHUNK = 64
NCH = T // CHUNK
LEVELS = (2, 4, 8, 16, 32)
DECAY_SCALE = float(np.exp(-0.5))
FOX_COLS = 4 * W1 + FOX_HEADS
RWKV_COLS = 4 * W1 + 2 * LORA

MLA_HEADS = 16
QR, KVR, ROPE = 768, 512, 64
MLA_SCALE = float(192) ** -0.5
SWA_HEADS, SWA_KV, SWA_HD = 32, 4, 64
SWA_SCALE = float(SWA_HD) ** -0.5
NEG = -1e30
D_FF = 5632
FT = D_FF // P
BUCKETS = 32

BLK = 1024
RING = 4
AHEAD = RING - 1
NQ = 8


def _columns(sizes):
    out, at = {}, 0
    for name, n in sizes:
        out[name] = (at, n)
        at += n
    return out, at


VEC, NVEC = _columns([
    ("g1", 16), ("mu", 32), ("mu_w", 1), ("mu_a", 1), ("fbias", 1), ("w0", 8), ("a0", 8), ("k_k", 8), ("k_a", 8),
    ("r_k", 8), ("ln_w", 8), ("ln_b", 8), ("gf", 16), ("c", 16), ("b_ada", 96), ("g_pre_mix", 16),
    ("g_post_mix", 16), ("g_q", 6), ("g_kv", 4), ("sinks", 32), ("g_pre_ffn", 16), ("g_post_ffn", 16),
    ("conv_w", 264), ("conv_b", 88),
])
CON1, NCON1 = _columns([
    ("ident", 128), ("ones", 128), ("bones", 128), ("m_su", 128), ("m_ui", 128), ("m_u1", 128), ("m_low", 768),
    ("causal", 512), ("reset", 256), ("selcol", 8), ("bmask", 128),
])
CON2, NCON2 = _columns([
    ("ident", 128), ("ones", 128), ("causal", 512), ("rot", 128), ("cos", 256), ("sin", 256),
    ("onehot", 384),
])


def constants():
    f = np.float32
    i, j = np.arange(P)[:, None], np.arange(P)[None, :]
    same = (i // CHUNK) == (j // CHUNK)
    ident = np.eye(P, dtype=f)
    causal = np.full((P, 2, T), NEG, f)
    for b in range(2):
        causal[:, b, :][(np.arange(T)[None, :] <= b * P + np.arange(P)[:, None])] = 0
    low = []
    for m in (1,) + LEVELS:
        low.append(((i // (2 * m)) == (j // (2 * m))) & ((i // m) % 2 == 1) & ((j // m) % 2 == 0))
    u1 = low[0].T
    reset = np.broadcast_to((np.arange(T) % CHUNK != 0), (P, T))
    selcol = np.zeros((P, 8), f)
    for h in range(8):
        selcol[h, h] = selcol[32 + h, h] = 1
    one = {
        "ident": ident, "ones": np.ones((P, P)), "bones": (i // 64 == j // 64), "m_su": same & (i < j),
        "m_ui": same & (i <= j), "m_u1": u1, "m_low": np.concatenate(low, 1), "causal": causal.reshape(P, 512),
        "reset": reset, "selcol": selcol, "bmask": (i // 64 == j // 64),
    }
    c1 = np.concatenate([np.asarray(one[n], f) for n in CON1], 1)
    pos = np.arange(T, dtype=f)
    inv = f(10000.0) ** (-np.arange(0, ROPE, 2, dtype=f) / f(ROPE))
    ang = pos[None, :] * np.concatenate([inv, inv])[:, None]
    cos, sin = np.tile(np.cos(ang).astype(f), (2, 1)), np.tile(np.sin(ang).astype(f), (2, 1))
    rot = np.zeros((P, P), f)
    for g in range(2):
        for m in range(32):
            rot[64 * g + m + 32, 64 * g + m] = -1
            rot[64 * g + m, 64 * g + m + 32] = 1
    n = np.maximum(255 - np.arange(384), 0)
    exact = BUCKETS // 2
    large = exact + (np.log(np.maximum(n, 1).astype(f) / f(exact)) / f(np.log(P / exact))
                     * f(BUCKETS - exact)).astype(np.int32)
    bucket = np.where(n < exact, n, np.minimum(large, BUCKETS - 1))
    onehot = np.zeros((P, 384), f)
    onehot[bucket, np.arange(384)] = 1
    two = {"ident": ident, "ones": np.ones((P, P)), "causal": causal.reshape(P, 512), "rot": rot, "cos": cos,
           "sin": sin, "onehot": onehot}
    c2 = np.concatenate([np.asarray(two[n], f) for n in CON2], 1)
    return np.ascontiguousarray(c1), np.ascontiguousarray(c2)


STRETCH = (
    ("fox", 64), ("waf", 4), ("rwkv", 64), ("gates1", 64), ("proj1", 32), ("out1", 32),
    ("lat", 22), ("swa", 40), ("gates2", 64), ("uq", 18), ("ukv", 16), ("out2", 32), ("up", 176), ("down", 88),
)
B0, NBLK = {}, 0
for _name, _n in STRETCH:
    B0[_name] = NBLK
    NBLK += _n
Q0, _q = {}, 0
for _name, _n in (("fox", 8), ("waf", 1), ("rwkv", 8), ("gates1", 8), ("proj1", 8), ("out1", 4), ("lat", 4), ("swa", 5),
                  ("gates2", 8), ("uq", 6), ("ukv", 8), ("out2", 4), ("up", 22)):
    Q0[_name] = _q
    _q += _n

WORK = 20224


SHARED = {}
for _kind, _counts in {
    "sq": dict(n1=4, nf=4, n2=4, nq=2, nk=1, r1=4, n3=4, r2=4),
    **{k: dict(n1=1, nf=1, n2=1, nq=1, nk=1, r1=1, n3=1, r2=1) for k in ("part", "sum", "ms", "inv", "rstd")},
    "xr": dict(n1=4, nf=4, n2=4, nq=1, nk=1, r1=1, n3=4, r2=1),
    "h": dict(n1=16, m1=16, nf=16, n2=16, nq=6, nk=4, m2=16, n3=16),
    **{k: dict(n1=4, oa=1, obo=1, m1=4, n2=4, nq=1, nk=1, m2=4, n3=4) for k in ("hi", "lo")},
    **{k: dict(fox=8, swa=16, mla=8) for k in ("qk", "pv", "t", "mx", "nm", "rs", "o")},
    "q": dict(fox=8, swa=32, mla=8), "v": dict(fox=8, swa=4), "e": dict(fox=16, swa=64, mla=32),
    "s": dict(fox=8, swa=32, mla=8), "pt": dict(fox=8, swa=32, mla=16), "p": dict(fox=16, swa=16, mla=8),
}.items():
    _at = 0
    for _step, _n in _counts.items():
        SHARED[f"{_step}_{_kind}"] = (("norm_" if "n1" in _counts else "attn_") + _kind, _at)
        _at += _n

for _first, _n, _later in (
    ("rw_kk0", 8, "swa_sb"), ("rw_ld", 8, "swa_m"), ("rw_lc", 8, "swa_d"), ("rw_lp", 8, "swa_tot"),
    ("rw_kkm", 8, "swa_zero"), ("rw_kkinv", 8, "swa_neg"), ("rw_kf", 8, "mla_zero"), ("rw_kh", 8, "rope_s"),
    ("rw_kk", 8, "rope_c"), ("rw_rk", 8, "rope"), ("rw_ba", 8, "gain"), ("rw_kt", 8, "ada_mod"), ("rw_bt", 8, "rev"),
    ("rw_rt", 8, "ffn_cv"), ("rw_s0", 8, "m2_g"), ("rw_v", 8, "swa_es"), ("rw_sg", 8, "swa_k"), ("rw_a", 8, "ffn_c"),
    ("rw_kk2", 8, "ffn_z"), ("rw_kkr", 8, "y_hi"), ("gn_mean", 4, "rot"), ("gn_var", 4, "rev_p"), ("f_x", 1, "gn_sq"),
    ("f_abs", 1, "gn_rstd"), ("f_exp", 1, "gn_z"), ("f_ln", 1, "down_out"), ("f_min", 1, "gn_yc"),
    ("f_log", 1, "gn_v"), ("f_sum", 1, "gn_inv"), ("aug_z", 3, "gn_y"), ("aug_1", 3, "gn_w"), ("omm", 1, "gn_b"),
    ("fox_aug", 8, "y_lo"), ("x_loaded", 16, "con2_in"), ("vec_loaded", 16, "rel_in"), ("con_loaded", 16, "gates2_in"),
):
    SHARED[_later] = (_first, _n)

PRIMED = {
    "rw_lora": "pe", "rw_y": "act", "ffn_y": "dve",
    "attn_qk": "pe", "attn_pv": "pe", "attn_e": "act", "attn_s": "dve", "attn_pt": "act", "attn_o": "dve",
}


def at(c, per=0, i=None):
    return c if i is None else c + i * per


def build(nc, ins, out):
    with ExitStack() as ctx:
        def sb(name, cols, dt=F32):
            return ctx.enter_context(nc.sbuf_tensor(name, [P, cols], dt))

        def pb(name):
            return ctx.enter_context(nc.psum_tensor(name, [P, 1024], F32))

        sems = {}

        def sem(name):
            name = SHARED.get(name, (name, 0))[0]
            if name not in sems:
                sems[name] = ctx.enter_context(nc.semaphore(name))
            return sems[name]

        raw = sb("w_raw", RING * BLK)
        whi = sb("w_hi", RING * BLK, F32R)
        wlo = sb("w_lo", RING * BLK, F32R)
        hhi = sb("h_hi", DT * T, F32R)
        hlo = sb("h_lo", DT * T, F32R)
        x = sb("x", DT * T)
        vec = sb("vec", NVEC)
        con = sb("con", max(NCON1, NCON2))
        work = sb("work", WORK)
        adaw = sb("ada_w", 2 * 1024)
        adap = sb("ada_p", 2 * 1024)
        small = sb("small", 896)
        G = [pb("gemm0"), pb("gemm1")]
        A = [pb("aux0"), pb("aux1")]
        bank = [A[0][:, 0:512], A[0][:, 512:1024], A[1][:, 0:512], A[1][:, 512:1024]]

        def V(name, k=None, n=1):
            a, w = VEC[name]
            return vec[:, a:a + w] if k is None else vec[:, a + k:a + k + n]

        def C1(name, rows=P):
            a, w = CON1[name]
            return con[0:rows, a:a + w]

        def C2(name, rows=P):
            a, w = CON2[name]
            return con[0:rows, a:a + w]

        x3 = x[:].rearrange("p (k t) -> p k t", t=T)
        hh = hhi[:].rearrange("p (k t) -> p k t", t=T)
        hl = hlo[:].rearrange("p (k t) -> p k t", t=T)

        def area(off, cols, t=T):
            return work[:, off:off + cols].rearrange("p (k t) -> p k t", t=t)

        def tiles(k, n=1):
            return work[:, k * T:(k + n) * T]

        def tile_at(k, i, n=1, per=1):
            return work[:, bass.ds(i * (per * T) + k * T, n * T)]

        fox = area(0, 24 * T)
        foxv = area(24 * T, 2 * W1, W1)
        waf = area(32 * T, 2 * T)
        RR, RK, RV, RZ = 34, 42, 50, 58
        sq = area(34 * T, DT * T)
        sc, scf = area(66 * T, 2 * T), tiles(66, 2)
        pr = area(68 * T, 2 * T)
        ptf = tiles(70, 2)
        aug_l, aug_r, aug_h = (work[0:40, (72 + n) * T:(73 + n) * T] for n in range(3))
        fq = tiles(75)
        fv = area(76 * T, T, P)
        lsg = [work[0:8, (66 + n) * T:(67 + n) * T] for n in range(4)]
        low = tiles(8, 12).rearrange("p (l u t) -> p l u t", l=6, u=4)
        um, wm, gm, lak, rb, rk = (tiles(20 + 2 * n, 2) for n in range(6))
        at_, bt_, kt_, rt_ = (tiles(66 + n) for n in range(4))
        btok, ktok, vtok = (area((70 + n) * T, T, P) for n in range(3))
        xv, sa = area(73 * T, T, P), area(74 * T, T, P)
        xs, sbd = work[:, 75 * T:75 * T + P], work[:, 75 * T + P:76 * T]
        t1, t2 = tiles(77), tiles(78)
        e0, e1, e2, e5 = tiles(73), tiles(71), tiles(72), tiles(76)
        ep, en, bkt = tiles(74), tiles(70), tiles(70, 2)
        vf = x[:, 8 * T:9 * T]
        lw = x[0:LORA, 9 * T:10 * T]
        ah = x[:, 10 * T:12 * T].rearrange("p (h t) -> p h t", t=T)
        rh_ = x[:, 12 * T:14 * T].rearrange("p (h t) -> p h t", t=T)
        gates2 = nc.dram_tensor("gates2", (8, P, BLK), F32).ap()
        gates = nc.dram_tensor("gates", (8, P, BLK), F32).ap()
        lat = area(0, 11 * T)
        SQ, SK, SV = 11, 27, 55
        swv = area(SV * T, 2 * T)
        MQ, MR = 31, 47
        bias = [area((31 + 2 * n) * T, 2 * T) for n in range(2)]
        qz, vst = area(38 * T, 2 * T), area(40 * T, P, 64)
        revs = work[0:36, 73 * T:73 * T + 384]
        stage = [tiles(57 + 4 * n, 4) for n in range(2)]
        s4, p4 = area(65 * T, 4 * T), area(69 * T, 4 * T)
        spt = tiles(35, 3)
        kn, vv, qn, qr = (area((55 + 2 * n) * T, 2 * T) for n in range(4))
        ms4, mp4, mpt, krr = area(63 * T, 4 * T), area(67 * T, 4 * T), tiles(71, 3), tiles(74)
        rt1, rt2 = tiles(75), tiles(76)
        msq = area(57 * T, 10 * T)
        rel = work[0:BUCKETS, 77 * T:77 * T + SWA_HEADS + 4]
        mod = adap[:, 0:96]
        gg1, gg2, gr1, gr2 = (adap[:, 96 + 16 * n:112 + 16 * n] for n in range(4))
        adasum = nc.dram_tensor("adasum", (12, P, 1024), F32).ap()
        revd = nc.dram_tensor("revd", (SWA_HEADS + 4, P * 384), F32).ap()
        yh, yl = hh[:, 0:4, :], hl[:, 0:4, :]
        stat = [small[:, n * T:(n + 1) * T] for n in range(3)]
        st = small[:, 3 * T:3 * T + 32]
        omm = small[:, 3 * T + 32:3 * T + 66]
        omka = small[:, 3 * T + 66:3 * T + 74]

        def load_block(eng, c, per=0, i=None):
            n = at(c, per, i)
            if c >= RING:
                eng.wait_ge(sem("lo_ready"), n - AHEAD)
            s = c % RING
            eng.dma_start(raw[:, s * BLK:(s + 1) * BLK],
                          ins["w"][bass.ds(n, 1), :, :].rearrange("a p n -> p (a n)")).then_inc(sem(f"raw{s}"), 16)

        def waiter(eng):
            def hold(name, v):
                name, before = SHARED.get(name, (name, 0))
                eng.wait_ge(sem(name), v + before + (name in PRIMED))
            return hold

        def prime(eng, who):
            if who == "act":
                for n in range(2):
                    eng.sem_inc(sem(f"gate_out{n}"), 16)
                    eng.sem_inc(sem(f"gate2_out{n}"), 16)

            for name, by in PRIMED.items():
                if by == who:
                    eng.sem_inc(sem(name), 1)

        def split_hi(eng, c, per=0, i=None):
            if c >= NBLK:
                return
            s = c % RING
            eng.wait_ge(sem(f"raw{s}"), at(16 * (c // RING + 1), 4 * per, i))
            if c >= RING:
                eng.wait_ge(sem("block_used"), at(c - AHEAD, per, i))
            eng.activation(whi[:, s * BLK:(s + 1) * BLK], raw[:, s * BLK:(s + 1) * BLK],
                           ACT.Copy).then_inc(sem("hi_ready"), 1)

        def split_lo(eng, c, per=0, i=None):
            if c >= NBLK:
                return
            s = c % RING
            eng.wait_ge(sem("hi_ready"), at(c + 1, per, i))
            eng.tensor_tensor(wlo[:, s * BLK:(s + 1) * BLK], raw[:, s * BLK:(s + 1) * BLK],
                              whi[:, s * BLK:(s + 1) * BLK].bitcast(F32), ALU.subtract).then_inc(sem("lo_ready"), 1)

        def block(eng, c, per, i, cols, rh, rl, k0, set_, first, last, token=False, parts=None):
            s = c % RING
            ks = BLK // cols
            eng.wait_ge(sem("lo_ready"), at(c + 1, per, i))
            wh = whi[:, s * BLK:(s + 1) * BLK].rearrange("p (k n) -> p k n", n=cols)
            wl = wlo[:, s * BLK:(s + 1) * BLK].rearrange("p (k n) -> p k n", n=cols)
            if parts is None:
                parts = [(True, slice(0, cols), 0)] if token else [(False, t, t * T) for t in range(cols // P)]
            g = G[set_] if isinstance(set_, int) else set_
            for tok, what, col in parts:
                for t in range(TT if tok else 1):
                    for k in range(ks):
                        for a, (w_, r_) in enumerate(((wh, rh), (wh, rl), (wl, rh))):
                            if tok:
                                r = w_[:, k, :].rearrange("p (h e n) -> p h e n", e=2, n=P)[:, :, 1, :] \
                                    if what == "v" else w_[:, k, what]
                                n = TT * P if what == "v" else what.stop - what.start
                                o = g[:, col + t * n:col + (t + 1) * n]
                                if what == "v":
                                    o = o.rearrange("p (h n) -> p h n", n=P)
                                l, st_ = r_[:, k0 + k, t * P:(t + 1) * P], (col + t * n) % 512 == 0
                            else:
                                o = g[:, col:col + T]
                                l, r, st_ = w_[:, k, what * P:(what + 1) * P], r_[:, k0 + k, :], col % 512 == 0
                            mm = eng.matmul(o, l, r, start=first and k == 0 and a == 0 and st_,
                                            stop=last and k == ks - 1 and a == 2, skip_group_check=True)
            mm.then_inc(sem("block_used"), 1)
            return mm

        def quad_pe(eng, c, per, i, q, qper, set_, cols=512, nb=NQ, rh=hh, rl=hl, token=False, parts=None):
            if q >= 2:
                eng.wait_ge(sem("quad_read"), at(q - 1, qper, i))
            for b in range(nb):
                block(eng, c + b, per, i, cols, rh, rl, b * (BLK // cols), set_, b == 0, b == nb - 1, token, parts)

        def quad_done(eng, c_end, per=0, i=None):
            eng.wait_ge(sem("block_used"), at(c_end, per, i))

        blk = ctx.enter_context(nc.Block())

        @blk.sync
        def _(sp):
            hold = waiter(sp)
            sp.dma_start(x[:], ins["x"]).then_inc(sem("x_loaded"), 16)
            sp.dma_start(vec[:], ins["vec"]).then_inc(sem("vec_loaded"), 16)
            sp.dma_start(con[:, 0:NCON1], ins["con1"]).then_inc(sem("con_loaded"), 16)
            for c in range(RING):
                load_block(sp, c)
            turns = NBLK // RING - 1
            with sp.Fori(0, turns) as i:
                for c in range(RING, 2 * RING):
                    load_block(sp, c, RING, i)
            for c in range((turns + 1) * RING, NBLK):
                load_block(sp, c)
            hold("r2_x", 16)
            sp.dma_start(out, x[:]).then_inc(sem("stored"), 16)
            sp.wait_ge(sem("stored"), 16)

        @blk.gpsimd
        def _(pool):
            prime(pool, "pool")
            hold = waiter(pool)
            prod, acc = adap[:, 0:1024], adap[:, 1024:2048]

            def load(n, s):
                pool.dma_start(adaw[:, s * 1024:(s + 1) * 1024],
                               ins["ada"][bass.ds(n, 1), :, :].rearrange("a p n -> p (a n)"))\
                    .then_inc(sem(f"ada_in{s}"), 16)

            load(0, 0)
            load(1, 1)
            hold("c_silu", 1)
            with pool.Fori(0, 12) as g:
                for k in range(DT):
                    w = adaw[:, (k % 2) * 1024:(k % 2 + 1) * 1024]
                    pool.wait_ge(sem(f"ada_in{k % 2}"), g * 128 + 16 * (k // 2 + 1))
                    if k >= 2:
                        hold("ada_acc", g * 15 + k - 1)
                    pool.sem_inc(sem("ada_turn"), 1)
                    pool.tensor_scalar(prod if k else acc, w, V("c", k), 0.0, ALU.mult, ALU.add)\
                        .then_inc(sem("ada_prod"), 1)
                    hold("ada_prod", g * 16 + k + 1)
                    load(g * 16 + k + 2, k % 2)
                    if k:
                        pool.tensor_tensor(acc, acc, prod, ALU.add).then_inc(sem("ada_acc"), 1)
                hold("ada_acc", g * 15 + 15)
                pool.dma_start(adasum[bass.ds(g, 1), :, :].rearrange("a p n -> p (a n)"), acc)\
                    .then_inc(sem("ada_st"), 16)
                pool.wait_ge(sem("ada_st"), g * 16 + 16)
            for n in range(2):
                pool.wait_ge(sem(f"ada_in{n}"), 12 * 128 + 16)
            for g in range(12):
                if g >= 4:
                    hold("ada_sum", g - 3)
                s = g % 4
                dst = (adaw if s < 2 else adap)[:, (s % 2) * 1024:(s % 2 + 1) * 1024]
                pool.dma_start(dst, adasum[g]).then_inc(sem(f"ada_back{s}"), 16)

        @blk.scalar
        def _(act):
            hold = waiter(act)
            prime(act, "act")

            def norm_squares(tag, src, tiles=DT, sq=sq):
                for c in range(0, tiles, 4):
                    n = min(4, tiles - c)
                    act.activation(sq[:, c:c + n, :], src[:, c:c + n, :], ACT.Square).then_inc(sem(tag + "_sq"), 1)

            def norm_root(tag):
                hold(tag + "_inv", 1)
                act.activation(stat[2], stat[1], ACT.Sqrt).then_inc(sem(tag + "_rstd"), 1)

            def operand_hi(tag, src, dst, tiles=DT, step=4):
                for c in range(0, tiles, step):
                    n = min(step, tiles - c)
                    if tag not in ("oa", "obo"):
                        hold(tag + "_h", min(c + n, tiles))
                    act.activation(dst[:, c:c + n, :], src[:, c:c + n, :], ACT.Copy).then_inc(sem(tag + "_hi"), 1)

            def rwkv_act():
                act.activation(waf[0:LORA, 0, :], waf[0:LORA, 0, :], ACT.Tanh).then_inc(sem("tanh_w"), 1)
                c = B0["gates1"]
                with act.Fori(0, WT // 2) as i:
                    for s in range(2):
                        n, g, b0 = 2 * i + s, G[(Q0["gates1"] + s) % 2], c + 8 * s

                        def split(b):
                            split_hi(act, b0 + b + AHEAD, 16, i)

                        def copy(out_, in_, name, f=ACT.Copy, **kw):
                            return act.activation(out_, in_, f, **kw).then_inc(sem(name), 1)

                        hold("rw_lora", n)
                        act.dma_start(lw, ins["lora"][bass.ds(n, 1), :, :].rearrange("a p n -> p (a n)"))\
                            .then_inc(sem("lora_in"), 16)
                        copy(vf, tile_at(RV + s, i, 1, 2), "rw_v")
                        hold("rw_lora", n + 1)
                        copy(t1, bank[0][:, 0:T], "rw_sg", ACT.Sigmoid, bias=vec[:, bass.ds(n + VEC["w0"][0], 1)])
                        copy(t2, bank[0][:, T:2 * T], "rw_a", ACT.Sigmoid, bias=vec[:, bass.ds(n + VEC["a0"][0], 1)])
                        split(0)
                        hold("rw_kk0", n + 1)
                        copy(e2, e1, "rw_kk2", ACT.Square)
                        hold("rw_kkinv", n + 1)
                        copy(e2, e2, "rw_kkr", ACT.Sqrt)
                        hold("rw_lc", n + 1)
                        copy(ep, e0, "rw_p", ACT.Exp)
                        copy(en, e0, "rw_n", ACT.Exp, scale=-1.0)
                        hold("rw_lp", n + 1)
                        copy(e5, e5, "rw_pp", ACT.Exp)
                        split(1)
                        hold("rw_rt", n + 1)
                        for h in range(2):
                            copy(rh_[64 * h:64 * h + 64, h, :], rt_[64 * h:64 * h + 64, :], "rw_rh")
                        hold("rw_tr", n + 1)
                        copy(bkt, bank[2][:, 0:4 * P], "rw_tok")
                        hold("rw_trv", n + 1)
                        copy(vtok.rearrange("p t n -> p (t n)"), bank[3][:, 0:2 * P], "rw_vtok")
                        split(2)
                        for lv in range(1, 6):
                            hold("rw_g", 5 * n + lv)
                            copy(gm, bank[1], "rw_gc")
                            split(2 + lv)
                        hold("rw_xv", n + 1)
                        copy(xv.rearrange("p t n -> p (t n)"), bank[0][:, 0:T], "rw_xvc")
                        for ch in range(NCH):
                            r = slice((ch % 2) * 64, (ch % 2) * 64 + 64)
                            hold("rw_sa", 4 * n + ch + 1)
                            copy(sa[r, ch // 2, :], bank[2][r, 0:P], "rw_sac")
                        quad_done(act, b0 + 8, 16, i)
                        act.wait_ge(sem(f"gate_out{s}"), 16 * i + 16)
                        copy(x[:, s * 1024:(s + 1) * 1024], g[:], "quad_read", ACT.Sigmoid)
                        act.wait_ge(sem("quad_read"), at(Q0["gates1"] + s + 1, 2, i))
                        act.dma_start(gates[bass.ds(n, 1), :, :].rearrange("a p n -> p (a n)"),
                                      x[:, s * 1024:(s + 1) * 1024]).then_inc(sem(f"gate_out{s}"), 16)
                        hold("rw_yp", n + 1)
                        copy(tile_at(RR + s, i, 1, 2), bank[0][:, 0:T], "rw_y")
                operand_hi("oa", area(0, 8 * T), hh[:, 0:8, :], 8, 8)
                for q in range(4):
                    hold("gn_yc", q + 1)
                    copy(tiles(16 + 2 * q, 2), tiles(8 + 2 * q, 2), "gn_sq", ACT.Square)
                hold("gn_inv", 4)
                copy(tiles(16, 8), tiles(16, 8), "gn_rstd", ACT.Sqrt)
                copy(tiles(RZ, 8), tiles(RZ, 8), "gn_z", ACT.Silu)

            def mix1_act():
                hold("gn_o", 1)
                operand_hi("obo", area(RR * T, 8 * T), hh[:, 8:16, :], 8, 8)
                for n in range(2):
                    act.wait_ge(sem(f"gate_out{n}"), 80)
                for k, a in ((8, 0), (50, 4)):
                    act.dma_start(area(k * T, 16 * T, BLK), gates[a:a + 4, :, :].rearrange("q p n -> p q n"))\
                        .then_inc(sem("gates_in"), 16)
                act.dma_start(x[:], ins["x"]).then_inc(sem("x_again"), 16)
                with act.Fori(0, 4) as i:
                    for b in range(8):
                        split_hi(act, B0["proj1"] + b + AHEAD, 8, i)
                operand_hi("m1", area(8 * T, 16 * T), hh)
                with act.Fori(0, 2) as i:
                    for b in range(16):
                        split_hi(act, B0["out1"] + b + AHEAD, 16, i)

            def layer2_act():
                act.wait_ge(sem("quad_read"), Q0["out1"] + 4)
                norm_squares("nf", x3)
                hold("nf_part", 1)
                norm_root("nf")
                hold("nf_x", 1)
                norm_squares("n2", x3)
                norm_root("n2")
                hold("ada_mod", 1)
                act.dma_start(con[:, 0:NCON2], ins["con2"]).then_inc(sem("con2_in"), 16)
                act.dma_start(rel, ins["rel"]).then_inc(sem("rel_in"), 16)
                operand_hi("n2", sq, hh)
                hold("rev", 3)
                act.dma_start(revd.rearrange("h (a m) -> h a m", m=384),
                              revs.unsqueeze(1).to_broadcast([SWA_HEADS + 4, P, 384])).then_inc(sem("rev_out"), 16)
                c = B0["lat"]
                at_tile = 0
                for q, (cols, nb) in enumerate(((512, 8), (512, 8), (256, 4), (P, 2))):
                    for b in range(nb):
                        split_hi(act, c + b + AHEAD)
                    c += nb
                    quad_done(act, c)
                    n = cols // P
                    act.activation(tiles(at_tile, n), G[(Q0["lat"] + q) % 2][:, 0:n * T], ACT.Copy)\
                        .then_inc(sem("quad_read"), 1)
                    at_tile += n
                with act.Fori(0, 2) as i:
                    for s in range(2):
                        for b in range(8):
                            split_hi(act, B0["swa"] + 8 * s + b + AHEAD, 16, i)
                        quad_done(act, B0["swa"] + 8 * s + 8, 16, i)
                        act.activation(tile_at(SQ + 4 * s, i, 4, 8), G[(Q0["swa"] + s) % 2][:], ACT.Copy)\
                            .then_inc(sem("quad_read"), 1)
                for b in range(8):
                    split_hi(act, B0["swa"] + 32 + b + AHEAD)
                quad_done(act, B0["swa"] + 40)
                g = G[(Q0["swa"] + 4) % 2]
                for kv in range(SWA_KV):
                    for o in range(2):
                        r = 64 * (kv % 2)
                        act.activation(work[64 * o:64 * o + 64, (SK + kv) * T:(SK + kv + 1) * T],
                                       g[r:r + 64, (kv // 2) * T:(kv // 2 + 1) * T], ACT.Copy).then_inc(sem("swa_k"), 1)
                act.activation(tiles(SV, 2), g[:, 512:1024], ACT.Copy).then_inc(sem("quad_read"), 1)
                swa_act()
                mla_act()
                mix2_act()
                ffn_act()

            def swa_act():
                def bias_in(n, s):
                    act.dma_start(bias[s], revd[bass.ds(2 * n, 2), 127:127 + P * 383]
                                  .rearrange("h (a m) -> a h m", m=383)[:, :, 0:T]).then_inc(sem(f"bias_in{s}"), 16)

                hold("swa_zero", 4)
                act.wait_ge(sem("quad_read"), Q0["gates2"])
                act.wait_ge(sem("rev_out"), 16)
                bias_in(0, 0)
                c = B0["gates2"]
                with act.Fori(0, 4) as i:
                    for p in range(4):
                        n, b0 = 4 * i + p, c + 4 * p

                        def split(b):
                            split_hi(act, b0 + b + AHEAD, 16, i)

                        hold("swa_s", 2 * n)
                        bias_in(n + 1, (p + 1) % 2)
                        hold("swa_qk", n)
                        for h in range(2):
                            r = slice(64 * h, 64 * h + 64)
                            act.activation(qz[r, h, :], work[r, bass.ds(i * 4 * T + (SQ + p) * T, T)], ACT.Copy)\
                                .then_inc(sem("swa_q"), 1)
                        if p == 0:
                            hold("swa_pv", n)
                            act.activation(vst, swv[:, :, bass.ds(i * 64, 64)], ACT.Copy).then_inc(sem("swa_v"), 1)
                        split(0)
                        hold("swa_d", n + 1)
                        act.activation(st[:, 28:32], st[:, 12:16], ACT.Exp).then_inc(sem("swa_es"), 1)
                        for m in range(4):
                            k0 = 0 if m % 2 else P
                            act.activation(p4[:, m, k0:T], s4[:, m, k0:T], ACT.Exp, bias=st[:, 8 + m:9 + m],
                                           accum_out=st[:, 16 + m:17 + m]).then_inc(sem("swa_e"), 1)
                        split(1)
                        hold("swa_t", n + 1)
                        for h in range(2):
                            act.activation(spt[:, 384 * h:384 * h + 384], bank[2 + h][:, 0:384], ACT.Copy)\
                                .then_inc(sem("swa_pt"), 1)
                        split(2)
                        split(3)
                        if p % 2:
                            s = p // 2
                            quad_done(act, c + 8 * s + 8, 16, i)
                            act.wait_ge(sem(f"gate2_out{s}"), 16 * i + 16)
                            act.activation(stage[s], G[(Q0["gates2"] + s) % 2][:], ACT.Sigmoid)\
                                .then_inc(sem("quad_read"), 1)
                            act.wait_ge(sem("quad_read"), at(Q0["gates2"] + s + 1, 2, i))
                            act.dma_start(gates2[bass.ds(2 * i + s, 1), :, :].rearrange("a p n -> p (a n)"), stage[s])\
                                .then_inc(sem(f"gate2_out{s}"), 16)
                act.wait_ge(sem("bias_in0"), 16 * 9)
                act.wait_ge(sem("bias_in1"), 16 * 8)

            def mla_act():
                for n in range(2):
                    act.wait_ge(sem(f"gate2_out{n}"), 80)
                hold("swa_o", 16)
                norm_squares("nq", lat, 6, msq)
                norm_squares("nk", lat[:, 6:10, :], 4, msq[:, 6:10, :])
                norm_root("nq")
                operand_hi("nq", msq, hh, 6, 6)
                norm_root("nk")
                operand_hi("nk", msq[:, 6:10, :], hh[:, 6:10, :], 4, 4)
                for q in range(6):
                    for b in range(3):
                        split_hi(act, B0["uq"] + 3 * q + b + AHEAD)
                    quad_done(act, B0["uq"] + 3 * q + 3)
                    act.activation(tiles(MQ + 4 * q, 4), G[(Q0["uq"] + q) % 2][:], ACT.Copy, scale=MLA_SCALE)\
                        .then_inc(sem("quad_read"), 1)
                c = B0["ukv"]
                with act.Fori(0, 4) as i:
                    for s in range(2):
                        n = 2 * i + s
                        hold("mla_pv", n)
                        for b in range(2):
                            split_hi(act, c + 2 * s + b + AHEAD, 4, i)
                        act.activation(qn.rearrange("p a t -> p (a t)"), tile_at(MQ + 2 * s, i, 2, 4), ACT.Copy)\
                            .then_inc(sem("mla_q"), 1)
                        for h in range(2):
                            r = slice(64 * h, 64 * h + 64)
                            act.activation(qr[r, h, :], work[r, bass.ds(i * 2 * T + (MR + s) * T, T)], ACT.Copy)\
                                .then_inc(sem("mla_qr"), 1)
                        quad_done(act, c + 2 * s + 2, 4, i)
                        g = G[(Q0["ukv"] + s) % 2]
                        act.activation(kn.rearrange("p a t -> p (a t)"), g[:, 0:512], ACT.Copy).then_inc(sem("mla_k"), 1)
                        act.activation(vv.rearrange("p a t -> p (a t)"), g[:, 512:1024], ACT.Copy)\
                            .then_inc(sem("quad_read"), 1)
                        hold("mla_nm", n + 1)
                        for m in range(4):
                            act.activation(mp4[:, m, :], ms4[:, m, :], ACT.Exp, bias=st[:, 8 + m:9 + m],
                                           accum_out=st[:, 16 + m:17 + m]).then_inc(sem("mla_e"), 1)
                        hold("mla_t", n + 1)
                        for h in range(2):
                            act.activation(mpt[:, 384 * h:384 * h + 384], bank[2 + h][:, 0:384], ACT.Copy)\
                                .then_inc(sem("mla_pt"), 1)

            def mix2_act():
                hold("mla_o", 8)
                hold("mla_pv", 8)
                hold("mla_t", 8)
                for k, a in ((47, 0), (63, 4)):
                    act.dma_start(area(k * T, 16 * T, BLK), gates2[a:a + 4, :, :].rearrange("q p n -> p q n"))\
                        .then_inc(sem("gates2_in"), 16)
                operand_hi("m2", area(MQ * T, 16 * T), hh)
                with act.Fori(0, 2) as i:
                    for s in range(2):
                        for b in range(8):
                            split_hi(act, B0["out2"] + 8 * s + b + AHEAD, 16, i)
                        quad_done(act, B0["out2"] + 8 * s + 8, 16, i)
                        act.activation(tile_at(4 * s, i, 4, 8), G[(Q0["out2"] + s) % 2][:], ACT.Copy)\
                            .then_inc(sem("quad_read"), 1)
                act.wait_ge(sem("quad_read"), Q0["out2"] + 4)
                norm_squares("r1", area(0, 16 * T))
                norm_root("r1")

            def ffn_act():
                hold("r1_x", 16)
                norm_squares("n3", x3)
                norm_root("n3")
                operand_hi("n3", sq, hh)
                c = B0["up"]
                with act.Fori(0, 11) as i:
                    for s in range(2):
                        for b in range(8):
                            split_hi(act, c + 8 * s + b + AHEAD, 16, i)
                        quad_done(act, c + 8 * s + 8, 16, i)
                        if s == 0:
                            hold("ffn_y", i)
                        g = G[(Q0["up"] + s) % 2]
                        for k in range(4):
                            col = i * 4 + 44 * s + k
                            act.activation(tiles(44 + 4 * s + k), g[:, k * T:(k + 1) * T], ACT.Identity,
                                           scale=vec[:, bass.ds(col + VEC["conv_w"][0] + 176, 1)],
                                           bias=vec[:, bass.ds(col + VEC["conv_b"][0], 1)]).then_inc(sem("ffn_c"), 1)
                        if s == 0:
                            act.wait_ge(sem("quad_read"), at(Q0["up"] + 1, 2, i))
                            hold("ffn_cv", 14 * i + 7)
                            act.activation(tiles(44, 4), tiles(44, 4), ACT.Silu).then_inc(sem("ffn_z"), 1)
                hold("ffn_y", 11)
                c = B0["down"]

                def y_hi(k, i=None):
                    if k >= 2:
                        act.wait_ge(sem("block_used"), at(c + 4 * (k - 1), 8, i))
                    act.activation(yh[:, 2 * (k % 2):2 * (k % 2) + 2, :].rearrange("p k t -> p (k t)"),
                                   tiles(2 * k, 2) if i is None else tile_at(2 * k, i, 2, 4), ACT.Copy)\
                        .then_inc(sem("y_hi"), 1)

                def turn(k0, i=None, last=False):
                    for k in (k0, k0 + 1):
                        if not (last and k == k0 + 1):
                            y_hi(k + 1, i)
                        for b in range(4):
                            split_hi(act, c + 4 * k + b + AHEAD, 8, i)

                act.wait_ge(sem("block_used"), c)
                y_hi(0)
                turn(0)
                with act.Fori(0, 9) as i:
                    turn(2, i)
                turn(20, last=True)
                act.wait_ge(sem("block_used"), c + 88)
                for g, k in ((G[0], 44), (G[1], 48), (A[0], 52), (A[1], 56)):
                    act.activation(tiles(k, 4), g[:], ACT.Copy).then_inc(sem("down_out"), 1)
                hold("down_out", 4)
                norm_squares("r2", area(44 * T, 16 * T), DT, area(0, 16 * T))
                norm_root("r2")

            hold("vec_loaded", 16)
            act.activation(V("c"), V("c"), ACT.Silu).then_inc(sem("c_silu"), 1)
            hold("x_loaded", 16)
            norm_squares("n1", x3)
            for c in range(AHEAD):
                split_hi(act, c)
            norm_root("n1")
            operand_hi("n1", sq, hh)
            c = B0["fox"]
            for b in range(16):
                split_hi(act, c + b + AHEAD)
                if b % 8 == 7:
                    quad_done(act, c + b + 1)
                    act.activation(foxv[:, :, (b // 8) * 512:(b // 8 + 1) * 512],
                                   G[b // 8][:].rearrange("p (t n) -> p t n", t=TT), ACT.Copy)\
                        .then_inc(sem("quad_read"), 1)
            c += 16
            with act.Fori(0, 3) as i:
                for b in range(16):
                    split_hi(act, c + b + AHEAD, 16, i)
                    if b % 8 == 7:
                        quad_done(act, c + b + 1, 16, i)
                        act.activation(work[:, bass.ds(i * 2048 + (b // 8) * 1024, 1024)], G[b // 8][:],
                                       ACT.Copy).then_inc(sem("quad_read"), 1)
            c = B0["waf"]
            for b in range(4):
                split_hi(act, c + b + AHEAD)
            quad_done(act, c + 4)
            hold("omm", 1)
            for k in range(2):
                act.activation(waf[:, k, :], G[0][:, k * T:(k + 1) * T], ACT.Copy,
                               scale=omm[:, 32 + k:33 + k]).then_inc(sem("waf_own"), 1)
            act.activation(lsg[0], G[0][96:104, 0:T], ACT.Identity, bias=V("fbias")[0:8, :]).then_inc(sem("f_x"), 1)
            hold("f_x", 1)
            act.activation(lsg[1], lsg[0], ACT.Abs).then_inc(sem("f_abs"), 1)
            hold("f_abs", 1)
            act.activation(lsg[1], lsg[1], ACT.Exp, scale=-1.0).then_inc(sem("f_exp"), 1)
            hold("f_exp", 1)
            act.activation(lsg[1], lsg[1], ACT.Ln, bias=1.0).then_inc(sem("f_ln"), 1)
            act.activation(fox[:, 16:24, :], fox[:, 16:24, :], ACT.Silu).then_inc(sem("fox_z"), 1)
            c = B0["rwkv"]
            with act.Fori(0, FOX_HEADS // 2) as i:
                for s in range(2):
                    g, b0 = G[(Q0["rwkv"] + s) % 2], c + 8 * s
                    hold("fox_qk", 2 * i + s)
                    act.activation(fq, tile_at(s, i, 1, 2), ACT.Copy, scale=FOX_SCALE).then_inc(sem("fox_q"), 1)
                    hold("fox_pv", 2 * i + s)
                    act.activation(fv, foxv[:, :, bass.ds(i * 2 * P + s * P, P)], ACT.Copy).then_inc(sem("fox_v"), 1)
                    for b in (0, 1):
                        split_hi(act, b0 + b + AHEAD, 16, i)
                    hold("fox_nm", 2 * i + s + 1)
                    for b in range(TT):
                        act.activation(pr[:, b, :], sc[:, b, :], ACT.Exp, bias=st[:, 2 + b:3 + b],
                                       accum_out=st[:, 4 + b:5 + b]).then_inc(sem("fox_e"), 1)
                    for b in (2, 3, 4):
                        split_hi(act, b0 + b + AHEAD, 16, i)
                    hold("fox_t", 2 * i + s + 1)
                    act.activation(ptf[:, 0:384], bank[1][:, 0:384], ACT.Copy).then_inc(sem("fox_pt"), 1)
                    for b in (5, 6, 7):
                        split_hi(act, b0 + b + AHEAD, 16, i)
                    quad_done(act, b0 + 8, 16, i)
                    for k in range(4):
                        act.activation(tile_at(RR + 4 * s + k, i, 1, 8), g[:, k * T:(k + 1) * T], ACT.Copy,
                                       scale=small[:, bass.ds(i * 8 + 3 * T + 32 + 4 * s + k, 1)])\
                            .then_inc(sem("rw_own"), 1)
            rwkv_act()
            mix1_act()
            layer2_act()

        @blk.vector
        def _(dve):
            hold = waiter(dve)
            prime(dve, "dve")

            def norm_stats(tag, n, tiles=DT, sq=sq):
                hold(tag + "_sq", (tiles + 3) // 4)
                dve.tensor_reduce(stat[0], sq[:, 0:tiles, :].rearrange("p k t -> p t k"), AX.X,
                                  ALU.add).then_inc(sem(tag + "_part"), 1)
                hold(tag + "_sum", 1)
                dve.tensor_scalar(stat[0], bank[0][:, 0:T], 1.0 / n, 1e-6, ALU.mult, ALU.add)\
                    .then_inc(sem(tag + "_ms"), 1)
                hold(tag + "_ms", 1)
                dve.reciprocal(stat[1], stat[0]).then_inc(sem(tag + "_inv"), 1)

            def norm_apply(tag, src, gain, shift, tiles=DT, step=4, sq=sq):
                hold(tag + "_rstd", 1)
                for c in range(0, tiles, step):
                    n = min(step, tiles - c)
                    dve.tensor_tensor(sq[:, c:c + n, :], src[:, c:c + n, :],
                                      stat[2].unsqueeze(1).to_broadcast([P, n, T]), ALU.mult)\
                        .then_inc(sem(tag + "_xr"), 1)
                    hold(tag + "_xr", c // step + 1)
                    for k in range(c, c + n):
                        dve.tensor_scalar(sq[:, k, :], sq[:, k, :], gain[:, k:k + 1],
                                          0.0 if shift is None else shift[:, k:k + 1], ALU.mult, ALU.add)\
                            .then_inc(sem(tag + "_h"), 1)

            def operand_lo(tag, src, hi, dst, tiles=DT, step=4):
                for c in range(0, tiles, step):
                    n = min(step, tiles - c)
                    hold(tag + "_hi", c // step + 1)
                    dve.tensor_tensor(dst[:, c:c + n, :], src[:, c:c + n, :], hi[:, c:c + n, :].bitcast(F32),
                                      ALU.subtract).then_inc(sem(tag + "_lo"), 1)

            def rwkv_dve():
                c = B0["gates1"]
                dve.tensor_scalar(omka, V("k_a"), -1.0, 1.0, ALU.mult, ALU.add).then_inc(sem("rw_omka"), 1)
                hold("rw_omka", 1)
                for o in (ah, rh_):
                    for h in range(2):
                        dve.memset(o[64 - 64 * h:128 - 64 * h, h, :], 0.0).then_inc(sem("rw_zero"), 1)
                with dve.Fori(0, WT // 2) as i:
                    for s in range(2):
                        n, b0 = 2 * i + s, c + 8 * s
                        R, K = tile_at(RR + s, i, 1, 2), tile_at(RK + s, i, 1, 2)

                        def col(name):
                            return vec[:, bass.ds(n + VEC[name][0], 1)]

                        def split(b):
                            split_lo(dve, b0 + b + AHEAD, 16, i)

                        def mul(o, a, b, name, op=ALU.mult):
                            dve.tensor_tensor(o, a, b, op).then_inc(sem(name), 1)

                        def mask(o, b, m, name, units=4):
                            dve.tensor_tensor(o.rearrange("p (u t) -> p u t", t=P), b.rearrange("p (u t) -> p u t", t=P),
                                              m.unsqueeze(1).to_broadcast([P, units, P]), ALU.mult).then_inc(sem(name), 1)

                        dve.tensor_scalar(e1, K, col("k_k"), None, ALU.mult).then_inc(sem("rw_kk0"), 1)
                        hold("rw_sg", n + 1)
                        dve.tensor_scalar(t1, t1, -DECAY_SCALE, None, ALU.mult).then_inc(sem("rw_ld"), 1)
                        hold("rw_ld", n + 1)
                        dve.tensor_tensor_scan(e0, C1("reset"), t1, 0.0, ALU.mult, ALU.add).then_inc(sem("rw_lc"), 1)
                        hold("rw_lc", n + 1)
                        mul(e5, e0, t1, "rw_lp", ALU.subtract)
                        split(0)
                        hold("rw_kks", n + 1)
                        dve.tensor_scalar(e2, bank[1][:, 0:T], 1e-24, None, ALU.max).then_inc(sem("rw_kkm"), 1)
                        hold("rw_kkm", n + 1)
                        dve.reciprocal(e2, e2).then_inc(sem("rw_kkinv"), 1)
                        hold("rw_a", n + 1)
                        dve.tensor_scalar(t1, t2, col("k_a"), small[:, bass.ds(n + 3 * T + 66, 1)], ALU.mult, ALU.add)\
                            .then_inc(sem("rw_kf"), 1)
                        hold("rw_kf", n + 1)
                        mul(t1, t1, K, "rw_kh")
                        hold("rw_kkr", n + 1)
                        mul(e1, e1, e2, "rw_kk")
                        hold("rw_kh", n + 1)
                        hold("rw_kk", n + 1)
                        dve.scalar_tensor_tensor(out=e2, in0=R, scalar=col("r_k"), in1=t1, op0=ALU.mult,
                                                 op1=ALU.mult).then_inc(sem("rw_rk"), 1)
                        mul(t2, t2, e1, "rw_ba")
                        hold("rw_pp", n + 1)
                        dve.scalar_tensor_tensor(out=at_, in0=e1, scalar=-1.0, in1=e5, op0=ALU.mult,
                                                 op1=ALU.mult).then_inc(sem("rw_at"), 1)
                        for h in range(2):
                            f = slice(64 * h, 64 * h + 64)
                            dve.scalar_tensor_tensor(out=ah[f, h, :], in0=e1[f, :], scalar=-1.0, in1=e5[f, :],
                                                     op0=ALU.mult, op1=ALU.mult).then_inc(sem("rw_at"), 1)
                        mul(kt_, t1, en, "rw_kt")
                        hold("rw_ba", n + 1)
                        mul(bt_, t2, en, "rw_bt")
                        mul(rt_, R, ep, "rw_rt")
                        dve.tensor_copy(st[:, 8:12], ep.rearrange("p (c t) -> p c t", t=CHUNK)[:, :, CHUNK - 1])\
                            .then_inc(sem("rw_pc"), 1)
                        split(1)
                        dve.memset(sbd, 0.0).then_inc(sem("rw_s0"), 1)
                        hold("rw_bonus", n + 1)
                        mul(K, bank[1][:, T:2 * T], vf, "rw_bon")
                        hold("rw_l", n + 1)
                        for lv in range(6):
                            mask(low[:, lv].rearrange("p u t -> p (u t)"), bank[0],
                                 C1("m_low")[:, lv * P:(lv + 1) * P], "rw_low")
                        hold("rw_lt", n + 1)
                        mask(um, bank[1], C1("m_u1"), "rw_u0")
                        hold("rw_low", 6 * n + 6)
                        ident4 = C1("ident").unsqueeze(1).to_broadcast([P, 4, P])
                        hold("rw_u0", n + 1)
                        dve.tensor_tensor(um.rearrange("p (u t) -> p u t", t=P), um.rearrange("p (u t) -> p u t", t=P),
                                          ident4, ALU.add).then_inc(sem("rw_u"), 1)
                        dve.tensor_tensor(wm.rearrange("p (u t) -> p u t", t=P), low[:, 0], ident4,
                                          ALU.add).then_inc(sem("rw_w"), 1)
                        split(2)
                        hold("rw_lak", n + 1)
                        mask(lak, bank[2], C1("m_su"), "rw_lakc")
                        hold("rw_rb", n + 1)
                        mask(rb, bank[3], C1("m_ui"), "rw_rbc")
                        hold("rw_rkp", n + 1)
                        mask(rk, bank[0], C1("m_ui"), "rw_rkc")
                        for lv in range(1, 6):
                            hold("rw_du", 5 * n + lv)
                            mul(um, bank[2], um, "rw_u", ALU.add)
                            if lv < 5:
                                hold("rw_dw", 4 * n + lv)
                                mul(wm, bank[3], wm, "rw_w", ALU.add)
                            split(2 + lv)
                        hold("rw_xvc", n + 1)
                        for ch in range(NCH):
                            r = slice((ch % 2) * 64, (ch % 2) * 64 + 64)
                            hold("rw_x0", 4 * n + ch + 1)
                            mul(xs[r, :], bank[1][r, 0:P], xv[r, ch // 2, :], "rw_x", ALU.add)
                            hold("rw_ds", 4 * n + ch + 1)
                            dve.scalar_tensor_tensor(out=sbd, in0=bank[3][:, 0:P], scalar=st[:, 8 + ch:9 + ch],
                                                     in1=C1("bmask"), op0=ALU.mult, op1=ALU.mult)\
                                .then_inc(sem("rw_s"), 1)
                operand_lo("oa", area(0, 8 * T), hh[:, 0:8, :], hl[:, 0:8, :], 8, 8)
                for q in range(4):
                    hold("gn_mean", q + 1)
                    dve.scalar_tensor_tensor(out=tiles(8 + 2 * q, 2), in0=bank[q], scalar=-1.0 / RWKV_HD,
                                             in1=tiles(RR + 2 * q, 2), op0=ALU.mult, op1=ALU.add)\
                        .then_inc(sem("gn_yc"), 1)
                for q in range(4):
                    hold("gn_var", q + 1)
                    o = tiles(16 + 2 * q, 2)
                    dve.tensor_scalar(o, bank[q], 1.0 / RWKV_HD, 64e-5, ALU.mult, ALU.add).then_inc(sem("gn_v"), 1)
                    hold("gn_v", q + 1)
                    dve.reciprocal(o, o).then_inc(sem("gn_inv"), 1)
                hold("gn_rstd", 1)
                dve.tensor_tensor(tiles(8, 8), tiles(8, 8), tiles(16, 8), ALU.mult).then_inc(sem("gn_y"), 1)
                hold("gn_y", 1)
                for k in range(WT):
                    dve.tensor_scalar(tiles(8 + k), tiles(8 + k), V("ln_w", k), V("ln_b", k), ALU.mult, ALU.add)\
                        .then_inc(sem("gn_w"), 1)
                hold("gn_w", 8)
                dve.tensor_tensor(tiles(8, 8), tiles(8, 8), tiles(RK, 8), ALU.add).then_inc(sem("gn_b"), 1)
                hold("gn_b", 1)
                hold("gn_z", 1)
                dve.tensor_tensor(tiles(RR, 8), tiles(8, 8), tiles(RZ, 8), ALU.mult).then_inc(sem("gn_o"), 1)

            def mix1_dve():
                operand_lo("obo", area(RR * T, 8 * T), hh[:, 8:16, :], hl[:, 8:16, :], 8, 8)
                hold("gates_in", 32)
                with dve.Fori(0, 4) as i:
                    for s, k in ((0, 8), (1, 50)):
                        for b in range(4):
                            split_lo(dve, B0["proj1"] + 4 * s + b + AHEAD, 8, i)
                        quad_done(dve, B0["proj1"] + 4 * s + 4, 8, i)
                        dve.tensor_tensor(tile_at(k, i, 4, 4), G[(Q0["proj1"] + s) % 2][:], tile_at(k, i, 4, 4),
                                          ALU.mult).then_inc(sem("quad_read"), 1)
                    dve.wait_ge(sem("quad_read"), at(Q0["proj1"] + 2, 2, i))
                    dve.tensor_tensor(tile_at(8, i, 4, 4), tile_at(8, i, 4, 4), tile_at(50, i, 4, 4), ALU.add)\
                        .then_inc(sem("m1_h"), 4)
                operand_lo("m1", area(8 * T, 16 * T), hh, hl)
                hold("x_again", 16)
                with dve.Fori(0, 2) as i:
                    for s in range(2):
                        for b in range(8):
                            split_lo(dve, B0["out1"] + 8 * s + b + AHEAD, 16, i)
                        quad_done(dve, B0["out1"] + 8 * s + 8, 16, i)
                        xq = x[:, bass.ds(i * 2048 + s * 1024, 1024)]
                        dve.tensor_tensor(xq, G[(Q0["out1"] + s) % 2][:], xq, ALU.add).then_inc(sem("quad_read"), 1)

            def residual(tag, src, gain, ones=None):
                hold(tag + "_rstd", 1)
                dve.tensor_tensor(src, src, stat[2].unsqueeze(1).to_broadcast([P, DT, T]), ALU.mult)\
                    .then_inc(sem(tag + "_xr"), 1)
                hold(tag + "_xr", 1)
                for k in range(DT):
                    dve.scalar_tensor_tensor(out=x3[:, k, :], in0=src[:, k, :], scalar=gain[:, k:k + 1],
                                             in1=x3[:, k, :], op0=ALU.mult, op1=ALU.add).then_inc(sem(tag + "_x"), 1)

            def layer2_dve():
                norm_stats("nf", D)
                norm_apply("nf", x3, V("gf"), None)
                hold("nf_h", DT)
                dve.tensor_copy(x3, sq).then_inc(sem("nf_x"), 1)
                norm_stats("n2", D)
                hold("ada_sum", 12)
                dve.tensor_tensor(mod, bank[3][:, 0:96], V("b_ada"), ALU.add).then_inc(sem("ada_mod"), 1)
                hold("ada_mod", 1)
                for o, sc_, g in ((gg1, 16, "g_pre_mix"), (gg2, 64, "g_pre_ffn")):
                    dve.tensor_scalar(o, mod[:, sc_:sc_ + 16], 1.0, None, ALU.add).then_inc(sem("gain"), 1)
                hold("gain", 2)
                for o, a, g in ((gg1, gg1, "g_pre_mix"), (gg2, gg2, "g_pre_ffn"), (gr1, mod[:, 32:48], "g_post_mix"),
                                (gr2, mod[:, 80:96], "g_post_ffn")):
                    dve.tensor_tensor(o, a, V(g), ALU.mult).then_inc(sem("gain"), 1)
                hold("gain", 6)
                norm_apply("n2", x3, gg1, mod[:, 0:16])
                operand_lo("n2", sq, hh, hl)
                hold("n2_lo", 4)
                hold("rev_p", 1)
                dve.tensor_copy(revs[:, P:2 * P], bank[0][0:36, P:2 * P]).then_inc(sem("rev"), 1)
                dve.memset(revs[:, 0:P], NEG).then_inc(sem("rev"), 1)
                dve.memset(revs[:, 2 * P:3 * P], NEG).then_inc(sem("rev"), 1)
                for o in (qz[64:128, 0, :], qz[0:64, 1, :], p4[:, 0, 0:P], p4[:, 2, 0:P]):
                    dve.memset(o, 0.0).then_inc(sem("swa_zero"), 1)
                for o in (s4[:, 0, 0:P], s4[:, 2, 0:P]):
                    dve.memset(o, NEG).then_inc(sem("swa_neg"), 1)
                for b in range(22):
                    split_lo(dve, B0["lat"] + b + AHEAD)
                with dve.Fori(0, 2) as i:
                    for b in range(16):
                        split_lo(dve, B0["swa"] + b + AHEAD, 16, i)
                for b in range(8):
                    split_lo(dve, B0["swa"] + 32 + b + AHEAD)
                swa_dve()
                mla_dve()
                mix2_dve()
                ffn_dve()

            def swa_dve():
                c = B0["gates2"]
                hold("swa_neg", 2)
                with dve.Fori(0, 4) as i:
                    for p in range(4):
                        n, b0 = 4 * i + p, c + 4 * p

                        def split(b):
                            split_lo(dve, b0 + b + AHEAD, 16, i)

                        split(0)
                        hold("swa_qk", n + 1)
                        dve.wait_ge(sem(f"bias_in{p % 2}"), i * 32 + 16 * (p // 2 + 1))
                        bs = bias[p % 2]
                        for h in range(2):
                            dve.scalar_tensor_tensor(out=s4[:, 2 * h, P:T], in0=bank[h][:, 0:P], scalar=SWA_SCALE,
                                                     in1=bs[:, h, P:T], op0=ALU.mult, op1=ALU.add)\
                                .then_inc(sem("swa_sb"), 1)
                            dve.scalar_tensor_tensor(out=s4[:, 2 * h + 1, :], in0=bank[h][:, P:P + T],
                                                     scalar=SWA_SCALE, in1=bs[:, h, :], op0=ALU.mult, op1=ALU.add)\
                                .then_inc(sem("swa_s"), 1)
                        hold("swa_sb", 2 * n + 2)
                        hold("swa_s", 2 * n + 2)
                        dve.tensor_reduce(st[:, 0:4], s4, AX.X, ALU.max).then_inc(sem("swa_mx"), 1)
                        hold("swa_mx", n + 1)
                        sink = vec[:, bass.ds(2 * n + VEC["sinks"][0], 2)].unsqueeze(2).to_broadcast([P, 2, 2])

                        def two(a):
                            return st[:, a:a + 4].rearrange("p (h b) -> p h b", b=2)

                        dve.tensor_tensor(two(4), two(0), sink, ALU.max).then_inc(sem("swa_m"), 1)
                        hold("swa_m", n + 1)
                        dve.tensor_scalar(st[:, 8:12], st[:, 4:8], -1.0, None, ALU.mult).then_inc(sem("swa_nm"), 1)
                        hold("swa_nm", n + 1)
                        dve.tensor_tensor(two(12), two(8), sink, ALU.add).then_inc(sem("swa_d"), 1)
                        hold("swa_es", n + 1)
                        hold("swa_e", 4 * n + 4)
                        dve.tensor_tensor(st[:, 20:24], st[:, 16:20], st[:, 28:32], ALU.add).then_inc(sem("swa_tot"), 1)
                        hold("swa_tot", n + 1)
                        dve.reciprocal(st[:, 24:28], st[:, 20:24]).then_inc(sem("swa_rs"), 1)
                        hold("swa_rs", n + 1)
                        dve.tensor_tensor(p4, p4, st[:, 24:28].unsqueeze(2).to_broadcast([P, 4, T]), ALU.mult)\
                            .then_inc(sem("swa_p"), 1)
                        split(1)
                        split(2)
                        hold("swa_pv", n + 1)
                        dve.tensor_copy(work[:, bass.ds(i * 4 * T + (SQ + p) * T, T)], bank[0][:, 0:T])\
                            .then_inc(sem("swa_o"), 1)
                        split(3)

            def mla_dve():
                hold("swa_o", 16)
                norm_stats("nq", QR, 6, msq)
                norm_apply("nq", lat, V("g_q"), None, 6, 6, msq)
                norm_stats("nk", KVR, 4, msq[:, 6:10, :])
                operand_lo("nq", msq, hh, hl, 6, 6)
                norm_apply("nk", lat[:, 6:10, :], V("g_kv"), None, 4, 4, msq[:, 6:10, :])
                operand_lo("nk", msq[:, 6:10, :], hh[:, 6:10, :], hl[:, 6:10, :], 4, 4)
                hold("nk_lo", 1)
                for o in (qr[64:128, 0, :], qr[0:64, 1, :]):
                    dve.memset(o, 0.0).then_inc(sem("mla_zero"), 1)

                def rope(src, dst, n):
                    if n:
                        hold("rope", n)
                    hold("rot", n + 1)
                    dve.tensor_tensor(rt1, bank[2][:, 0:T], C2("sin"), ALU.mult).then_inc(sem("rope_s"), 1)
                    dve.tensor_tensor(rt2, src, C2("cos"), ALU.mult).then_inc(sem("rope_c"), 1)
                    hold("rope_s", n + 1)
                    hold("rope_c", n + 1)
                    dve.tensor_tensor(dst, rt1, rt2, ALU.add).then_inc(sem("rope"), 1)

                rope(lat[:, 10, :], krr, 0)
                for b in range(18):
                    split_lo(dve, B0["uq"] + b + AHEAD)
                for k in range(8):
                    rope(tiles(MR + k), tiles(MR + k), k + 1)
                c = B0["ukv"]
                with dve.Fori(0, 4) as i:
                    for s in range(2):
                        n = 2 * i + s
                        for b in range(2):
                            split_lo(dve, c + 2 * s + b + AHEAD, 4, i)
                        hold("mla_qk", n + 1)
                        dve.tensor_tensor(ms4.rearrange("p (h b) t -> p h (b t)", b=2),
                                          A[0][:].rearrange("p (h b) -> p h b", h=2),
                                          C2("causal").unsqueeze(1).to_broadcast([P, 2, 512]), ALU.add)\
                            .then_inc(sem("mla_s"), 1)
                        hold("mla_s", n + 1)
                        dve.tensor_reduce(st[:, 0:4], ms4, AX.X, ALU.max).then_inc(sem("mla_mx"), 1)
                        hold("mla_mx", n + 1)
                        dve.tensor_scalar(st[:, 8:12], st[:, 0:4], -1.0, None, ALU.mult).then_inc(sem("mla_nm"), 1)
                        hold("mla_e", 4 * n + 4)
                        dve.reciprocal(st[:, 24:28], st[:, 16:20]).then_inc(sem("mla_rs"), 1)
                        hold("mla_rs", n + 1)
                        dve.tensor_tensor(mp4, mp4, st[:, 24:28].unsqueeze(2).to_broadcast([P, 4, T]), ALU.mult)\
                            .then_inc(sem("mla_p"), 1)
                        hold("mla_pv", n + 1)
                        dve.tensor_copy(tile_at(MQ + 2 * s, i, 2, 4), bank[0]).then_inc(sem("mla_o"), 1)

            def mix2_dve():
                hold("gates2_in", 32)
                oa, ob, ga, gb = (tiles(k, 16) for k in (MQ, SQ, 47, 63))
                for h in range(2):
                    for o, g in ((oa, ga), (ob, gb)):
                        r = slice(h * 8 * T, (h + 1) * 8 * T)
                        dve.tensor_tensor(o[:, r], o[:, r], g[:, r], ALU.mult).then_inc(sem("m2_g"), 1)
                    hold("m2_g", 2 * h + 2)
                    dve.tensor_tensor(oa[:, r], oa[:, r], ob[:, r], ALU.add).then_inc(sem("m2_h"), 8)
                operand_lo("m2", area(MQ * T, 16 * T), hh, hl)
                with dve.Fori(0, 2) as i:
                    for b in range(16):
                        split_lo(dve, B0["out2"] + b + AHEAD, 16, i)
                norm_stats("r1", D)
                residual("r1", area(0, 16 * T), gr1)

            def ffn_dve():
                norm_stats("n3", D)
                norm_apply("n3", x3, gg2, mod[:, 48:64])
                operand_lo("n3", sq, hh, hl)
                c = B0["up"]
                with dve.Fori(0, 11) as i:
                    for s in range(2):
                        for b in range(8):
                            split_lo(dve, c + 8 * s + b + AHEAD, 16, i)
                        hold("ffn_c", 8 * i + 4 * s + 4)
                        g = G[(Q0["up"] + s) % 2]
                        for j in (1, 2):
                            for k in range(4):
                                col = i * 4 + 44 * s + k
                                if j == 2:
                                    hold("ffn_cv", 14 * i + 7 * s + k + 1)
                                o = tiles(44 + 4 * s + k)[:, j:T]
                                dve.scalar_tensor_tensor(
                                    out=o, in0=g[:, k * T:(k + 1) * T - j],
                                    scalar=vec[:, bass.ds(col + VEC["conv_w"][0] + 88 * (2 - j), 1)], in1=o,
                                    op0=ALU.mult, op1=ALU.add)\
                                    .then_inc(sem("quad_read" if j == 2 and k == 3 else "ffn_cv"), 1)
                    dve.wait_ge(sem("quad_read"), at(Q0["up"] + 2, 2, i))
                    hold("ffn_z", i + 1)
                    dve.tensor_tensor(tile_at(0, i, 4, 4), tiles(44, 4), tiles(48, 4), ALU.mult)\
                        .then_inc(sem("ffn_y"), 1)
                c = B0["down"]

                def y_lo(k, i=None):
                    hold("y_hi", at(k + 1, 2, i))
                    r = slice(2 * (k % 2), 2 * (k % 2) + 2)
                    dve.tensor_tensor(yl[:, r, :].rearrange("p k t -> p (k t)"),
                                      tiles(2 * k, 2) if i is None else tile_at(2 * k, i, 2, 4),
                                      yh[:, r, :].rearrange("p k t -> p (k t)").bitcast(F32), ALU.subtract)\
                        .then_inc(sem("y_lo"), 1)

                def turn(k0, i=None, last=False):
                    for k in (k0, k0 + 1):
                        if not (last and k == k0 + 1):
                            y_lo(k + 1, i)
                        for b in range(4):
                            split_lo(dve, c + 4 * k + b + AHEAD, 8, i)

                y_lo(0)
                turn(0)
                with dve.Fori(0, 9) as i:
                    turn(2, i)
                turn(20, last=True)
                norm_stats("r2", D, DT, area(0, 16 * T))
                residual("r2", area(44 * T, 16 * T), gr2)

            hold("vec_loaded", 16)
            dve.tensor_scalar(omm, vec[:, VEC["mu"][0]:VEC["mu"][0] + 34], -1.0, 1.0, ALU.mult, ALU.add).then_inc(sem("omm"), 1)
            norm_stats("n1", D)
            for c in range(AHEAD):
                split_lo(dve, c)
            norm_apply("n1", x3, V("g1"), None)
            operand_lo("n1", sq, hh, hl)
            c = B0["fox"]
            for b in range(16):
                split_lo(dve, c + b + AHEAD)
            with dve.Fori(0, 3) as i:
                for b in range(16):
                    split_lo(dve, c + 16 + b + AHEAD, 16, i)
            c = B0["waf"]
            for b in range(4):
                split_lo(dve, c + b + AHEAD)
            for k in range(2):
                hold("waf_own", 2)
                hold("f_x", 1)
                dve.scalar_tensor_tensor(out=waf[:, k, 1:T], in0=G[0][:, k * T:(k + 1) * T - 1],
                                         scalar=V("mu_w" if k == 0 else "mu_a"), in1=waf[:, k, 1:T],
                                         op0=ALU.mult, op1=ALU.add).then_inc(sem("waf_mix" if k == 0 else "quad_read"), 1)
            hold("f_ln", 1)
            dve.tensor_scalar(lsg[2], lsg[0], 0.0, None, ALU.min).then_inc(sem("f_min"), 1)
            dve.memset(aug_l, 0.0).then_inc(sem("aug_z"), 1)
            dve.memset(aug_r, 0.0).then_inc(sem("aug_z"), 1)
            dve.memset(lsg[3], 1.0).then_inc(sem("aug_z"), 1)
            hold("f_min", 1)
            dve.tensor_tensor(lsg[2], lsg[2], lsg[1], ALU.subtract).then_inc(sem("f_log"), 1)
            hold("f_log", 1)
            hold("aug_z", 3)
            dve.tensor_tensor_scan(aug_l[0:8, :], lsg[3], lsg[2], 0.0, ALU.mult, ALU.add).then_inc(sem("f_sum"), 1)
            dve.memset(aug_l[32:40, :], 1.0).then_inc(sem("aug_1"), 1)
            dve.memset(aug_r[0:8, :], 1.0).then_inc(sem("aug_1"), 1)
            hold("f_sum", 1)
            dve.tensor_scalar(aug_r[32:40, :], aug_l[0:8, :], -1.0, None, ALU.mult).then_inc(sem("aug_1"), 1)
            hold("aug_1", 3)
            hold("fox_z", 1)
            c = B0["rwkv"]
            with dve.Fori(0, FOX_HEADS // 2) as i:
                for s in range(2):
                    g, b0 = G[(Q0["rwkv"] + s) % 2], c + 8 * s
                    n = 2 * i + s
                    hold("fox_qk", n)
                    dve.tensor_scalar(aug_h, aug_r, con[0:40, bass.ds(2 * i + s + CON1["selcol"][0], 1)], None,
                                      ALU.mult).then_inc(sem("fox_aug"), 1)
                    for b in (0, 1):
                        split_lo(dve, b0 + b + AHEAD, 16, i)
                    hold("fox_qk", n + 1)
                    hold("fox_e", n * 2)
                    dve.tensor_tensor(scf, bank[0], C1("causal"), ALU.add).then_inc(sem("fox_s"), 1)
                    hold("fox_s", n + 1)
                    dve.tensor_reduce(st[:, 0:2], sc, AX.X, ALU.max).then_inc(sem("fox_mx"), 1)
                    hold("fox_mx", n + 1)
                    dve.tensor_scalar(st[:, 2:4], st[:, 0:2], -1.0, None, ALU.mult).then_inc(sem("fox_nm"), 1)
                    hold("fox_e", n * 2 + 2)
                    dve.reciprocal(st[:, 6:8], st[:, 4:6]).then_inc(sem("fox_rs"), 1)
                    hold("fox_rs", n + 1)
                    dve.tensor_scalar(pr[:, 0, 0:P], pr[:, 0, 0:P], st[:, 6:7], None, ALU.mult)\
                        .then_inc(sem("fox_p"), 1)
                    dve.tensor_scalar(pr[:, 1, :], pr[:, 1, :], st[:, 7:8], None, ALU.mult).then_inc(sem("fox_p"), 1)
                    for b in (2, 3, 4, 5):
                        split_lo(dve, b0 + b + AHEAD, 16, i)
                    hold("fox_pv", n + 1)
                    dve.tensor_tensor(tile_at(s, i, 1, 2), bank[2][:, 0:T], tile_at(16 + s, i, 1, 2), ALU.mult)\
                        .then_inc(sem("fox_o"), 1)
                    for b in (6, 7):
                        split_lo(dve, b0 + b + AHEAD, 16, i)
                    hold("rw_own", n * 4 + 4)
                    for k in range(4):
                        o = i * (8 * T) + (RR + 4 * s + k) * T + 1
                        dve.scalar_tensor_tensor(
                            out=work[:, bass.ds(o, T - 1)], in0=g[:, k * T:(k + 1) * T - 1],
                            scalar=vec[:, bass.ds(i * 8 + VEC["mu"][0] + 4 * s + k, 1)], in1=work[:, bass.ds(o, T - 1)],
                            op0=ALU.mult, op1=ALU.add).then_inc(sem("rw_shift" if k < 3 else "quad_read"), 1)
            rwkv_dve()
            mix1_dve()
            layer2_dve()

        @blk.tensor
        def _(pe):
            hold = waiter(pe)
            prime(pe, "pe")

            def norm_sum(tag):
                hold(tag + "_part", 1)
                pe.matmul(bank[0][:, 0:T], C1("ones") if tag in ("n1", "nf", "n2") else C2("ones"), stat[0], start=True,
                          stop=True).then_inc(sem(tag + "_sum"), 1)

            def rwkv_pe():
                c, q = B0["gates1"], Q0["gates1"]
                hold("tanh_w", 1)
                hold("rw_zero", 4)
                pe.wait_ge(sem("quad_read"), Q0["rwkv"])
                with pe.Fori(0, WT // 2) as i:
                    for s in range(2):
                        n, g = 2 * i + s, (q + s) % 2

                        def part(b):
                            if b == 0:
                                pe.wait_ge(sem("quad_read"), at(q + s - 1, 2, i))
                            block(pe, c + 8 * s + b, 16, i, 512, hh, hl, 2 * b, g, b == 0, b == NQ - 1)

                        def mm(o, l, r, start=True, stop=True):
                            return pe.matmul(o, l, r, start=start, stop=stop, skip_group_check=True)

                        def gram(o, l, r, name):
                            for u in range(4):
                                t = slice(P * (u % 2), P * (u % 2) + P)
                                m = mm(o[:, u * P:(u + 1) * P], l[:, t] if l is bt_ or l is kt_ else l[:, u // 2, t],
                                       r[:, t] if r is bt_ else r[:, u // 2, t], start=u == 0)
                            m.then_inc(sem(name), 1)

                        pe.wait_ge(sem("lora_in"), 16 * n + 16)
                        hold("rw_y", n)
                        mm(bank[0][:, 0:T], lw[:, 0:P], waf[0:LORA, 0, :])
                        mm(bank[0][:, T:2 * T], lw[:, P:2 * P], waf[0:LORA, 1, :], start=False)\
                            .then_inc(sem("rw_lora"), 1)
                        part(0)
                        hold("rw_kk2", n + 1)
                        mm(bank[1][:, 0:T], C1("bones"), e2).then_inc(sem("rw_kks"), 1)
                        part(1)
                        hold("rw_rk", n + 1)
                        mm(bank[1][:, T:2 * T], C1("bones"), e2, start=False).then_inc(sem("rw_bonus"), 1)
                        hold("rw_bt", n + 1)
                        hold("rw_kt", n + 1)
                        for m, src in enumerate((bt_, bt_, kt_, kt_)):
                            t = pe.transpose(bank[2][:, m * P:(m + 1) * P], src[:, (m % 2) * P:(m % 2 + 1) * P],
                                             C1("ident"))
                        t.then_inc(sem("rw_tr"), 1)
                        hold("rw_v", n + 1)
                        for m in range(2):
                            t = pe.transpose(bank[3][:, m * P:(m + 1) * P], vf[:, m * P:(m + 1) * P], C1("ident"))
                        t.then_inc(sem("rw_trv"), 1)
                        hold("rw_a", n + 1)
                        hold("rw_at", 3 * n + 3)
                        gram(bank[0], ah, bt_, "rw_l")
                        hold("rw_bon", n + 1)
                        gram(bank[1], bt_, ah, "rw_lt")
                        hold("rw_tok", n + 1)
                        gram(bank[2], kt_, ah, "rw_lak")
                        hold("rw_vtok", n + 1)
                        hold("rw_rh", 2 * n + 2)
                        gram(bank[3], bt_, rh_, "rw_rb")
                        part(2)
                        hold("rw_low", 6 * n + 6)
                        gram(bank[0], kt_, rh_, "rw_rkp")
                        for lv in range(1, 6):
                            hold("rw_u", 6 * n + lv)
                            for u in range(4):
                                m = mm(bank[1][:, u * P:(u + 1) * P], low[:, lv, u, :], um[:, u * P:(u + 1) * P],
                                       start=u == 0)
                            m.then_inc(sem("rw_g"), 1)
                            hold("rw_gc", 5 * n + lv)
                            hold("rw_w", 5 * n + lv)
                            hold("rw_rbc", n + 1)
                            for u in range(4):
                                m = mm(bank[2][:, u * P:(u + 1) * P], wm[:, u * P:(u + 1) * P],
                                       gm[:, u * P:(u + 1) * P], start=u == 0)
                            m.then_inc(sem("rw_du"), 1)
                            if lv < 5:
                                for u in range(4):
                                    m = mm(bank[3][:, u * P:(u + 1) * P], gm[:, u * P:(u + 1) * P],
                                           wm[:, u * P:(u + 1) * P], start=u == 0)
                                m.then_inc(sem("rw_dw"), 1)
                            part(2 + lv)
                        hold("rw_rkc", n + 1)
                        for u in range(4):
                            h, t = u // 2, u % 2
                            m = mm(bank[0][:, t * P + 64 * h:t * P + 64 * h + 64], lak[:, u * P:(u + 1) * P],
                                   vtok[:, t, 64 * h:64 * h + 64], start=u == 0)
                        m.then_inc(sem("rw_xv"), 1)
                        hold("rw_u", 6 * n + 6)
                        hold("rw_s0", n + 1)
                        hold("rw_xvc", n + 1)
                        for ch in range(NCH):
                            r0, t = (ch % 2) * 64, ch // 2
                            r, k = slice(r0, r0 + 64), slice(ch * CHUNK, (ch + 1) * CHUNK)
                            if ch:
                                hold("rw_s", 4 * n + ch)
                            mm(bank[1][r, 0:P], at_[:, k], sbd).then_inc(sem("rw_x0"), 1)
                            mm(bank[0][:, k], sbd, rt_[:, k], start=ch == 0, stop=False)
                            hold("rw_x", 4 * n + ch + 1)
                            mm(bank[3][:, 0:P], C1("ident"), sbd, stop=False)
                            for h in range(2):
                                u = 2 * h + t
                                m = mm(bank[2][r, 64 * h:64 * h + 64], um[r, u * P + r0:u * P + r0 + 64],
                                       xs[r, 64 * h:64 * h + 64], start=h == 0)
                            m.then_inc(sem("rw_sa"), 1)
                            mm(bank[3][:, 0:P], ktok[r, t, :], vtok[r, t, :], start=False, stop=False)
                            hold("rw_sac", 4 * n + ch + 1)
                            mm(bank[3][:, 0:P], btok[r, t, :], sa[r, t, :], start=False).then_inc(sem("rw_ds"), 1)
                        for u in range(4):
                            h, t = u // 2, u % 2
                            o = bank[0][64 * h:64 * h + 64, t * P:(t + 1) * P]
                            mm(o, sa[:, t, 64 * h:64 * h + 64], rb[:, u * P:(u + 1) * P], start=False, stop=False)
                            m = mm(o, vtok[:, t, 64 * h:64 * h + 64], rk[:, u * P:(u + 1) * P], start=False)
                        m.then_inc(sem("rw_yp"), 1)
                for q in range(4):
                    hold("rw_y", 8)
                    if q:
                        hold("rw_s", 32)
                    pe.matmul(bank[q], C1("bones"), tiles(RR + 2 * q, 2), start=True, stop=True)\
                        .then_inc(sem("gn_mean"), 1)
                for q in range(4):
                    hold("gn_sq", q + 1)
                    pe.matmul(bank[q], C1("bones"), tiles(16 + 2 * q, 2), start=True, stop=True)\
                        .then_inc(sem("gn_var"), 1)

            def mix1_pe():
                hold("oa_lo", 1)
                hold("obo_lo", 1)
                with pe.Fori(0, 4) as i:
                    for s in range(2):
                        quad_pe(pe, B0["proj1"] + 4 * s, 8, i, Q0["proj1"] + s, 2, (Q0["proj1"] + s) % 2, nb=4,
                                rh=hh[:, 8 * s:8 * s + 8, :], rl=hl[:, 8 * s:8 * s + 8, :])
                hold("m1_lo", 4)
                with pe.Fori(0, 2) as i:
                    for s in range(2):
                        quad_pe(pe, B0["out1"] + 8 * s, 16, i, Q0["out1"] + s, 2, (Q0["out1"] + s) % 2)

            def layer2_pe():
                norm_sum("nf")
                hold("nf_ms", 1)
                norm_sum("n2")
                for g in range(12):
                    s = g % 4
                    src = (adaw if s < 2 else adap)[:, (s % 2) * 1024:(s % 2 + 1) * 1024]
                    pe.wait_ge(sem(f"ada_back{s}"), 16 * (g // 4 + 1))
                    for j in range(8):
                        m = pe.matmul(bank[3][:, 8 * g + j:8 * g + j + 1], src[:, j * P:(j + 1) * P],
                                      C1("ones")[:, 0:1], start=g == 0 and j == 0, stop=True, skip_group_check=True)
                    m.then_inc(sem("ada_sum"), 1)
                hold("n2_ms", 1)
                hold("con2_in", 16)
                hold("rel_in", 16)
                pe.matmul(bank[0][0:36, 0:384], rel, C2("onehot", BUCKETS), start=True, stop=True)\
                    .then_inc(sem("rev_p"), 1)
                hold("n2_lo", 4)
                c, q = B0["lat"], Q0["lat"]
                for cols, nb in ((512, 8), (512, 8), (256, 4), (P, 2)):
                    quad_pe(pe, c, 0, None, q, 0, q % 2, cols, nb)
                    c, q = c + nb, q + 1
                with pe.Fori(0, 2) as i:
                    for s in range(2):
                        quad_pe(pe, B0["swa"] + 8 * s, 16, i, Q0["swa"] + s, 2, (Q0["swa"] + s) % 2)
                q = Q0["swa"] + 4
                pe.wait_ge(sem("quad_read"), q - 1)
                for b in range(8):
                    block(pe, B0["swa"] + 32 + b, 0, None, 512, hh, hl, 2 * b, q % 2, b == 0, b == 7,
                          parts=((False, 0, 0), (False, 1, T), (True, slice(256, 512), 512)))
                swa_pe()
                mla_pe()
                mix2_pe()
                ffn_pe()

            def swa_pe():
                c, q = B0["gates2"], Q0["gates2"]
                hold("swa_k", 8)
                pe.wait_ge(sem("quad_read"), q)
                with pe.Fori(0, 4) as i:
                    for p in range(4):
                        n = 4 * i + p
                        s = p // 2

                        def part(b):
                            if p % 2 == 0 and b == 0:
                                pe.wait_ge(sem("quad_read"), at(q + s - 1, 2, i))
                            b += 4 * (p % 2)
                            block(pe, c + 8 * s + b, 16, i, 512, hh, hl, 2 * b, (q + s) % 2, b == 0, b == NQ - 1)

                        def mm(o, l, r, start):
                            return pe.matmul(o, l, r, start=start, stop=True, skip_group_check=True)

                        hold("swa_q", 2 * n + 2)
                        hold("swa_o", n)
                        for h in range(2):
                            mm(bank[h][:, 0:P], qz[:, h, 0:P], work[:, bass.ds(i * T + SK * T, P)], True)
                            m = mm(bank[h][:, P:P + T], qz[:, h, P:T], work[:, bass.ds(i * T + SK * T, T)], False)
                        m.then_inc(sem("swa_qk"), 1)
                        part(0)
                        hold("swa_p", n + 1)
                        hold("swa_pt", 2 * n)
                        for h in range(2):
                            for j, (b, k) in enumerate(((0, 1), (1, 0), (1, 1))):
                                m = pe.transpose(bank[2 + h][:, j * P:(j + 1) * P],
                                                 p4[:, 2 * h + b, k * P:(k + 1) * P], C2("ident"))
                        m.then_inc(sem("swa_t"), 1)
                        part(1)
                        part(2)
                        hold("swa_pt", 2 * n + 2)
                        hold("swa_v", i + 1)
                        for h in range(2):
                            o = bank[0][64 * h:64 * h + 64, :]
                            pt3 = spt[:, 384 * h:384 * h + 384]
                            mm(o[:, 0:P], vst[:, 0, :], pt3[:, 0:P], True)
                            mm(o[:, P:T], vst[:, 0, :], pt3[:, P:2 * P], False)
                            m = mm(o[:, P:T], vst[:, 1, :], pt3[:, 2 * P:3 * P], False)
                        m.then_inc(sem("swa_pv"), 1)
                        part(3)

            def mla_pe():
                hold("nq_part", 1)
                pe.matmul(bank[0][:, 0:T], C2("ones"), stat[0], start=True, stop=True).then_inc(sem("nq_sum"), 1)
                hold("nk_part", 1)
                pe.matmul(bank[0][:, 0:T], C2("ones"), stat[0], start=True, stop=True).then_inc(sem("nk_sum"), 1)
                pe.matmul(bank[2][:, 0:T], C2("rot"), lat[:, 10, :], start=True, stop=True).then_inc(sem("rot"), 1)
                hold("nq_lo", 1)
                for q in range(6):
                    quad_pe(pe, B0["uq"] + 3 * q, 0, None, Q0["uq"] + q, 0, (Q0["uq"] + q) % 2, nb=3)
                pe.wait_ge(sem("quad_read"), Q0["uq"] + 6)
                for k in range(8):
                    hold("rope_s", k + 1)
                    pe.matmul(bank[2][:, 0:T], C2("rot"), tiles(MR + k), start=True, stop=True).then_inc(sem("rot"), 1)
                hold("nk_lo", 1)
                hold("rope", 9)
                c, q = B0["ukv"], Q0["ukv"]
                with pe.Fori(0, 4) as i:
                    for s in range(2):
                        n = 2 * i + s
                        pe.wait_ge(sem("quad_read"), at(q + s - 1, 2, i))
                        for b in range(2):
                            block(pe, c + 2 * s + b, 4, i, 512, hh[:, 6:10, :], hl[:, 6:10, :], 2 * b, (q + s) % 2,
                                  b == 0, b == 1, parts=((False, 0, 0), (False, 2, T), (True, "v", 512)))

                        def mm(o, l, r, start):
                            return pe.matmul(o, l, r, start=start, stop=True, skip_group_check=True)

                        hold("mla_q", n + 1)
                        hold("mla_qr", 2 * n + 2)
                        hold("mla_k", n + 1)
                        hold("mla_o", n)
                        for h in range(2):
                            for b in range(2):
                                o = bank[h][:, b * T:(b + 1) * T]
                                mm(o, qn[:, h, b * P:(b + 1) * P], kn[:, h, :], b == 0)
                                m = mm(o, qr[:, h, b * P:(b + 1) * P], krr, False)
                        m.then_inc(sem("mla_qk"), 1)
                        hold("mla_p", n + 1)
                        hold("mla_pt", 2 * n)
                        for h in range(2):
                            for j, (b, k) in enumerate(((0, 0), (1, 0), (1, 1))):
                                m = pe.transpose(bank[2 + h][:, j * P:(j + 1) * P],
                                                 mp4[:, 2 * h + b, k * P:(k + 1) * P], C2("ident"))
                        m.then_inc(sem("mla_t"), 1)
                        hold("mla_pt", 2 * n + 2)
                        pe.wait_ge(sem("quad_read"), at(q + s + 1, 2, i))
                        for h in range(2):
                            o = bank[0][:, h * T:(h + 1) * T]
                            pt3 = mpt[:, 384 * h:384 * h + 384]
                            v0, v1 = (vv[:, t, h * P:(h + 1) * P] for t in range(2))
                            mm(o[:, 0:P], v0, pt3[:, 0:P], h == 0)
                            mm(o[:, P:T], v0, pt3[:, P:2 * P], False)
                            m = mm(o[:, P:T], v1, pt3[:, 2 * P:3 * P], False)
                        m.then_inc(sem("mla_pv"), 1)

            def mix2_pe():
                hold("m2_lo", 4)
                with pe.Fori(0, 2) as i:
                    for s in range(2):
                        quad_pe(pe, B0["out2"] + 8 * s, 16, i, Q0["out2"] + s, 2, (Q0["out2"] + s) % 2)
                norm_sum("r1")

            def ffn_pe():
                hold("r1_x", 1)
                norm_sum("n3")
                hold("n3_lo", 4)
                with pe.Fori(0, 11) as i:
                    for s in range(2):
                        quad_pe(pe, B0["up"] + 8 * s, 16, i, Q0["up"] + s, 2, (Q0["up"] + s) % 2)
                c = B0["down"]
                pe.wait_ge(sem("quad_read"), Q0["up"] + 22)

                def turn(k0, i=None, first=False, last=False):
                    for k in (k0, k0 + 1):
                        hold("y_lo", at(k + 1, 2, i))
                        for b, g in enumerate((G[0], G[1], A[0], A[1])):
                            block(pe, c + 4 * k + b, 8, i, 512, yh, yl, 2 * (k % 2), g, first and k == k0,
                                  last and k == k0 + 1)

                turn(0, first=True)
                with pe.Fori(0, 9) as i:
                    turn(2, i)
                turn(20, last=True)
                norm_sum("r2")

            hold("con_loaded", 16)
            norm_sum("n1")
            hold("n1_lo", 4)
            c, q = B0["fox"], Q0["fox"]
            for s in range(2):
                quad_pe(pe, c + 8 * s, 0, None, q + s, 0, s, token=True)
            with pe.Fori(0, 3) as i:
                for s in range(2):
                    quad_pe(pe, c + 16 + 8 * s, 16, i, q + 2 + s, 2, s)
            quad_pe(pe, B0["waf"], 0, None, Q0["waf"], 0, 0, cols=256, nb=4)
            c, q = B0["rwkv"], Q0["rwkv"]
            hold("fox_z", 1)
            with pe.Fori(0, FOX_HEADS // 2) as i:
                for s in range(2):
                    n, g = 2 * i + s, (q + s) % 2

                    def part(b0, b1):
                        for b in range(b0, b1):
                            block(pe, c + 8 * s + b, 16, i, 512, hh, hl, 2 * b, g, b == 0, b == NQ - 1)

                    hold("fox_q", n + 1)
                    hold("fox_aug", n + 1)
                    hold("fox_s", n)
                    for b in range(TT):
                        o = bank[0][:, b * T:(b + 1) * T]
                        pe.matmul(o, fq[:, b * P:(b + 1) * P], tile_at(8 + s, i, 1, 2), start=b == 0,
                                  stop=False, skip_group_check=True)
                        mm = pe.matmul(o, aug_l[:, b * P:(b + 1) * P], aug_h, start=False, stop=True,
                                       skip_group_check=True)
                    mm.then_inc(sem("fox_qk"), 1)
                    pe.wait_ge(sem("quad_read"), at(q + s - 1, 2, i))
                    part(0, 3)
                    hold("fox_p", n * 2 + 2)
                    hold("fox_pt", n)
                    for m, (b, k) in enumerate(((0, 0), (1, 0), (1, 1))):
                        mm = pe.transpose(bank[1][:, m * P:(m + 1) * P], pr[:, b, k * P:(k + 1) * P], C1("ident"))
                    mm.then_inc(sem("fox_t"), 1)
                    part(3, 5)
                    hold("fox_pt", n + 1)
                    hold("fox_v", n + 1)
                    hold("fox_o", n)
                    o = bank[2]
                    pe.matmul(o[:, 0:P], fv[:, 0, :], ptf[:, 0:P], start=True, stop=True, skip_group_check=True)
                    pe.matmul(o[:, P:T], fv[:, 0, :], ptf[:, P:2 * P], start=False, stop=False, skip_group_check=True)
                    pe.matmul(o[:, P:T], fv[:, 1, :], ptf[:, 2 * P:3 * P], start=False, stop=True,
                              skip_group_check=True).then_inc(sem("fox_pv"), 1)
                    part(5, 8)
            rwkv_pe()
            mix1_pe()
            layer2_pe()


def _blocks(w, cols, token=False):
    k, n = w.shape
    ks = BLK // cols
    b = w.reshape(k // (ks * P), ks, P, n // cols, cols).transpose(3, 0, 2, 1, 4)
    return b.reshape(-1, P, BLK)


def _cols(v, tiles):
    return np.ascontiguousarray(v.reshape(tiles, P).T)


def _layout(a):
    f = np.float32
    wi = a["w_in"][0]
    o = {"q": 0, "k": W1, "v": 2 * W1, "z": 3 * W1, "f": 4 * W1}
    r0 = FOX_COLS
    lora = r0 + 4 * W1
    zero = np.zeros((D, 1), f)
    waf = np.concatenate([wi[:, lora:lora + LORA], wi[:, 4 * W1:FOX_COLS], np.repeat(zero, 24, 1),
                          wi[:, lora + LORA:lora + 2 * LORA], np.repeat(zero, 32, 1)], 1)
    g0 = FOX_COLS + RWKV_COLS
    parts = [_blocks(np.concatenate([wi[:, 2 * W1:3 * W1], wi[:, 0:2 * W1], wi[:, 3 * W1:4 * W1]], 1), 512),
             _blocks(waf, 256), _blocks(wi[:, r0:r0 + 4 * W1], 512)]
    pf, pr_, wo = a["w_proj_fox"][0], a["w_proj_rwkv"][0], a["w_out"][0]
    parts.append(_blocks(wi[:, g0:g0 + 2 * D], 512))
    for q in range(4):
        s = slice(512 * q, 512 * q + 512)
        parts += [_blocks(pf[:, s], 512), _blocks(pr_[:, s], 512)]
    parts.append(_blocks(wo, 512))
    w2 = a["w_in_2"][0]
    lat = QR + KVR
    kr = w2[:, lat:lat + ROPE]
    parts += [_blocks(w2[:, 0:1024], 512), _blocks(w2[:, 1024:lat], 256), _blocks(np.concatenate([kr, kr], 1), 128)]
    s0 = lat + ROPE
    parts.append(_blocks(w2[:, s0:s0 + 2048 + 512], 512))
    parts.append(_blocks(w2[:, s0 + 2560:s0 + 2560 + 2 * D], 512))
    uq = a["w_uq_2"][0].reshape(QR, MLA_HEADS, 192)
    uq = np.concatenate([uq[:, :, :P].reshape(QR, -1), uq[:, :, P:].reshape(QR, -1)], 1)
    parts.append(_blocks(uq, 512))
    parts.append(_blocks(a["w_ukv_2"][0], 512))
    parts.append(_blocks(a["w_o_2"][0], 512))
    up = a["w_up_2"][0]
    for q in range(11):
        parts += [_blocks(up[:, 512 * q:512 * q + 512], 512), _blocks(up[:, D_FF + 512 * q:D_FF + 512 * q + 512], 512)]
    down = a["w_down_2"][0]
    parts.append(down.reshape(22, 2, P, 4, 512).transpose(0, 3, 2, 1, 4).reshape(-1, P, BLK))
    w = np.concatenate(parts, 0)
    assert w.shape == (NBLK, P, BLK), w.shape

    def pad(v):
        return np.concatenate([v.reshape(-1), np.zeros(P - v.size, f)])[:, None]

    mu = a["rwkv_shift_mix"][0]
    v = {
        "g1": _cols(a["norm_gain"], 16), "mu": _cols(mu[:4 * W1], 32), "mu_w": pad(mu[4 * W1:4 * W1 + LORA]),
        "mu_a": pad(mu[4 * W1 + LORA:]), "fbias": pad(a["fox_forget_bias"]), "w0": _cols(a["rwkv_w0"], 8),
        "a0": _cols(a["rwkv_a0"], 8), "k_k": _cols(a["rwkv_k_k"], 8), "k_a": _cols(a["rwkv_k_a"], 8),
        "r_k": _cols(a["rwkv_r_k"], 8), "ln_w": _cols(a["rwkv_ln_w"], 8), "ln_b": _cols(a["rwkv_ln_b"], 8),
        "gf": _cols(a["final_norm_gain"], 16), "c": _cols(a["c_2"], 16), "b_ada": _cols(a["b_ada_2"], 96),
        "g_pre_mix": _cols(a["g_pre_mix_2"], 16), "g_post_mix": _cols(a["g_post_mix_2"], 16),
        "g_q": _cols(a["g_q_lat_2"], 6), "g_kv": _cols(a["g_kv_lat_2"], 4),
        "sinks": np.repeat(a["sinks_2"].reshape(1, -1), P, 0), "g_pre_ffn": _cols(a["g_pre_ffn_2"], 16),
        "g_post_ffn": _cols(a["g_post_ffn_2"], 16),
        "conv_w": np.concatenate([_cols(a["conv_w_2"][0, j], 88) for j in range(3)], 1),
        "conv_b": _cols(a["conv_b_2"], 88),
    }
    c1, c2 = constants()
    tiled = np.ascontiguousarray(a["x"][0].T.reshape(DT, P, T).transpose(1, 0, 2).reshape(P, DT * T))
    return {
        "x": tiled, "w": w, "vec": np.ascontiguousarray(np.concatenate([v[n] for n in VEC], 1)),
        "con1": c1, "con2": c2,
        "lora": np.ascontiguousarray(np.stack([a["rwkv_w2"][0], a["rwkv_a2"][0]], 1).reshape(LORA, 2, WT, P)
                                     .transpose(2, 0, 1, 3).reshape(WT, LORA, 2 * P)),
        "rel": np.ascontiguousarray(np.concatenate([a["rel_bias_2"], np.zeros((BUCKETS, 4), f)], 1)),
        "ada": np.concatenate([a["w_ada_2"][0].reshape(DT, P, 12, 1024).transpose(2, 0, 1, 3).reshape(-1, P, 1024),
                               np.zeros((2, P, 1024), f)], 0),
    }


def kernel(**inputs):
    import concourse.bacc as bacc
    from concourse.bass_utils import run_bass_kernel_spmd

    nc = bacc.Bacc("TRN2", target_bir_lowering=False, num_devices=1)
    arrays = _layout({n: np.asarray(v) for n, v in inputs.items()})
    ins = {n: nc.dram_tensor(f"in_{n}", v.shape, F32, kind="ExternalInput").ap() for n, v in arrays.items()}
    out = nc.dram_tensor("out_x", (P, DT * T), F32, kind="ExternalOutput").ap()
    build(nc, ins, out)
    r = run_bass_kernel_spmd(nc, [{f"in_{n}": v for n, v in arrays.items()}], core_ids=[0])
    y = r.results[0]["out_x"]
    return np.ascontiguousarray(y.reshape(P, DT, T).transpose(1, 0, 2).reshape(D, T).T)[None]
```

```python
from contextlib import ExitStack

import numpy as np

import concourse.bass as bass
from concourse import mybir

F32 = mybir.dt.float32
F32R = mybir.dt.float32r
ALU = mybir.AluOpType
ACT = mybir.ActivationFunctionType
AX = mybir.AxisListType

P = 128
D = 2048
T = 256
DT = D // P
TT = T // P
FOX_HEADS = 8
FOX_SCALE = float(P) ** -0.5
W1 = D // 2
WT = W1 // P
LORA = 96
RWKV_HD = 64
CHUNK = 64
NCH = T // CHUNK
LEVELS = (2, 4, 8, 16, 32)
DECAY_SCALE = float(np.exp(-0.5))
FOX_COLS = 4 * W1 + FOX_HEADS
RWKV_COLS = 4 * W1 + 2 * LORA

MLA_HEADS = 16
QR, KVR, ROPE = 768, 512, 64
MLA_SCALE = float(192) ** -0.5
SWA_HEADS, SWA_KV, SWA_HD = 32, 4, 64
SWA_SCALE = float(SWA_HD) ** -0.5
NEG = -1e30
D_FF = 5632
FT = D_FF // P
BUCKETS = 32

BLK = 1024
RING = 4
AHEAD = RING - 1
NQ = 8


def _columns(sizes):
    out, at = {}, 0
    for name, n in sizes:
        out[name] = (at, n)
        at += n
    return out, at


VEC, NVEC = _columns([
    ("g1", 16), ("mu", 32), ("mu_w", 1), ("mu_a", 1), ("fbias", 1), ("w0", 8), ("a0", 8), ("k_k", 8), ("k_a", 8),
    ("r_k", 8), ("ln_w", 8), ("ln_b", 8), ("gf", 16), ("c", 16), ("b_ada", 96), ("g_pre_mix", 16),
    ("g_post_mix", 16), ("g_q", 6), ("g_kv", 4), ("sinks", 32), ("g_pre_ffn", 16), ("g_post_ffn", 16),
    ("conv_w", 264), ("conv_b", 88),
])
CON1, NCON1 = _columns([
    ("ident", 128), ("ones", 128), ("bones", 128), ("m_su", 128), ("m_ui", 128), ("m_u1", 128), ("m_low", 768),
    ("causal", 512), ("reset", 256), ("selcol", 8), ("bmask", 128),
])
CON2, NCON2 = _columns([
    ("ident", 128), ("ones", 128), ("causal", 512), ("rot", 128), ("cos", 256), ("sin", 256),
    ("onehot", 384),
])


def constants():
    f = np.float32
    i, j = np.arange(P)[:, None], np.arange(P)[None, :]
    same = (i // CHUNK) == (j // CHUNK)
    ident = np.eye(P, dtype=f)
    causal = np.full((P, 2, T), NEG, f)
    for b in range(2):
        causal[:, b, :][(np.arange(T)[None, :] <= b * P + np.arange(P)[:, None])] = 0
    low = []
    for m in (1,) + LEVELS:
        low.append(((i // (2 * m)) == (j // (2 * m))) & ((i // m) % 2 == 1) & ((j // m) % 2 == 0))
    u1 = low[0].T
    reset = np.broadcast_to((np.arange(T) % CHUNK != 0), (P, T))
    selcol = np.zeros((P, 8), f)
    for h in range(8):
        selcol[h, h] = selcol[32 + h, h] = 1
    one = {
        "ident": ident, "ones": np.ones((P, P)), "bones": (i // 64 == j // 64), "m_su": same & (i < j),
        "m_ui": same & (i <= j), "m_u1": u1, "m_low": np.concatenate(low, 1), "causal": causal.reshape(P, 512),
        "reset": reset, "selcol": selcol, "bmask": (i // 64 == j // 64),
    }
    c1 = np.concatenate([np.asarray(one[n], f) for n in CON1], 1)
    pos = np.arange(T, dtype=f)
    inv = f(10000.0) ** (-np.arange(0, ROPE, 2, dtype=f) / f(ROPE))
    ang = pos[None, :] * np.concatenate([inv, inv])[:, None]
    cos, sin = np.tile(np.cos(ang).astype(f), (2, 1)), np.tile(np.sin(ang).astype(f), (2, 1))
    rot = np.zeros((P, P), f)
    for g in range(2):
        for m in range(32):
            rot[64 * g + m + 32, 64 * g + m] = -1
            rot[64 * g + m, 64 * g + m + 32] = 1
    n = np.maximum(255 - np.arange(384), 0)
    exact = BUCKETS // 2
    large = exact + (np.log(np.maximum(n, 1).astype(f) / f(exact)) / f(np.log(P / exact))
                     * f(BUCKETS - exact)).astype(np.int32)
    bucket = np.where(n < exact, n, np.minimum(large, BUCKETS - 1))
    onehot = np.zeros((P, 384), f)
    onehot[bucket, np.arange(384)] = 1
    two = {"ident": ident, "ones": np.ones((P, P)), "causal": causal.reshape(P, 512), "rot": rot, "cos": cos,
           "sin": sin, "onehot": onehot}
    c2 = np.concatenate([np.asarray(two[n], f) for n in CON2], 1)
    return np.ascontiguousarray(c1), np.ascontiguousarray(c2)


STRETCH = (
    ("fox", 64), ("waf", 4), ("rwkv", 64), ("gates1", 64), ("proj1", 32), ("out1", 32),
    ("lat", 22), ("swa", 40), ("gates2", 64), ("uq", 18), ("ukv", 16), ("out2", 32), ("up", 176), ("down", 88),
)
B0, NBLK = {}, 0
for _name, _n in STRETCH:
    B0[_name] = NBLK
    NBLK += _n
Q0, _q = {}, 0
for _name, _n in (("fox", 8), ("waf", 1), ("rwkv", 8), ("gates1", 8), ("proj1", 8), ("out1", 4), ("lat", 4), ("swa", 5),
                  ("gates2", 8), ("uq", 6), ("ukv", 8), ("out2", 4), ("up", 22)):
    Q0[_name] = _q
    _q += _n

WORK = 20224


SHARED = {}
for _kind, _counts in {
    "sq": dict(n1=4, nf=4, n2=4, nq=2, nk=1, r1=4, n3=4, r2=4),
    "part": dict(n1=4, nf=4, n2=4, nq=1, nk=1, r1=4, n3=4, r2=4),
    **{k: dict(n1=1, nf=1, n2=1, nq=1, nk=1, r1=1, n3=1, r2=1) for k in ("sum", "ms", "inv", "rstd")},
    "xr": dict(n1=4, nf=4, n2=4, nq=1, nk=1, r1=4, n3=4, r2=4),
    "h": dict(n1=16, m1=16, nf=16, n2=16, nq=6, nk=4, m2=16, n3=16),
    **{k: dict(n1=4, oa=1, obo=1, m1=4, n2=4, nq=1, nk=1, m2=4, n3=4) for k in ("hi", "lo")},
    "qk": dict(fox=9, swa=16, mla=8),
    **{k: dict(fox=8, swa=16, mla=8) for k in ("pv", "t", "mx", "nm", "rs", "o")},
    "q": dict(fox=9, swa=32, mla=8), "v": dict(fox=8, swa=4), "e": dict(fox=16, swa=64, mla=32),
    "s": dict(fox=8, swa=32, mla=8), "pt": dict(fox=8, swa=32, mla=16), "p": dict(fox=16, swa=16, mla=8),
}.items():
    _at = 0
    for _step, _n in _counts.items():
        SHARED[f"{_step}_{_kind}"] = (("norm_" if "n1" in _counts else "attn_") + _kind, _at)
        _at += _n

for _first, _n, _later in (
    ("rw_kk0", 8, "swa_sb"), ("rw_ld", 8, "swa_m"), ("rw_lc", 8, "swa_d"), ("rw_lp", 8, "swa_tot"),
    ("rw_kkm", 8, "swa_zero"), ("rw_kkinv", 8, "swa_neg"), ("rw_kf", 8, "mla_zero"), ("rw_kh", 8, "rope_s"),
    ("rw_kk", 8, "rope_c"), ("rw_rk", 8, "rope"), ("rw_ba", 8, "gain"), ("rw_kt", 8, "ada_mod"), ("rw_bt", 8, "rev"),
    ("rw_rt", 8, "ffn_cv"), ("rw_s0", 8, "m2_g"), ("rw_v", 8, "swa_es"), ("rw_sg", 8, "swa_k"), ("rw_a", 8, "ffn_c"),
    ("rw_kk2", 8, "ffn_z"), ("rw_kkr", 8, "y_hi"), ("gn_mean", 4, "rot"), ("gn_var", 4, "rev_p"), ("f_x", 1, "gn_sq"),
    ("f_abs", 1, "gn_rstd"), ("f_exp", 1, "gn_z"), ("f_ln", 1, "down_out"), ("f_min", 1, "gn_yc"),
    ("f_log", 1, "gn_v"), ("f_sum", 1, "gn_inv"), ("aug_z", 3, "gn_y"), ("aug_1", 3, "gn_w"), ("omm", 1, "gn_b"),
    ("fox_aug", 9, "y_lo"), ("x_loaded", 16, "con2_in"), ("vec_loaded", 16, "rel_in"), ("con_loaded", 16, "gates2_in"),
):
    SHARED[_later] = (_first, _n)

PRIMED = {
    "rw_lora": "pe", "rw_y": "act", "ffn_y": "dve",
    "attn_qk": "pe", "attn_pv": "pe", "attn_e": "act", "attn_s": "dve", "attn_pt": "act", "attn_o": "dve",
}


def at(c, per=0, i=None):
    return c if i is None else c + i * per


def build(nc, ins, out):
    with ExitStack() as ctx:
        def sb(name, cols, dt=F32):
            return ctx.enter_context(nc.sbuf_tensor(name, [P, cols], dt))

        def pb(name):
            return ctx.enter_context(nc.psum_tensor(name, [P, 1024], F32))

        sems = {}

        def sem(name):
            name = SHARED.get(name, (name, 0))[0]
            if name not in sems:
                sems[name] = ctx.enter_context(nc.semaphore(name))
            return sems[name]

        raw = sb("w_raw", RING * BLK)
        whi = sb("w_hi", RING * BLK, F32R)
        wlo = sb("w_lo", RING * BLK, F32R)
        hhi = sb("h_hi", DT * T, F32R)
        hlo = sb("h_lo", DT * T, F32R)
        x = sb("x", DT * T)
        vec = sb("vec", NVEC)
        con = sb("con", max(NCON1, NCON2))
        work = sb("work", WORK)
        adaw = sb("ada_w", 2 * 1024)
        adap = sb("ada_p", 2 * 1024)
        small = sb("small", 896)
        G = [pb("gemm0"), pb("gemm1")]
        A = [pb("aux0"), pb("aux1")]
        bank = [A[0][:, 0:512], A[0][:, 512:1024], A[1][:, 0:512], A[1][:, 512:1024]]

        def V(name, k=None, n=1):
            a, w = VEC[name]
            return vec[:, a:a + w] if k is None else vec[:, a + k:a + k + n]

        def C1(name, rows=P):
            a, w = CON1[name]
            return con[0:rows, a:a + w]

        def C2(name, rows=P):
            a, w = CON2[name]
            return con[0:rows, a:a + w]

        x3 = x[:].rearrange("p (k t) -> p k t", t=T)
        hh = hhi[:].rearrange("p (k t) -> p k t", t=T)
        hl = hlo[:].rearrange("p (k t) -> p k t", t=T)

        def area(off, cols, t=T):
            return work[:, off:off + cols].rearrange("p (k t) -> p k t", t=t)

        def tiles(k, n=1):
            return work[:, k * T:(k + n) * T]

        def tile_at(k, i, n=1, per=1):
            if i is None:
                return tiles(k, n)
            return work[:, bass.ds(i * (per * T) + k * T, n * T)]

        fox = area(0, 24 * T)
        foxv = area(24 * T, 2 * W1, W1)
        waf = area(32 * T, 2 * T)
        RR, RK, RV, RZ = 34, 42, 50, 58
        sq = area(34 * T, DT * T)
        sc, scf = area(66 * T, 2 * T), tiles(66, 2)
        pr = area(68 * T, 2 * T)
        ptf = tiles(70, 2)
        aug_l, aug_r, aug_h = (work[0:40, (72 + n) * T:(73 + n) * T] for n in range(3))
        fq = tiles(75)
        fv = area(76 * T, T, P)
        nsum = area(27 * T, 4 * T)
        lsg = [work[0:8, (66 + n) * T:(67 + n) * T] for n in range(4)]
        low = tiles(8, 12).rearrange("p (l u t) -> p l u t", l=6, u=4)
        um, wm, gm, lak, rb, rk = (tiles(20 + 2 * n, 2) for n in range(6))
        at_, bt_, kt_, rt_ = (tiles(66 + n) for n in range(4))
        btok, ktok, vtok = (area((70 + n) * T, T, P) for n in range(3))
        xv, sa = area(73 * T, T, P), area(74 * T, T, P)
        xs, sbd = work[:, 75 * T:75 * T + P], work[:, 75 * T + P:76 * T]
        t1, t2 = tiles(77), tiles(78)
        e0, e1, e2, e5 = tiles(73), tiles(71), tiles(72), tiles(76)
        ep, en, bkt = tiles(74), tiles(70), tiles(70, 2)
        vf = x[:, 8 * T:9 * T]
        lw = x[0:LORA, 9 * T:10 * T]
        ah = x[:, 10 * T:12 * T].rearrange("p (h t) -> p h t", t=T)
        rh_ = x[:, 12 * T:14 * T].rearrange("p (h t) -> p h t", t=T)
        gates2 = nc.dram_tensor("gates2", (8, P, BLK), F32).ap()
        gates = nc.dram_tensor("gates", (8, P, BLK), F32).ap()
        lat = area(0, 11 * T)
        SQ, SK, SV = 11, 27, 55
        swv = area(SV * T, 2 * T)
        MQ, MR = 31, 47
        bias = [area((31 + 2 * n) * T, 2 * T) for n in range(2)]
        qz, vst = area(38 * T, 2 * T), area(40 * T, P, 64)
        revs = work[0:36, 73 * T:73 * T + 384]
        stage = [tiles(57 + 4 * n, 4) for n in range(2)]
        s4, p4 = area(65 * T, 4 * T), area(69 * T, 4 * T)
        spt = tiles(35, 3)
        kn, vv = ([area(k * T, 2 * T) for k in ks] for ks in ((55, 27), (57, 29)))
        qn, qr = (area((59 + 2 * n) * T, 2 * T) for n in range(2))
        ms4, mp4, mpt, krr = area(63 * T, 4 * T), area(67 * T, 4 * T), tiles(71, 3), tiles(74)
        rt1, rt2 = tiles(75), tiles(76)
        gbuf = adaw[:, :]
        msq = area(57 * T, 10 * T)
        rel = work[0:BUCKETS, 77 * T:77 * T + SWA_HEADS + 4]
        mod = adap[:, 0:96]
        gg1, gg2, gr1, gr2 = (adap[:, 96 + 16 * n:112 + 16 * n] for n in range(4))
        adasum = nc.dram_tensor("adasum", (12, P, 1024), F32).ap()
        revd = nc.dram_tensor("revd", (SWA_HEADS + 4, P * 384), F32).ap()
        yh, yl = hh[:, 0:4, :], hl[:, 0:4, :]
        stat = [small[:, n * T:(n + 1) * T] for n in range(3)]
        st = small[:, 3 * T:3 * T + 32]
        omm = small[:, 3 * T + 32:3 * T + 66]
        omka = small[:, 3 * T + 66:3 * T + 74]

        def load_block(eng, c, per=0, i=None):
            n = at(c, per, i)
            if c >= RING:
                eng.wait_ge(sem("lo_ready"), n - AHEAD)
            s = c % RING
            eng.dma_start(raw[:, s * BLK:(s + 1) * BLK],
                          ins["w"][bass.ds(n, 1), :, :].rearrange("a p n -> p (a n)")).then_inc(sem(f"raw{s}"), 16)

        def waiter(eng):
            def hold(name, v):
                name, before = SHARED.get(name, (name, 0))
                eng.wait_ge(sem(name), v + before + (name in PRIMED))
            return hold

        def prime(eng, who):
            if who == "act":
                for n in range(2):
                    eng.sem_inc(sem(f"gate_out{n}"), 16)
                    eng.sem_inc(sem(f"gate2_out{n}"), 16)

            for name, by in PRIMED.items():
                if by == who:
                    eng.sem_inc(sem(name), 1)

        def split_hi(eng, c, per=0, i=None):
            if c >= NBLK:
                return
            s = c % RING
            eng.wait_ge(sem(f"raw{s}"), at(16 * (c // RING + 1), 4 * per, i))
            if c >= RING:
                eng.wait_ge(sem("block_used"), at(c - AHEAD, per, i))
            eng.activation(whi[:, s * BLK:(s + 1) * BLK], raw[:, s * BLK:(s + 1) * BLK],
                           ACT.Copy).then_inc(sem("hi_ready"), 1)

        def split_lo(eng, c, per=0, i=None):
            if c >= NBLK:
                return
            s = c % RING
            eng.wait_ge(sem("hi_ready"), at(c + 1, per, i))
            eng.tensor_tensor(wlo[:, s * BLK:(s + 1) * BLK], raw[:, s * BLK:(s + 1) * BLK],
                              whi[:, s * BLK:(s + 1) * BLK].bitcast(F32), ALU.subtract).then_inc(sem("lo_ready"), 1)

        def block(eng, c, per, i, cols, rh, rl, k0, set_, first, last, token=False, parts=None,
                  piece=(0, 4)):
            s = c % RING
            ks = BLK // cols
            if piece[0] == 0:
                eng.wait_ge(sem("lo_ready"), at(c + 1, per, i))
            wh = whi[:, s * BLK:(s + 1) * BLK].rearrange("p (k n) -> p k n", n=cols)
            wl = wlo[:, s * BLK:(s + 1) * BLK].rearrange("p (k n) -> p k n", n=cols)
            if parts is None:
                parts = [(True, slice(0, cols), 0)] if token else [(False, t, t * T) for t in range(cols // P)]
            g = G[set_] if isinstance(set_, int) else set_
            for tok, what, col in parts[piece[0]:piece[1]]:
                for t in range(TT if tok else 1):
                    for k in range(ks):
                        for a, (w_, r_) in enumerate(((wh, rh), (wh, rl), (wl, rh))):
                            if tok:
                                r = w_[:, k, :].rearrange("p (h e n) -> p h e n", e=2, n=P)[:, :, 1, :] \
                                    if what == "v" else w_[:, k, what]
                                n = TT * P if what == "v" else what.stop - what.start
                                o = g[:, col + t * n:col + (t + 1) * n]
                                if what == "v":
                                    o = o.rearrange("p (h n) -> p h n", n=P)
                                l, st_ = r_[:, k0 + k, t * P:(t + 1) * P], (col + t * n) % 512 == 0
                            else:
                                o = g[:, col:col + T]
                                l, r, st_ = w_[:, k, what * P:(what + 1) * P], r_[:, k0 + k, :], col % 512 == 0
                            mm = eng.matmul(o, l, r, start=first and k == 0 and a == 0 and st_,
                                            stop=last and k == ks - 1 and a == 2, skip_group_check=True)
            if piece[1] == 4:
                mm.then_inc(sem("block_used"), 1)

        def quad_pe(eng, c, per, i, q, qper, set_, cols=512, nb=NQ, rh=hh, rl=hl, token=False, operand=None):
            if q >= 2:
                eng.wait_ge(sem("quad_read"), at(q - 1, qper, i))
            for b in range(nb):
                if operand and b % 2 == 0:
                    name, before = SHARED[operand + "_lo"]
                    eng.wait_ge(sem(name), before + b // 2 + 1)
                block(eng, c + b, per, i, cols, rh, rl, b * (BLK // cols), set_, b == 0, b == nb - 1, token)

        def quad_done(eng, c_end, per=0, i=None):
            eng.wait_ge(sem("block_used"), at(c_end, per, i))

        blk = ctx.enter_context(nc.Block())

        @blk.sync
        def _(sp):
            hold = waiter(sp)
            sp.dma_start(x[:], ins["x"]).then_inc(sem("x_loaded"), 16)
            sp.dma_start(vec[:], ins["vec"]).then_inc(sem("vec_loaded"), 16)
            sp.dma_start(con[:, 0:NCON1], ins["con1"]).then_inc(sem("con_loaded"), 16)
            for c in range(RING):
                load_block(sp, c)
            turns = NBLK // RING - 1
            with sp.Fori(0, turns) as i:
                for c in range(RING, 2 * RING):
                    load_block(sp, c, RING, i)
            for c in range((turns + 1) * RING, NBLK):
                load_block(sp, c)
            for k in range(0, DT, 4):
                hold("r2_x", k + 4)
                sp.dma_start(out[:, k * T:(k + 4) * T], x[:, k * T:(k + 4) * T]).then_inc(sem("stored"), 16)
            sp.wait_ge(sem("stored"), 64)

        @blk.gpsimd
        def _(pool):
            prime(pool, "pool")
            hold = waiter(pool)
            prod, acc = adap[:, 0:1024], adap[:, 1024:2048]

            def load(n, s):
                pool.dma_start(adaw[:, s * 1024:(s + 1) * 1024],
                               ins["ada"][bass.ds(n, 1), :, :].rearrange("a p n -> p (a n)"))\
                    .then_inc(sem(f"ada_in{s}"), 16)

            load(0, 0)
            load(1, 1)
            hold("c_silu", 1)
            with pool.Fori(0, 12) as g:
                for k in range(DT):
                    w = adaw[:, (k % 2) * 1024:(k % 2 + 1) * 1024]
                    pool.wait_ge(sem(f"ada_in{k % 2}"), g * 128 + 16 * (k // 2 + 1))
                    if k >= 2:
                        hold("ada_acc", g * 15 + k - 1)
                    pool.sem_inc(sem("ada_turn"), 1)
                    pool.tensor_scalar(prod if k else acc, w, V("c", k), 0.0, ALU.mult, ALU.add)\
                        .then_inc(sem("ada_prod"), 1)
                    hold("ada_prod", g * 16 + k + 1)
                    load(g * 16 + k + 2, k % 2)
                    if k:
                        pool.tensor_tensor(acc, acc, prod, ALU.add).then_inc(sem("ada_acc"), 1)
                hold("ada_acc", g * 15 + 15)
                pool.dma_start(adasum[bass.ds(g, 1), :, :].rearrange("a p n -> p (a n)"), acc)\
                    .then_inc(sem("ada_st"), 16)
                pool.wait_ge(sem("ada_st"), g * 16 + 16)
            for n in range(2):
                pool.wait_ge(sem(f"ada_in{n}"), 12 * 128 + 16)
            for g in range(12):
                if g >= 4:
                    hold("ada_sum", g - 3)
                s = g % 4
                dst = (adaw if s < 2 else adap)[:, (s % 2) * 1024:(s % 2 + 1) * 1024]
                pool.dma_start(dst, adasum[g]).then_inc(sem(f"ada_back{s}"), 16)

        @blk.scalar
        def _(act):
            hold = waiter(act)
            prime(act, "act")

            def norm_squares(tag, src, tiles=DT, sq=sq, after=None):
                for c in range(0, tiles, 4):
                    if after:
                        hold(after, c + 4)
                    n = min(4, tiles - c)
                    act.activation(sq[:, c:c + n, :], src[:, c:c + n, :], ACT.Square).then_inc(sem(tag + "_sq"), 1)

            def norm_root(tag):
                hold(tag + "_inv", 1)
                act.activation(stat[2], stat[1], ACT.Sqrt).then_inc(sem(tag + "_rstd"), 1)

            def operand_hi(tag, src, dst, tiles=DT, step=4):
                for c in range(0, tiles, step):
                    n = min(step, tiles - c)
                    if tag not in ("oa", "obo"):
                        hold(tag + "_h", min(c + n, tiles))
                    act.activation(dst[:, c:c + n, :], src[:, c:c + n, :], ACT.Copy).then_inc(sem(tag + "_hi"), 1)

            def norm_operand_hi(tag, gain, shift):
                for c in range(5):
                    if c < 4:
                        hold(tag + "_xr", c + 1)
                        for k in range(4 * c, 4 * c + 4):
                            act.activation(sq[:, k, :], sq[:, k, :], ACT.Identity, scale=gain[:, k:k + 1],
                                           bias=0.0 if shift is None else shift[:, k:k + 1]).then_inc(sem(tag + "_h"), 1)
                    if c:
                        hold(tag + "_h", 4 * c)
                        act.activation(hh[:, 4 * c - 4:4 * c, :], sq[:, 4 * c - 4:4 * c, :], ACT.Copy)\
                            .then_inc(sem(tag + "_hi"), 1)

            def rwkv_act():
                act.activation(waf[0:LORA, 0, :], waf[0:LORA, 0, :], ACT.Tanh).then_inc(sem("tanh_w"), 1)
                c = B0["gates1"]

                def lora_in(n):
                    act.dma_start(lw, ins["lora"][bass.ds(n, 1), :, :].rearrange("a p n -> p (a n)"))\
                        .then_inc(sem("lora_in"), 16)

                lora_in(0)
                with act.Fori(0, WT // 2) as i:
                    for s in range(2):
                        n, g, b0 = 2 * i + s, G[(Q0["gates1"] + s) % 2], c + 8 * s

                        def split(b):
                            split_hi(act, b0 + b + AHEAD, 16, i)

                        def copy(out_, in_, name, f=ACT.Copy, **kw):
                            return act.activation(out_, in_, f, **kw).then_inc(sem(name), 1)

                        copy(vf, tile_at(RV + s, i, 1, 2), "rw_v")
                        hold("rw_kk0", n + 1)
                        copy(e2, e1, "rw_kk2", ACT.Square)
                        hold("rw_lora", n + 1)
                        copy(t1, bank[0][:, 0:T], "rw_sg", ACT.Sigmoid, bias=vec[:, bass.ds(n + VEC["w0"][0], 1)])
                        copy(t2, bank[0][:, T:2 * T], "rw_a", ACT.Sigmoid, bias=vec[:, bass.ds(n + VEC["a0"][0], 1)])
                        hold("rw_kkinv", n + 1)
                        copy(e2, e2, "rw_kkr", ACT.Sqrt)
                        hold("rw_lc", n + 1)
                        copy(ep, e0, "rw_p", ACT.Exp)
                        copy(en, e0, "rw_n", ACT.Exp, scale=-1.0)
                        hold("rw_lp", n + 1)
                        copy(e5, e5, "rw_pp", ACT.Exp)
                        lora_in(at(1 + s, 2, i))
                        split(0)
                        split(1)
                        hold("rw_rt", n + 1)
                        for h in range(2):
                            copy(rh_[64 * h:64 * h + 64, h, :], rt_[64 * h:64 * h + 64, :], "rw_rh")
                        hold("rw_tr", n + 1)
                        copy(bkt, bank[2][:, 0:4 * P], "rw_tok")
                        hold("rw_trv", n + 1)
                        copy(vtok.rearrange("p t n -> p (t n)"), bank[3][:, 0:2 * P], "rw_vtok")
                        split(2)
                        for lv in range(1, 6):
                            hold("rw_g", 5 * n + lv)
                            copy(gm, bank[1], "rw_gc")
                            if lv != 4:
                                split(2 + lv if lv < 5 else 6)
                        hold("rw_xv", n + 1)
                        copy(xv.rearrange("p t n -> p (t n)"), bank[0][:, 0:T], "rw_xvc")
                        for ch in range(NCH):
                            r = slice((ch % 2) * 64, (ch % 2) * 64 + 64)
                            hold("rw_sa", 4 * n + ch + 1)
                            copy(sa[r, ch // 2, :], bank[2][r, 0:P], "rw_sac")
                        quad_done(act, b0 + 8, 16, i)
                        act.wait_ge(sem(f"gate_out{s}"), 16 * i + 16)
                        copy(x[:, s * 1024:(s + 1) * 1024], g[:], "quad_read", ACT.Sigmoid)
                        act.wait_ge(sem("quad_read"), at(Q0["gates1"] + s + 1, 2, i))
                        act.dma_start(gates[bass.ds(n, 1), :, :].rearrange("a p n -> p (a n)"),
                                      x[:, s * 1024:(s + 1) * 1024]).then_inc(sem(f"gate_out{s}"), 16)
                        hold("rw_yp", n + 1)
                        copy(tile_at(RR + s, i, 1, 2), bank[0][:, 0:T], "rw_y")
                        split(7)
                act.wait_ge(sem("lora_in"), 16 * WT + 16)
                operand_hi("oa", area(0, 8 * T), hh[:, 0:8, :], 8, 8)
                for q in range(4):
                    hold("gn_yc", q + 1)
                    copy(tiles(16 + 2 * q, 2), tiles(8 + 2 * q, 2), "gn_sq", ACT.Square)
                hold("gn_inv", 4)
                copy(tiles(16, 8), tiles(16, 8), "gn_rstd", ACT.Sqrt)
                copy(tiles(RZ, 8), tiles(RZ, 8), "gn_z", ACT.Silu)

            def mix1_act():
                hold("gn_o", 1)
                operand_hi("obo", area(RR * T, 8 * T), hh[:, 8:16, :], 8, 8)
                for n in range(2):
                    act.wait_ge(sem(f"gate_out{n}"), 80)
                for k, a in ((8, 0), (50, 4)):
                    act.dma_start(area(k * T, 16 * T, BLK), gates[a:a + 4, :, :].rearrange("q p n -> p q n"))\
                        .then_inc(sem("gates_in"), 16)
                act.dma_start(x[:], ins["x"]).then_inc(sem("x_again"), 16)
                with act.Fori(0, 4) as i:
                    for b in range(8):
                        split_hi(act, B0["proj1"] + b + AHEAD, 8, i)
                operand_hi("m1", area(8 * T, 16 * T), hh)
                with act.Fori(0, 2) as i:
                    for b in range(16):
                        split_hi(act, B0["out1"] + b + AHEAD, 16, i)

            def layer2_act():
                act.wait_ge(sem("quad_read"), Q0["out1"] + 4)
                norm_squares("nf", x3)
                hold("nf_part", 4)
                norm_root("nf")
                norm_squares("n2", x3, after="nf_h")
                norm_root("n2")
                hold("ada_mod", 1)
                act.dma_start(con[:, 0:NCON2], ins["con2"]).then_inc(sem("con2_in"), 16)
                act.dma_start(rel, ins["rel"]).then_inc(sem("rel_in"), 16)
                hold("gain", 6)
                norm_operand_hi("n2", gg1, mod[:, 0:16])
                hold("rev", 3)
                act.dma_start(revd.rearrange("h (a m) -> h a m", m=384),
                              revs.unsqueeze(1).to_broadcast([SWA_HEADS + 4, P, 384])).then_inc(sem("rev_out"), 16)
                c = B0["lat"]
                at_tile = 0
                for q, (cols, nb) in enumerate(((512, 8), (512, 8), (256, 4), (P, 2))):
                    for b in range(nb):
                        split_hi(act, c + b + AHEAD)
                    c += nb
                    quad_done(act, c)
                    n = cols // P
                    act.activation(tiles(at_tile, n), G[(Q0["lat"] + q) % 2][:, 0:n * T], ACT.Copy)\
                        .then_inc(sem("quad_read"), 1)
                    at_tile += n
                with act.Fori(0, 2) as i:
                    for s in range(2):
                        for b in range(8):
                            split_hi(act, B0["swa"] + 8 * s + b + AHEAD, 16, i)
                        quad_done(act, B0["swa"] + 8 * s + 8, 16, i)
                        act.activation(tile_at(SQ + 4 * s, i, 4, 8), G[(Q0["swa"] + s) % 2][:], ACT.Copy)\
                            .then_inc(sem("quad_read"), 1)
                for b in range(8):
                    split_hi(act, B0["swa"] + 32 + b + AHEAD)
                quad_done(act, B0["swa"] + 40)
                g = G[(Q0["swa"] + 4) % 2]
                for kv in range(SWA_KV):
                    for o in range(2):
                        r = 64 * (kv % 2)
                        act.activation(work[64 * o:64 * o + 64, (SK + kv) * T:(SK + kv + 1) * T],
                                       g[r:r + 64, (kv // 2) * T:(kv // 2 + 1) * T], ACT.Copy).then_inc(sem("swa_k"), 1)
                act.activation(tiles(SV, 2), g[:, 512:1024], ACT.Copy).then_inc(sem("quad_read"), 1)
                swa_act()
                mla_act()
                mix2_act()
                ffn_act()

            def swa_act():
                def bias_in(n, s):
                    act.dma_start(bias[s], revd[bass.ds(2 * n, 2), 127:127 + P * 383]
                                  .rearrange("h (a m) -> a h m", m=383)[:, :, 0:T]).then_inc(sem(f"bias_in{s}"), 16)

                hold("swa_zero", 4)
                act.wait_ge(sem("quad_read"), Q0["gates2"])
                act.wait_ge(sem("rev_out"), 16)
                bias_in(0, 0)
                c = B0["gates2"]
                with act.Fori(0, 4) as i:
                    for p in range(4):
                        n, b0 = 4 * i + p, c + 4 * p

                        def split(b):
                            split_hi(act, b0 + b + AHEAD, 16, i)

                        def query(p):
                            for h in range(2):
                                r = slice(64 * h, 64 * h + 64)
                                act.activation(qz[r, h, :], work[r, bass.ds(i * 4 * T + (SQ + p) * T, T)], ACT.Copy)\
                                    .then_inc(sem("swa_q"), 1)

                        hold("swa_s", 2 * n)
                        bias_in(n + 1, (p + 1) % 2)
                        if p == 0:
                            hold("swa_qk", n)
                            query(0)
                            hold("swa_pv", n)
                            act.activation(vst, swv[:, :, bass.ds(i * 64, 64)], ACT.Copy).then_inc(sem("swa_v"), 1)
                        split(0)
                        split(1)
                        hold("swa_d", n + 1)
                        act.activation(st[:, 28:32], st[:, 12:16], ACT.Exp).then_inc(sem("swa_es"), 1)
                        for m in range(4):
                            k0 = 0 if m % 2 else P
                            act.activation(p4[:, m, k0:T], s4[:, m, k0:T], ACT.Exp, bias=st[:, 8 + m:9 + m],
                                           accum_out=st[:, 16 + m:17 + m]).then_inc(sem("swa_e"), 1)
                        if p < 3:
                            hold("swa_qk", n + 1)
                            query(p + 1)
                        split(2)
                        split(3)
                        hold("swa_t", n + 1)
                        for h in range(2):
                            act.activation(spt[:, 384 * h:384 * h + 384], bank[2 + h][:, 0:384], ACT.Copy)\
                                .then_inc(sem("swa_pt"), 1)
                        if p % 2:
                            s = p // 2
                            quad_done(act, c + 8 * s + 8, 16, i)
                            act.wait_ge(sem(f"gate2_out{s}"), 16 * i + 16)
                            act.activation(stage[s], G[(Q0["gates2"] + s) % 2][:], ACT.Sigmoid)\
                                .then_inc(sem("quad_read"), 1)
                            act.wait_ge(sem("quad_read"), at(Q0["gates2"] + s + 1, 2, i))
                            act.dma_start(gates2[bass.ds(2 * i + s, 1), :, :].rearrange("a p n -> p (a n)"), stage[s])\
                                .then_inc(sem(f"gate2_out{s}"), 16)
                act.wait_ge(sem("bias_in0"), 16 * 9)
                act.wait_ge(sem("bias_in1"), 16 * 8)

            def gates_back(a, dst):
                act.dma_start(dst.rearrange("p (q n) -> p q n", n=BLK),
                              gates2[a:a + 2, :, :].rearrange("q p n -> p q n")).then_inc(sem("gates2_in"), 16)

            def mla_act():
                for n in range(2):
                    act.wait_ge(sem(f"gate2_out{n}"), 80)
                hold("swa_o", 16)
                gates_back(4, gbuf)
                norm_squares("nq", lat, 6, msq)
                norm_squares("nk", lat[:, 6:10, :], 4, msq[:, 6:10, :])
                norm_root("nq")
                operand_hi("nq", msq, hh, 6, 6)
                norm_root("nk")
                operand_hi("nk", msq[:, 6:10, :], hh[:, 6:10, :], 4, 4)
                for q in range(6):
                    for b in range(3):
                        split_hi(act, B0["uq"] + 3 * q + b + AHEAD)
                    quad_done(act, B0["uq"] + 3 * q + 3)
                    act.activation(tiles(MQ + 4 * q, 4), G[(Q0["uq"] + q) % 2][:], ACT.Copy, scale=MLA_SCALE)\
                        .then_inc(sem("quad_read"), 1)
                    if q in (2, 5):
                        hold("m2_g", 1 + q // 3)
                        gates_back(6 if q == 2 else 0, gbuf)
                def operands(n0, i=None):
                    if n0:
                        hold("mla_qk", at(n0, 2, i))
                    act.activation(qn.rearrange("p a t -> p (a t)"), tile_at(MQ + 2 * n0, i, 2, 4), ACT.Copy)\
                        .then_inc(sem("mla_q"), 1)
                    for h in range(2):
                        r = slice(64 * h, 64 * h + 64)
                        src = tile_at(MR + n0, i, 1, 2)
                        act.activation(qr[r, h, :], src[r, :], ACT.Copy).then_inc(sem("mla_qr"), 1)
                    quad_done(act, B0["ukv"] + 2 * n0 + 2, 4, i)
                    g = G[(Q0["ukv"] + n0) % 2]
                    act.activation(kn[n0 % 2].rearrange("p a t -> p (a t)"), g[:, 0:512], ACT.Copy)\
                        .then_inc(sem("mla_k"), 1)
                    if n0 >= 2 or i is not None:
                        hold("mla_pv", at(n0 - 1, 2, i))
                    act.activation(vv[n0 % 2].rearrange("p a t -> p (a t)"), g[:, 512:1024], ACT.Copy)\
                        .then_inc(sem("quad_read"), 1)

                def turn(n0, i=None, last=False):
                    hold("mla_nm", at(n0 + 1, 2, i))
                    for m in range(4):
                        act.activation(mp4[:, m, :], ms4[:, m, :], ACT.Exp, bias=st[:, 8 + m:9 + m],
                                       accum_out=st[:, 16 + m:17 + m]).then_inc(sem("mla_e"), 1)
                    if not last:
                        for b in range(2):
                            split_hi(act, B0["ukv"] + 2 * n0 + 2 + b + AHEAD, 4, i)
                        operands(n0 + 1, i)
                    hold("mla_t", at(n0 + 1, 2, i))
                    for h in range(2):
                        act.activation(mpt[:, 384 * h:384 * h + 384], bank[2 + h][:, 0:384], ACT.Copy)\
                            .then_inc(sem("mla_pt"), 1)

                for b in range(2):
                    split_hi(act, B0["ukv"] + b + AHEAD)
                operands(0)
                turn(0)
                with act.Fori(0, 3) as i:
                    for s in range(2):
                        turn(1 + s, i)
                turn(7, last=True)

            def mix2_act():
                hold("mla_o", 8)
                hold("mla_t", 8)
                hold("gates2_in", 48)
                gates_back(2, tiles(63, 8))
                operand_hi("m2", area(MQ * T, 16 * T), hh)
                with act.Fori(0, 2) as i:
                    for s in range(2):
                        for b in range(8):
                            split_hi(act, B0["out2"] + 8 * s + b + AHEAD, 16, i)
                        quad_done(act, B0["out2"] + 8 * s + 8, 16, i)
                        act.activation(tile_at(4 * s, i, 4, 8), G[(Q0["out2"] + s) % 2][:], ACT.Copy)\
                            .then_inc(sem("quad_read"), 1)
                act.wait_ge(sem("quad_read"), Q0["out2"] + 4)
                norm_squares("r1", area(0, 16 * T))
                norm_root("r1")

            def ffn_act():
                norm_squares("n3", x3, after="r1_x")
                norm_root("n3")
                norm_operand_hi("n3", gg2, mod[:, 48:64])
                c = B0["up"]
                with act.Fori(0, 11) as i:
                    for s in range(2):
                        for b in range(8):
                            split_hi(act, c + 8 * s + b + AHEAD, 16, i)
                        quad_done(act, c + 8 * s + 8, 16, i)
                        if s == 0:
                            hold("ffn_y", i)
                        g = G[(Q0["up"] + s) % 2]
                        for k in range(4):
                            col = i * 4 + 44 * s + k
                            act.activation(tiles(44 + 4 * s + k), g[:, k * T:(k + 1) * T], ACT.Identity,
                                           scale=vec[:, bass.ds(col + VEC["conv_w"][0] + 176, 1)],
                                           bias=vec[:, bass.ds(col + VEC["conv_b"][0], 1)]).then_inc(sem("ffn_c"), 1)
                        if s == 0:
                            act.wait_ge(sem("quad_read"), at(Q0["up"] + 1, 2, i))
                            hold("ffn_cv", 14 * i + 7)
                            act.activation(tiles(44, 4), tiles(44, 4), ACT.Silu).then_inc(sem("ffn_z"), 1)
                hold("ffn_y", 11)
                c = B0["down"]

                def y_hi(k, i=None):
                    if k >= 2:
                        act.wait_ge(sem("block_used"), at(c + 4 * (k - 1), 8, i))
                    act.activation(yh[:, 2 * (k % 2):2 * (k % 2) + 2, :].rearrange("p k t -> p (k t)"),
                                   tiles(2 * k, 2) if i is None else tile_at(2 * k, i, 2, 4), ACT.Copy)\
                        .then_inc(sem("y_hi"), 1)

                def turn(k0, i=None, last=False):
                    for k in (k0, k0 + 1):
                        if not (last and k == k0 + 1):
                            y_hi(k + 1, i)
                        for b in range(4):
                            split_hi(act, c + 4 * k + b + AHEAD, 8, i)

                act.wait_ge(sem("block_used"), c)
                y_hi(0)
                turn(0)
                with act.Fori(0, 9) as i:
                    turn(2, i)
                turn(20, last=True)
                act.wait_ge(sem("block_used"), c + 88)
                for c, g in enumerate((A[0], G[0], G[1], A[1])):
                    act.activation(tiles(4 * c, 4), g[:], ACT.Square).then_inc(sem("r2_sq"), 1)
                    if c == 0:
                        act.activation(tiles(52, 4), g[:], ACT.Copy).then_inc(sem("down_out"), 1)
                norm_root("r2")

            hold("vec_loaded", 16)
            act.activation(V("c"), V("c"), ACT.Silu).then_inc(sem("c_silu"), 1)
            hold("x_loaded", 16)
            norm_squares("n1", x3)
            for c in range(AHEAD):
                split_hi(act, c)
            norm_root("n1")
            norm_operand_hi("n1", V("g1"), None)
            c = B0["fox"]
            for b in range(16):
                split_hi(act, c + b + AHEAD)
                if b % 8 == 7:
                    quad_done(act, c + b + 1)
                    act.activation(foxv[:, :, (b // 8) * 512:(b // 8 + 1) * 512],
                                   G[b // 8][:].rearrange("p (t n) -> p t n", t=TT), ACT.Copy)\
                        .then_inc(sem("quad_read"), 1)
            c += 16
            with act.Fori(0, 3) as i:
                for b in range(16):
                    split_hi(act, c + b + AHEAD, 16, i)
                    if b % 8 == 7:
                        quad_done(act, c + b + 1, 16, i)
                        act.activation(work[:, bass.ds(i * 2048 + (b // 8) * 1024, 1024)], G[b // 8][:],
                                       ACT.Copy).then_inc(sem("quad_read"), 1)
            c = B0["waf"]
            for b in range(4):
                split_hi(act, c + b + AHEAD)
            quad_done(act, c + 4)
            hold("omm", 1)
            for k in range(2):
                act.activation(waf[:, k, :], G[0][:, k * T:(k + 1) * T], ACT.Copy,
                               scale=omm[:, 32 + k:33 + k]).then_inc(sem("waf_own"), 1)
            act.activation(lsg[0], G[0][96:104, 0:T], ACT.Identity, bias=V("fbias")[0:8, :]).then_inc(sem("f_x"), 1)
            hold("f_x", 1)
            act.activation(lsg[1], lsg[0], ACT.Abs).then_inc(sem("f_abs"), 1)
            hold("f_abs", 1)
            act.activation(lsg[1], lsg[1], ACT.Exp, scale=-1.0).then_inc(sem("f_exp"), 1)
            hold("f_exp", 1)
            act.activation(lsg[1], lsg[1], ACT.Ln, bias=1.0).then_inc(sem("f_ln"), 1)
            act.activation(fox[:, 16:24, :], fox[:, 16:24, :], ACT.Silu).then_inc(sem("fox_z"), 1)
            c = B0["rwkv"]
            act.activation(fq, tiles(0), ACT.Copy, scale=FOX_SCALE).then_inc(sem("fox_q"), 1)
            with act.Fori(0, FOX_HEADS // 2) as i:
                for s in range(2):
                    g, b0 = G[(Q0["rwkv"] + s) % 2], c + 8 * s
                    hold("fox_pv", 2 * i + s)
                    act.activation(fv, foxv[:, :, bass.ds(i * 2 * P + s * P, P)], ACT.Copy).then_inc(sem("fox_v"), 1)
                    for b in (0, 1):
                        split_hi(act, b0 + b + AHEAD, 16, i)
                    hold("fox_nm", 2 * i + s + 1)
                    for b in range(TT):
                        act.activation(pr[:, b, :], sc[:, b, :], ACT.Exp, bias=st[:, 2 + b:3 + b],
                                       accum_out=st[:, 4 + b:5 + b]).then_inc(sem("fox_e"), 1)
                    hold("fox_qk", 2 * i + s + 1)
                    act.activation(fq, tile_at(s + 1, i, 1, 2), ACT.Copy, scale=FOX_SCALE).then_inc(sem("fox_q"), 1)
                    for b in (2, 3, 4):
                        split_hi(act, b0 + b + AHEAD, 16, i)
                    hold("fox_t", 2 * i + s + 1)
                    act.activation(ptf[:, 0:384], bank[1][:, 0:384], ACT.Copy).then_inc(sem("fox_pt"), 1)
                    for b in (5, 6, 7):
                        split_hi(act, b0 + b + AHEAD, 16, i)
                    quad_done(act, b0 + 8, 16, i)
                    for k in range(4):
                        act.activation(tile_at(RR + 4 * s + k, i, 1, 8), g[:, k * T:(k + 1) * T], ACT.Copy,
                                       scale=small[:, bass.ds(i * 8 + 3 * T + 32 + 4 * s + k, 1)])\
                            .then_inc(sem("rw_own"), 1)
            rwkv_act()
            mix1_act()
            layer2_act()

        @blk.vector
        def _(dve):
            hold = waiter(dve)
            prime(dve, "dve")

            def norm_stats(tag, n, tiles=DT, sq=sq):
                if tiles == DT:
                    for c in range(4):
                        hold(tag + "_sq", c + 1)
                        dve.tensor_reduce(nsum[:, c, :], sq[:, 4 * c:4 * c + 4, :].rearrange("p k t -> p t k"), AX.X,
                                          ALU.add).then_inc(sem(tag + "_part"), 1)
                else:
                    hold(tag + "_sq", (tiles + 3) // 4)
                    dve.tensor_reduce(stat[0], sq[:, 0:tiles, :].rearrange("p k t -> p t k"), AX.X,
                                      ALU.add).then_inc(sem(tag + "_part"), 1)
                hold(tag + "_sum", 1)
                dve.tensor_scalar(stat[0], bank[0][:, 0:T], 1.0 / n, 1e-6, ALU.mult, ALU.add)\
                    .then_inc(sem(tag + "_ms"), 1)
                hold(tag + "_ms", 1)
                dve.reciprocal(stat[1], stat[0]).then_inc(sem(tag + "_inv"), 1)

            def norm_operand_lo(tag, src):
                hold(tag + "_rstd", 1)
                for c in range(6):
                    if c < 4:
                        dve.tensor_tensor(sq[:, 4 * c:4 * c + 4, :], src[:, 4 * c:4 * c + 4, :],
                                          stat[2].unsqueeze(1).to_broadcast([P, 4, T]), ALU.mult)\
                            .then_inc(sem(tag + "_xr"), 1)
                    if c >= 2:
                        k = slice(4 * c - 8, 4 * c - 4)
                        hold(tag + "_hi", c - 1)
                        dve.tensor_tensor(hl[:, k, :], sq[:, k, :], hh[:, k, :].bitcast(F32), ALU.subtract)\
                            .then_inc(sem(tag + "_lo"), 1)

            def norm_apply(tag, src, gain, shift, tiles=DT, step=4, sq=sq, out=None):
                hold(tag + "_rstd", 1)
                for c in range(0, tiles, step):
                    n = min(step, tiles - c)
                    dve.tensor_tensor(sq[:, c:c + n, :], src[:, c:c + n, :],
                                      stat[2].unsqueeze(1).to_broadcast([P, n, T]), ALU.mult)\
                        .then_inc(sem(tag + "_xr"), 1)
                    hold(tag + "_xr", c // step + 1)
                    for k in range(c, c + n):
                        dve.tensor_scalar((sq if out is None else out)[:, k, :], sq[:, k, :], gain[:, k:k + 1],
                                          0.0 if shift is None else shift[:, k:k + 1], ALU.mult, ALU.add)\
                            .then_inc(sem(tag + "_h"), 1)

            def operand_lo(tag, src, hi, dst, tiles=DT, step=4):
                for c in range(0, tiles, step):
                    n = min(step, tiles - c)
                    hold(tag + "_hi", c // step + 1)
                    dve.tensor_tensor(dst[:, c:c + n, :], src[:, c:c + n, :], hi[:, c:c + n, :].bitcast(F32),
                                      ALU.subtract).then_inc(sem(tag + "_lo"), 1)

            def rwkv_dve():
                c = B0["gates1"]
                dve.tensor_scalar(omka, V("k_a"), -1.0, 1.0, ALU.mult, ALU.add).then_inc(sem("rw_omka"), 1)
                hold("rw_omka", 1)
                for o in (ah, rh_):
                    for h in range(2):
                        dve.memset(o[64 - 64 * h:128 - 64 * h, h, :], 0.0).then_inc(sem("rw_zero"), 1)
                with dve.Fori(0, WT // 2) as i:
                    for s in range(2):
                        n, b0 = 2 * i + s, c + 8 * s
                        R, K = tile_at(RR + s, i, 1, 2), tile_at(RK + s, i, 1, 2)

                        def col(name):
                            return vec[:, bass.ds(n + VEC[name][0], 1)]

                        def split(b):
                            split_lo(dve, b0 + b + AHEAD, 16, i)

                        def mul(o, a, b, name, op=ALU.mult):
                            dve.tensor_tensor(o, a, b, op).then_inc(sem(name), 1)

                        def mask(o, b, m, name, units=4):
                            dve.tensor_tensor(o.rearrange("p (u t) -> p u t", t=P), b.rearrange("p (u t) -> p u t", t=P),
                                              m.unsqueeze(1).to_broadcast([P, units, P]), ALU.mult).then_inc(sem(name), 1)

                        dve.tensor_scalar(e1, K, col("k_k"), None, ALU.mult).then_inc(sem("rw_kk0"), 1)
                        hold("rw_kks", n + 1)
                        dve.tensor_scalar(e2, bank[1][:, 0:T], 1e-24, None, ALU.max).then_inc(sem("rw_kkm"), 1)
                        hold("rw_kkm", n + 1)
                        dve.reciprocal(e2, e2).then_inc(sem("rw_kkinv"), 1)
                        hold("rw_sg", n + 1)
                        dve.tensor_scalar(t1, t1, -DECAY_SCALE, None, ALU.mult).then_inc(sem("rw_ld"), 1)
                        hold("rw_ld", n + 1)
                        dve.tensor_tensor_scan(e0, C1("reset"), t1, 0.0, ALU.mult, ALU.add).then_inc(sem("rw_lc"), 1)
                        hold("rw_lc", n + 1)
                        mul(e5, e0, t1, "rw_lp", ALU.subtract)
                        hold("rw_a", n + 1)
                        hold("rw_lp", n + 1)
                        dve.tensor_scalar(t1, t2, col("k_a"), small[:, bass.ds(n + 3 * T + 66, 1)], ALU.mult, ALU.add)\
                            .then_inc(sem("rw_kf"), 1)
                        hold("rw_kf", n + 1)
                        mul(t1, t1, K, "rw_kh")
                        hold("rw_kkr", n + 1)
                        mul(e1, e1, e2, "rw_kk")
                        hold("rw_kh", n + 1)
                        hold("rw_kk", n + 1)
                        dve.scalar_tensor_tensor(out=e2, in0=R, scalar=col("r_k"), in1=t1, op0=ALU.mult,
                                                 op1=ALU.mult).then_inc(sem("rw_rk"), 1)
                        mul(t2, t2, e1, "rw_ba")
                        hold("rw_pp", n + 1)
                        dve.scalar_tensor_tensor(out=at_, in0=e1, scalar=-1.0, in1=e5, op0=ALU.mult,
                                                 op1=ALU.mult).then_inc(sem("rw_at"), 1)
                        for h in range(2):
                            f = slice(64 * h, 64 * h + 64)
                            dve.scalar_tensor_tensor(out=ah[f, h, :], in0=e1[f, :], scalar=-1.0, in1=e5[f, :],
                                                     op0=ALU.mult, op1=ALU.mult).then_inc(sem("rw_at"), 1)
                        mul(kt_, t1, en, "rw_kt")
                        hold("rw_ba", n + 1)
                        mul(bt_, t2, en, "rw_bt")
                        mul(rt_, R, ep, "rw_rt")
                        dve.tensor_copy(st[:, 8:12], ep.rearrange("p (c t) -> p c t", t=CHUNK)[:, :, CHUNK - 1])\
                            .then_inc(sem("rw_pc"), 1)
                        split(0)
                        split(1)
                        dve.memset(sbd, 0.0).then_inc(sem("rw_s0"), 1)
                        hold("rw_bonus", n + 1)
                        mul(K, bank[1][:, T:2 * T], vf, "rw_bon")
                        hold("rw_l", n + 1)
                        for lv in range(6):
                            mask(low[:, lv].rearrange("p u t -> p (u t)"), bank[0],
                                 C1("m_low")[:, lv * P:(lv + 1) * P], "rw_low")
                        hold("rw_lt", n + 1)
                        mask(um, bank[1], C1("m_u1"), "rw_u0")
                        hold("rw_low", 6 * n + 6)
                        ident4 = C1("ident").unsqueeze(1).to_broadcast([P, 4, P])
                        hold("rw_u0", n + 1)
                        dve.tensor_tensor(um.rearrange("p (u t) -> p u t", t=P), um.rearrange("p (u t) -> p u t", t=P),
                                          ident4, ALU.add).then_inc(sem("rw_u"), 1)
                        dve.tensor_tensor(wm.rearrange("p (u t) -> p u t", t=P), low[:, 0], ident4,
                                          ALU.add).then_inc(sem("rw_w"), 1)
                        split(2)
                        hold("rw_lak", n + 1)
                        mask(lak, bank[2], C1("m_su"), "rw_lakc")
                        hold("rw_rb", n + 1)
                        mask(rb, bank[3], C1("m_ui"), "rw_rbc")
                        hold("rw_rkp", n + 1)
                        mask(rk, bank[0], C1("m_ui"), "rw_rkc")
                        for lv in range(1, 6):
                            hold("rw_du", 5 * n + lv)
                            mul(um, bank[2], um, "rw_u", ALU.add)
                            if lv < 5:
                                hold("rw_dw", 4 * n + lv)
                                mul(wm, bank[3], wm, "rw_w", ALU.add)
                            if lv != 4:
                                split(2 + lv if lv < 5 else 6)
                        hold("rw_xvc", n + 1)
                        for ch in range(NCH):
                            r = slice((ch % 2) * 64, (ch % 2) * 64 + 64)
                            hold("rw_x0", 4 * n + ch + 1)
                            mul(xs[r, :], bank[1][r, 0:P], xv[r, ch // 2, :], "rw_x", ALU.add)
                            hold("rw_ds", 4 * n + ch + 1)
                            dve.scalar_tensor_tensor(out=sbd, in0=bank[3][:, 0:P], scalar=st[:, 8 + ch:9 + ch],
                                                     in1=C1("bmask"), op0=ALU.mult, op1=ALU.mult)\
                                .then_inc(sem("rw_s"), 1)
                        split(7)
                operand_lo("oa", area(0, 8 * T), hh[:, 0:8, :], hl[:, 0:8, :], 8, 8)
                for q in range(4):
                    hold("gn_mean", q + 1)
                    dve.scalar_tensor_tensor(out=tiles(8 + 2 * q, 2), in0=bank[q], scalar=-1.0 / RWKV_HD,
                                             in1=tiles(RR + 2 * q, 2), op0=ALU.mult, op1=ALU.add)\
                        .then_inc(sem("gn_yc"), 1)
                for q in range(4):
                    hold("gn_var", q + 1)
                    o = tiles(16 + 2 * q, 2)
                    dve.tensor_scalar(o, bank[q], 1.0 / RWKV_HD, 64e-5, ALU.mult, ALU.add).then_inc(sem("gn_v"), 1)
                    hold("gn_v", q + 1)
                    dve.reciprocal(o, o).then_inc(sem("gn_inv"), 1)
                hold("gn_rstd", 1)
                dve.tensor_tensor(tiles(8, 8), tiles(8, 8), tiles(16, 8), ALU.mult).then_inc(sem("gn_y"), 1)
                hold("gn_y", 1)
                for k in range(WT):
                    dve.tensor_scalar(tiles(8 + k), tiles(8 + k), V("ln_w", k), V("ln_b", k), ALU.mult, ALU.add)\
                        .then_inc(sem("gn_w"), 1)
                hold("gn_w", 8)
                dve.tensor_tensor(tiles(8, 8), tiles(8, 8), tiles(RK, 8), ALU.add).then_inc(sem("gn_b"), 1)
                hold("gn_b", 1)
                hold("gn_z", 1)
                dve.tensor_tensor(tiles(RR, 8), tiles(8, 8), tiles(RZ, 8), ALU.mult).then_inc(sem("gn_o"), 1)

            def mix1_dve():
                operand_lo("obo", area(RR * T, 8 * T), hh[:, 8:16, :], hl[:, 8:16, :], 8, 8)
                hold("gates_in", 32)
                with dve.Fori(0, 4) as i:
                    for s, k in ((0, 8), (1, 50)):
                        for b in range(4):
                            split_lo(dve, B0["proj1"] + 4 * s + b + AHEAD, 8, i)
                        quad_done(dve, B0["proj1"] + 4 * s + 4, 8, i)
                        dve.tensor_tensor(tile_at(k, i, 4, 4), G[(Q0["proj1"] + s) % 2][:], tile_at(k, i, 4, 4),
                                          ALU.mult).then_inc(sem("quad_read"), 1)
                    dve.wait_ge(sem("quad_read"), at(Q0["proj1"] + 2, 2, i))
                    dve.tensor_tensor(tile_at(8, i, 4, 4), tile_at(8, i, 4, 4), tile_at(50, i, 4, 4), ALU.add)\
                        .then_inc(sem("m1_h"), 4)
                operand_lo("m1", area(8 * T, 16 * T), hh, hl)
                hold("x_again", 16)
                with dve.Fori(0, 2) as i:
                    for s in range(2):
                        for b in range(8):
                            split_lo(dve, B0["out1"] + 8 * s + b + AHEAD, 16, i)
                        quad_done(dve, B0["out1"] + 8 * s + 8, 16, i)
                        xq = x[:, bass.ds(i * 2048 + s * 1024, 1024)]
                        dve.tensor_tensor(xq, G[(Q0["out1"] + s) % 2][:], xq, ALU.add).then_inc(sem("quad_read"), 1)

            def residual(tag, src, gain, banks=None):
                hold(tag + "_rstd", 1)
                for k in range(DT):
                    if k % 4 == 0:
                        s_ = banks[k // 4][:].rearrange("p (k t) -> p k t", t=T) if banks else src[:, k:k + 4, :]
                        dve.tensor_tensor(src[:, k:k + 4, :], s_, stat[2].unsqueeze(1).to_broadcast([P, 4, T]),
                                          ALU.mult).then_inc(sem(tag + "_xr"), 1)
                        hold(tag + "_xr", k // 4 + 1)
                    dve.scalar_tensor_tensor(out=x3[:, k, :], in0=src[:, k, :], scalar=gain[:, k:k + 1],
                                             in1=x3[:, k, :], op0=ALU.mult, op1=ALU.add).then_inc(sem(tag + "_x"), 1)

            def layer2_dve():
                norm_stats("nf", D)
                norm_apply("nf", x3, V("gf"), None, out=x3)
                norm_stats("n2", D)
                hold("ada_sum", 12)
                dve.tensor_tensor(mod, bank[3][:, 0:96], V("b_ada"), ALU.add).then_inc(sem("ada_mod"), 1)
                hold("ada_mod", 1)
                for o, sc_, g in ((gg1, 16, "g_pre_mix"), (gg2, 64, "g_pre_ffn")):
                    dve.tensor_scalar(o, mod[:, sc_:sc_ + 16], 1.0, None, ALU.add).then_inc(sem("gain"), 1)
                hold("gain", 2)
                for o, a, g in ((gg1, gg1, "g_pre_mix"), (gg2, gg2, "g_pre_ffn"), (gr1, mod[:, 32:48], "g_post_mix"),
                                (gr2, mod[:, 80:96], "g_post_ffn")):
                    dve.tensor_tensor(o, a, V(g), ALU.mult).then_inc(sem("gain"), 1)
                hold("gain", 6)
                norm_operand_lo("n2", x3)
                hold("n2_lo", 4)
                hold("rev_p", 1)
                dve.tensor_copy(revs[:, P:2 * P], bank[0][0:36, P:2 * P]).then_inc(sem("rev"), 1)
                dve.memset(revs[:, 0:P], NEG).then_inc(sem("rev"), 1)
                dve.memset(revs[:, 2 * P:3 * P], NEG).then_inc(sem("rev"), 1)
                for o in (qz[64:128, 0, :], qz[0:64, 1, :], p4[:, 0, 0:P], p4[:, 2, 0:P]):
                    dve.memset(o, 0.0).then_inc(sem("swa_zero"), 1)
                for o in (s4[:, 0, 0:P], s4[:, 2, 0:P]):
                    dve.memset(o, NEG).then_inc(sem("swa_neg"), 1)
                for b in range(22):
                    split_lo(dve, B0["lat"] + b + AHEAD)
                with dve.Fori(0, 2) as i:
                    for b in range(16):
                        split_lo(dve, B0["swa"] + b + AHEAD, 16, i)
                for b in range(8):
                    split_lo(dve, B0["swa"] + 32 + b + AHEAD)
                swa_dve()
                mla_dve()
                mix2_dve()
                ffn_dve()

            def swa_dve():
                c = B0["gates2"]
                hold("swa_neg", 2)
                with dve.Fori(0, 4) as i:
                    for p in range(4):
                        n, b0 = 4 * i + p, c + 4 * p

                        def split(b):
                            split_lo(dve, b0 + b + AHEAD, 16, i)

                        def output(p):
                            hold("swa_pv", 4 * i + p + 1)
                            dve.tensor_copy(work[:, bass.ds(i * 4 * T + (SQ + p) * T, T)], bank[2][:, 0:T])\
                                .then_inc(sem("swa_o"), 1)

                        split(0)
                        hold("swa_qk", n + 1)
                        dve.wait_ge(sem(f"bias_in{p % 2}"), i * 32 + 16 * (p // 2 + 1))
                        bs = bias[p % 2]
                        for h in range(2):
                            dve.scalar_tensor_tensor(out=s4[:, 2 * h, P:T], in0=bank[h][:, 0:P], scalar=SWA_SCALE,
                                                     in1=bs[:, h, P:T], op0=ALU.mult, op1=ALU.add)\
                                .then_inc(sem("swa_sb"), 1)
                            dve.scalar_tensor_tensor(out=s4[:, 2 * h + 1, :], in0=bank[h][:, P:P + T],
                                                     scalar=SWA_SCALE, in1=bs[:, h, :], op0=ALU.mult, op1=ALU.add)\
                                .then_inc(sem("swa_s"), 1)
                        hold("swa_sb", 2 * n + 2)
                        hold("swa_s", 2 * n + 2)
                        dve.tensor_reduce(st[:, 0:4], s4, AX.X, ALU.max).then_inc(sem("swa_mx"), 1)
                        hold("swa_mx", n + 1)
                        sink = vec[:, bass.ds(2 * n + VEC["sinks"][0], 2)].unsqueeze(2).to_broadcast([P, 2, 2])

                        def two(a):
                            return st[:, a:a + 4].rearrange("p (h b) -> p h b", b=2)

                        dve.tensor_tensor(two(4), two(0), sink, ALU.max).then_inc(sem("swa_m"), 1)
                        hold("swa_m", n + 1)
                        dve.tensor_scalar(st[:, 8:12], st[:, 4:8], -1.0, None, ALU.mult).then_inc(sem("swa_nm"), 1)
                        hold("swa_nm", n + 1)
                        dve.tensor_tensor(two(12), two(8), sink, ALU.add).then_inc(sem("swa_d"), 1)
                        if p:
                            output(p - 1)
                        split(1)
                        hold("swa_es", n + 1)
                        hold("swa_e", 4 * n + 4)
                        dve.tensor_tensor(st[:, 20:24], st[:, 16:20], st[:, 28:32], ALU.add).then_inc(sem("swa_tot"), 1)
                        hold("swa_tot", n + 1)
                        dve.reciprocal(st[:, 24:28], st[:, 20:24]).then_inc(sem("swa_rs"), 1)
                        hold("swa_rs", n + 1)
                        dve.tensor_tensor(p4, p4, st[:, 24:28].unsqueeze(2).to_broadcast([P, 4, T]), ALU.mult)\
                            .then_inc(sem("swa_p"), 1)
                        split(2)
                        split(3)
                        if p == 3:
                            output(3)

            def mla_dve():
                hold("swa_o", 16)
                norm_stats("nq", QR, 6, msq)
                norm_apply("nq", lat, V("g_q"), None, 6, 6, msq)
                norm_stats("nk", KVR, 4, msq[:, 6:10, :])
                operand_lo("nq", msq, hh, hl, 6, 6)
                norm_apply("nk", lat[:, 6:10, :], V("g_kv"), None, 4, 4, msq[:, 6:10, :])
                operand_lo("nk", msq[:, 6:10, :], hh[:, 6:10, :], hl[:, 6:10, :], 4, 4)
                hold("nk_lo", 1)
                for o in (qr[64:128, 0, :], qr[0:64, 1, :]):
                    dve.memset(o, 0.0).then_inc(sem("mla_zero"), 1)

                def rope(src, dst, n):
                    if n:
                        hold("rope", n)
                    hold("rot", n + 1)
                    dve.tensor_tensor(rt1, bank[2][:, 0:T], C2("sin"), ALU.mult).then_inc(sem("rope_s"), 1)
                    dve.tensor_tensor(rt2, src, C2("cos"), ALU.mult).then_inc(sem("rope_c"), 1)
                    hold("rope_s", n + 1)
                    hold("rope_c", n + 1)
                    dve.tensor_tensor(dst, rt1, rt2, ALU.add).then_inc(sem("rope"), 1)

                rope(lat[:, 10, :], krr, 0)
                for b in range(18):
                    split_lo(dve, B0["uq"] + b + AHEAD)
                    if b in (3, 14):
                        h = b // 14
                        r = slice(h * 8 * T, (h + 1) * 8 * T)
                        hold("gates2_in", 16 * h + 16)
                        dve.tensor_tensor(tiles(SQ, 16)[:, r], tiles(SQ, 16)[:, r], gbuf, ALU.mult)\
                            .then_inc(sem("m2_g"), 1)
                for k in range(8):
                    rope(tiles(MR + k), tiles(MR + k), k + 1)
                def output(n0, i=None):
                    hold("mla_pv", at(n0 + 1, 2, i))
                    dve.tensor_copy(tile_at(MQ + 2 * n0, i, 2, 4), bank[2]).then_inc(sem("mla_o"), 1)

                def turn(n0, i=None, last=False):
                    hold("mla_qk", at(n0 + 1, 2, i))
                    dve.tensor_tensor(ms4.rearrange("p (h b) t -> p h (b t)", b=2),
                                      A[0][:].rearrange("p (h b) -> p h b", h=2),
                                      C2("causal").unsqueeze(1).to_broadcast([P, 2, 512]), ALU.add)\
                        .then_inc(sem("mla_s"), 1)
                    hold("mla_s", at(n0 + 1, 2, i))
                    dve.tensor_reduce(st[:, 0:4], ms4, AX.X, ALU.max).then_inc(sem("mla_mx"), 1)
                    hold("mla_mx", at(n0 + 1, 2, i))
                    dve.tensor_scalar(st[:, 8:12], st[:, 0:4], -1.0, None, ALU.mult).then_inc(sem("mla_nm"), 1)
                    if n0:
                        output(n0 - 1, i)
                    hold("mla_e", at(4 * n0 + 4, 8, i))
                    dve.reciprocal(st[:, 24:28], st[:, 16:20]).then_inc(sem("mla_rs"), 1)
                    hold("mla_rs", at(n0 + 1, 2, i))
                    dve.tensor_tensor(mp4, mp4, st[:, 24:28].unsqueeze(2).to_broadcast([P, 4, T]), ALU.mult)\
                        .then_inc(sem("mla_p"), 1)
                    if not last:
                        for b in range(2):
                            split_lo(dve, B0["ukv"] + 2 * n0 + 2 + b + AHEAD, 4, i)

                for b in range(2):
                    split_lo(dve, B0["ukv"] + b + AHEAD)
                turn(0)
                with dve.Fori(0, 3) as i:
                    for s in range(2):
                        turn(1 + s, i)
                turn(7, last=True)
                output(7)

            def mix2_dve():
                oa, ob = tiles(MQ, 16), tiles(SQ, 16)
                hold("mla_o", 8)
                for c in range(5):
                    if c < 4:
                        r = slice(c * BLK, (c + 1) * BLK)
                        g = gbuf[:, r] if c < 2 else tiles(63 + 4 * (c - 2), 4)
                        hold("gates2_in", 48 if c < 2 else 64)
                        dve.tensor_tensor(oa[:, r], oa[:, r], g, ALU.mult).then_inc(sem("m2_g"), 1)
                        hold("m2_g", c + 3)
                        dve.tensor_tensor(oa[:, r], oa[:, r], ob[:, r], ALU.add).then_inc(sem("m2_h"), 4)
                    if c:
                        k = slice(4 * c - 4, 4 * c)
                        hold("m2_hi", c)
                        dve.tensor_tensor(hl[:, k, :], area(MQ * T, 16 * T)[:, k, :], hh[:, k, :].bitcast(F32),
                                          ALU.subtract).then_inc(sem("m2_lo"), 1)
                with dve.Fori(0, 2) as i:
                    for b in range(16):
                        split_lo(dve, B0["out2"] + b + AHEAD, 16, i)
                norm_stats("r1", D)
                residual("r1", area(0, 16 * T), gr1)

            def ffn_dve():
                norm_stats("n3", D)
                norm_operand_lo("n3", x3)
                c = B0["up"]
                with dve.Fori(0, 11) as i:
                    for s in range(2):
                        for b in range(8):
                            split_lo(dve, c + 8 * s + b + AHEAD, 16, i)
                        hold("ffn_c", 8 * i + 4 * s + 4)
                        g = G[(Q0["up"] + s) % 2]
                        for j in (1, 2):
                            for k in range(4):
                                col = i * 4 + 44 * s + k
                                if j == 2:
                                    hold("ffn_cv", 14 * i + 7 * s + k + 1)
                                o = tiles(44 + 4 * s + k)[:, j:T]
                                dve.scalar_tensor_tensor(
                                    out=o, in0=g[:, k * T:(k + 1) * T - j],
                                    scalar=vec[:, bass.ds(col + VEC["conv_w"][0] + 88 * (2 - j), 1)], in1=o,
                                    op0=ALU.mult, op1=ALU.add)\
                                    .then_inc(sem("quad_read" if j == 2 and k == 3 else "ffn_cv"), 1)
                    dve.wait_ge(sem("quad_read"), at(Q0["up"] + 2, 2, i))
                    hold("ffn_z", i + 1)
                    dve.tensor_tensor(tile_at(0, i, 4, 4), tiles(44, 4), tiles(48, 4), ALU.mult)\
                        .then_inc(sem("ffn_y"), 1)
                c = B0["down"]

                def y_lo(k, i=None):
                    hold("y_hi", at(k + 1, 2, i))
                    r = slice(2 * (k % 2), 2 * (k % 2) + 2)
                    dve.tensor_tensor(yl[:, r, :].rearrange("p k t -> p (k t)"),
                                      tiles(2 * k, 2) if i is None else tile_at(2 * k, i, 2, 4),
                                      yh[:, r, :].rearrange("p k t -> p (k t)").bitcast(F32), ALU.subtract)\
                        .then_inc(sem("y_lo"), 1)

                def turn(k0, i=None, last=False):
                    for k in (k0, k0 + 1):
                        if not (last and k == k0 + 1):
                            y_lo(k + 1, i)
                        for b in range(4):
                            split_lo(dve, c + 4 * k + b + AHEAD, 8, i)

                y_lo(0)
                turn(0)
                with dve.Fori(0, 9) as i:
                    turn(2, i)
                turn(20, last=True)
                norm_stats("r2", D, DT, area(0, 16 * T))
                hold("down_out", 1)
                residual("r2", area(44 * T, 16 * T), gr2, (G[0], G[1], tiles(52, 4), A[1]))

            hold("vec_loaded", 16)
            dve.tensor_scalar(omm, vec[:, VEC["mu"][0]:VEC["mu"][0] + 34], -1.0, 1.0, ALU.mult, ALU.add).then_inc(sem("omm"), 1)
            norm_stats("n1", D)
            for c in range(AHEAD):
                split_lo(dve, c)
            norm_operand_lo("n1", x3)
            c = B0["fox"]
            for b in range(16):
                split_lo(dve, c + b + AHEAD)
            with dve.Fori(0, 3) as i:
                for b in range(16):
                    split_lo(dve, c + 16 + b + AHEAD, 16, i)
            c = B0["waf"]
            for b in range(4):
                split_lo(dve, c + b + AHEAD)
            for k in range(2):
                hold("waf_own", 2)
                hold("f_x", 1)
                dve.scalar_tensor_tensor(out=waf[:, k, 1:T], in0=G[0][:, k * T:(k + 1) * T - 1],
                                         scalar=V("mu_w" if k == 0 else "mu_a"), in1=waf[:, k, 1:T],
                                         op0=ALU.mult, op1=ALU.add).then_inc(sem("waf_mix" if k == 0 else "quad_read"), 1)
            hold("f_ln", 1)
            dve.tensor_scalar(lsg[2], lsg[0], 0.0, None, ALU.min).then_inc(sem("f_min"), 1)
            dve.memset(aug_l, 0.0).then_inc(sem("aug_z"), 1)
            dve.memset(aug_r, 0.0).then_inc(sem("aug_z"), 1)
            dve.memset(lsg[3], 1.0).then_inc(sem("aug_z"), 1)
            hold("f_min", 1)
            dve.tensor_tensor(lsg[2], lsg[2], lsg[1], ALU.subtract).then_inc(sem("f_log"), 1)
            hold("f_log", 1)
            hold("aug_z", 3)
            dve.tensor_tensor_scan(aug_l[0:8, :], lsg[3], lsg[2], 0.0, ALU.mult, ALU.add).then_inc(sem("f_sum"), 1)
            dve.memset(aug_l[32:40, :], 1.0).then_inc(sem("aug_1"), 1)
            dve.memset(aug_r[0:8, :], 1.0).then_inc(sem("aug_1"), 1)
            hold("f_sum", 1)
            dve.tensor_scalar(aug_r[32:40, :], aug_l[0:8, :], -1.0, None, ALU.mult).then_inc(sem("aug_1"), 1)
            hold("aug_1", 3)
            hold("fox_z", 1)
            c = B0["rwkv"]
            dve.tensor_scalar(aug_h, aug_r, C1("selcol", 40)[:, 0:1], None, ALU.mult).then_inc(sem("fox_aug"), 1)
            with dve.Fori(0, FOX_HEADS // 2) as i:
                for s in range(2):
                    g, b0 = G[(Q0["rwkv"] + s) % 2], c + 8 * s
                    n = 2 * i + s
                    for b in (0, 1):
                        split_lo(dve, b0 + b + AHEAD, 16, i)
                    hold("fox_qk", n + 1)
                    hold("fox_e", n * 2)
                    dve.tensor_tensor(scf, bank[0], C1("causal"), ALU.add).then_inc(sem("fox_s"), 1)
                    hold("fox_s", n + 1)
                    dve.tensor_reduce(st[:, 0:2], sc, AX.X, ALU.max).then_inc(sem("fox_mx"), 1)
                    hold("fox_mx", n + 1)
                    dve.tensor_scalar(st[:, 2:4], st[:, 0:2], -1.0, None, ALU.mult).then_inc(sem("fox_nm"), 1)
                    hold("fox_e", n * 2 + 2)
                    dve.reciprocal(st[:, 6:8], st[:, 4:6]).then_inc(sem("fox_rs"), 1)
                    hold("fox_rs", n + 1)
                    dve.tensor_scalar(pr[:, 0, 0:P], pr[:, 0, 0:P], st[:, 6:7], None, ALU.mult)\
                        .then_inc(sem("fox_p"), 1)
                    dve.tensor_scalar(pr[:, 1, :], pr[:, 1, :], st[:, 7:8], None, ALU.mult).then_inc(sem("fox_p"), 1)
                    dve.tensor_scalar(aug_h, aug_r, con[0:40, bass.ds(2 * i + s + 1 + CON1["selcol"][0], 1)], None,
                                      ALU.mult).then_inc(sem("fox_aug"), 1)
                    for b in (2, 3, 4, 5):
                        split_lo(dve, b0 + b + AHEAD, 16, i)
                    hold("fox_pv", n + 1)
                    dve.tensor_tensor(tile_at(s, i, 1, 2), bank[2][:, 0:T], tile_at(16 + s, i, 1, 2), ALU.mult)\
                        .then_inc(sem("fox_o"), 1)
                    for b in (6, 7):
                        split_lo(dve, b0 + b + AHEAD, 16, i)
                    hold("rw_own", n * 4 + 4)
                    for k in range(4):
                        o = i * (8 * T) + (RR + 4 * s + k) * T + 1
                        dve.scalar_tensor_tensor(
                            out=work[:, bass.ds(o, T - 1)], in0=g[:, k * T:(k + 1) * T - 1],
                            scalar=vec[:, bass.ds(i * 8 + VEC["mu"][0] + 4 * s + k, 1)], in1=work[:, bass.ds(o, T - 1)],
                            op0=ALU.mult, op1=ALU.add).then_inc(sem("rw_shift" if k < 3 else "quad_read"), 1)
            rwkv_dve()
            mix1_dve()
            layer2_dve()

        @blk.tensor
        def _(pe):
            hold = waiter(pe)
            prime(pe, "pe")

            def norm_sum(tag):
                ones = C1("ones") if tag in ("n1", "nf", "n2") else C2("ones")
                for c in range(4):
                    hold(tag + "_part", c + 1)
                    m = pe.matmul(bank[0][:, 0:T], ones, nsum[:, c, :], start=c == 0, stop=c == 3)
                m.then_inc(sem(tag + "_sum"), 1)

            def rwkv_pe():
                c, q = B0["gates1"], Q0["gates1"]
                hold("tanh_w", 1)
                hold("rw_zero", 4)
                pe.wait_ge(sem("quad_read"), Q0["rwkv"])
                with pe.Fori(0, WT // 2) as i:
                    for s in range(2):
                        n, g = 2 * i + s, (q + s) % 2

                        def part(b, *tiles_):
                            if b == 0:
                                pe.wait_ge(sem("quad_read"), at(q + s - 1, 2, i))
                            block(pe, c + 8 * s + b, 16, i, 512, hh, hl, 2 * b, g, b == 0, b == NQ - 1,
                                  piece=tiles_ or (0, 4))

                        def quarter(n):
                            part(4 + n // 4, n % 4, n % 4 + 1)

                        def mm(o, l, r, start=True, stop=True):
                            return pe.matmul(o, l, r, start=start, stop=stop, skip_group_check=True)

                        def gram(o, l, r, name):
                            for u in range(4):
                                t = slice(P * (u % 2), P * (u % 2) + P)
                                m = mm(o[:, u * P:(u + 1) * P], l[:, t] if l is bt_ or l is kt_ else l[:, u // 2, t],
                                       r[:, t] if r is bt_ else r[:, u // 2, t], start=u == 0)
                            m.then_inc(sem(name), 1)

                        pe.wait_ge(sem("lora_in"), 16 * n + 16)
                        hold("rw_y", n)
                        mm(bank[0][:, 0:T], lw[:, 0:P], waf[0:LORA, 0, :])
                        mm(bank[0][:, T:2 * T], lw[:, P:2 * P], waf[0:LORA, 1, :], start=False)\
                            .then_inc(sem("rw_lora"), 1)
                        hold("rw_kk2", n + 1)
                        mm(bank[1][:, 0:T], C1("bones"), e2).then_inc(sem("rw_kks"), 1)
                        part(0)
                        part(1)
                        hold("rw_rk", n + 1)
                        mm(bank[1][:, T:2 * T], C1("bones"), e2, start=False).then_inc(sem("rw_bonus"), 1)
                        part(2)
                        hold("rw_bt", n + 1)
                        hold("rw_kt", n + 1)
                        for m, src in enumerate((bt_, bt_, kt_, kt_)):
                            t = pe.transpose(bank[2][:, m * P:(m + 1) * P], src[:, (m % 2) * P:(m % 2 + 1) * P],
                                             C1("ident"))
                        t.then_inc(sem("rw_tr"), 1)
                        hold("rw_v", n + 1)
                        for m in range(2):
                            t = pe.transpose(bank[3][:, m * P:(m + 1) * P], vf[:, m * P:(m + 1) * P], C1("ident"))
                        t.then_inc(sem("rw_trv"), 1)
                        hold("rw_a", n + 1)
                        hold("rw_at", 3 * n + 3)
                        gram(bank[0], ah, bt_, "rw_l")
                        hold("rw_bon", n + 1)
                        gram(bank[1], bt_, ah, "rw_lt")
                        hold("rw_tok", n + 1)
                        gram(bank[2], kt_, ah, "rw_lak")
                        hold("rw_vtok", n + 1)
                        hold("rw_rh", 2 * n + 2)
                        gram(bank[3], bt_, rh_, "rw_rb")
                        part(3)
                        hold("rw_low", 6 * n + 6)
                        gram(bank[0], kt_, rh_, "rw_rkp")
                        for lv in range(1, 6):
                            hold("rw_u", 6 * n + lv)
                            for u in range(4):
                                m = mm(bank[1][:, u * P:(u + 1) * P], low[:, lv, u, :], um[:, u * P:(u + 1) * P],
                                       start=u == 0)
                            m.then_inc(sem("rw_g"), 1)
                            if lv < 5:
                                quarter(2 * lv - 2)
                            hold("rw_gc", 5 * n + lv)
                            hold("rw_w", 5 * n + lv)
                            hold("rw_rbc", n + 1)
                            for u in range(4):
                                m = mm(bank[2][:, u * P:(u + 1) * P], wm[:, u * P:(u + 1) * P],
                                       gm[:, u * P:(u + 1) * P], start=u == 0)
                            m.then_inc(sem("rw_du"), 1)
                            if lv < 5:
                                for u in range(4):
                                    m = mm(bank[3][:, u * P:(u + 1) * P], gm[:, u * P:(u + 1) * P],
                                           wm[:, u * P:(u + 1) * P], start=u == 0)
                                m.then_inc(sem("rw_dw"), 1)
                            if lv < 5:
                                quarter(2 * lv - 1)
                        hold("rw_rkc", n + 1)
                        for u in range(4):
                            h, t = u // 2, u % 2
                            m = mm(bank[0][:, t * P + 64 * h:t * P + 64 * h + 64], lak[:, u * P:(u + 1) * P],
                                   vtok[:, t, 64 * h:64 * h + 64], start=u == 0)
                        m.then_inc(sem("rw_xv"), 1)
                        hold("rw_u", 6 * n + 6)
                        hold("rw_s0", n + 1)
                        hold("rw_xvc", n + 1)
                        for ch in range(NCH):
                            r0, t = (ch % 2) * 64, ch // 2
                            r, k = slice(r0, r0 + 64), slice(ch * CHUNK, (ch + 1) * CHUNK)
                            if ch:
                                hold("rw_s", 4 * n + ch)
                            mm(bank[1][r, 0:P], at_[:, k], sbd).then_inc(sem("rw_x0"), 1)
                            mm(bank[0][:, k], sbd, rt_[:, k], start=ch == 0, stop=False)
                            quarter(8 + 2 * ch)
                            hold("rw_x", 4 * n + ch + 1)
                            mm(bank[3][:, 0:P], C1("ident"), sbd, stop=False)
                            for h in range(2):
                                u = 2 * h + t
                                m = mm(bank[2][r, 64 * h:64 * h + 64], um[r, u * P + r0:u * P + r0 + 64],
                                       xs[r, 64 * h:64 * h + 64], start=h == 0)
                            m.then_inc(sem("rw_sa"), 1)
                            mm(bank[3][:, 0:P], ktok[r, t, :], vtok[r, t, :], start=False, stop=False)
                            hold("rw_sac", 4 * n + ch + 1)
                            mm(bank[3][:, 0:P], btok[r, t, :], sa[r, t, :], start=False).then_inc(sem("rw_ds"), 1)
                            quarter(9 + 2 * ch)
                        for u in range(4):
                            h, t = u // 2, u % 2
                            o = bank[0][64 * h:64 * h + 64, t * P:(t + 1) * P]
                            mm(o, sa[:, t, 64 * h:64 * h + 64], rb[:, u * P:(u + 1) * P], start=False, stop=False)
                            m = mm(o, vtok[:, t, 64 * h:64 * h + 64], rk[:, u * P:(u + 1) * P], start=False)
                        m.then_inc(sem("rw_yp"), 1)
                for q in range(4):
                    hold("rw_y", 8)
                    if q:
                        hold("rw_s", 32)
                    pe.matmul(bank[q], C1("bones"), tiles(RR + 2 * q, 2), start=True, stop=True)\
                        .then_inc(sem("gn_mean"), 1)
                for q in range(4):
                    hold("gn_sq", q + 1)
                    pe.matmul(bank[q], C1("bones"), tiles(16 + 2 * q, 2), start=True, stop=True)\
                        .then_inc(sem("gn_var"), 1)

            def ada_sums(groups):
                for g in groups:
                    s = g % 4
                    src = (adaw if s < 2 else adap)[:, (s % 2) * 1024:(s % 2 + 1) * 1024]
                    pe.wait_ge(sem(f"ada_back{s}"), 16 * (g // 4 + 1))
                    for j in range(8):
                        m = pe.matmul(bank[3][:, 8 * g + j:8 * g + j + 1], src[:, j * P:(j + 1) * P],
                                      C1("ones")[:, 0:1], start=g == 0 and j == 0, stop=True, skip_group_check=True)
                    m.then_inc(sem("ada_sum"), 1)

            def mix1_pe():
                hold("gn_inv", 4)
                hold("oa_lo", 1)
                with pe.Fori(0, 4) as i:
                    for s in range(2):
                        if s:
                            hold("obo_lo", 1)
                        quad_pe(pe, B0["proj1"] + 4 * s, 8, i, Q0["proj1"] + s, 2, (Q0["proj1"] + s) % 2, nb=4,
                                rh=hh[:, 8 * s:8 * s + 8, :], rl=hl[:, 8 * s:8 * s + 8, :])
                ada_sums(range(0, 4))
                with pe.Fori(0, 2) as i:
                    for s in range(2):
                        quad_pe(pe, B0["out1"] + 8 * s, 16, i, Q0["out1"] + s, 2, (Q0["out1"] + s) % 2,
                                operand=None if s else "m1")

                ada_sums(range(4, 8))

            def layer2_pe():
                norm_sum("nf")
                ada_sums(range(8, 12))
                hold("nf_ms", 1)
                norm_sum("n2")
                hold("n2_ms", 1)
                hold("con2_in", 16)
                hold("rel_in", 16)
                pe.matmul(bank[0][0:36, 0:384], rel, C2("onehot", BUCKETS), start=True, stop=True)\
                    .then_inc(sem("rev_p"), 1)
                c, q = B0["lat"], Q0["lat"]
                for cols, nb in ((512, 8), (512, 8), (256, 4), (P, 2)):
                    quad_pe(pe, c, 0, None, q, 0, q % 2, cols, nb, operand="n2" if nb == 8 else None)
                    c, q = c + nb, q + 1
                with pe.Fori(0, 2) as i:
                    for s in range(2):
                        quad_pe(pe, B0["swa"] + 8 * s, 16, i, Q0["swa"] + s, 2, (Q0["swa"] + s) % 2)
                q = Q0["swa"] + 4
                pe.wait_ge(sem("quad_read"), q - 1)
                for b in range(8):
                    block(pe, B0["swa"] + 32 + b, 0, None, 512, hh, hl, 2 * b, q % 2, b == 0, b == 7,
                          parts=((False, 0, 0), (False, 1, T), (True, slice(256, 512), 512)))
                swa_pe()
                mla_pe()
                mix2_pe()
                ffn_pe()

            def swa_pe():
                c, q = B0["gates2"], Q0["gates2"]
                hold("swa_k", 8)
                pe.wait_ge(sem("quad_read"), q)
                with pe.Fori(0, 4) as i:
                    for p in range(4):
                        n = 4 * i + p
                        s = p // 2

                        def part(b):
                            if p % 2 == 0 and b == 0:
                                pe.wait_ge(sem("quad_read"), at(q + s - 1, 2, i))
                            b += 4 * (p % 2)
                            block(pe, c + 8 * s + b, 16, i, 512, hh, hl, 2 * b, (q + s) % 2, b == 0, b == NQ - 1)

                        def mm(o, l, r, start):
                            return pe.matmul(o, l, r, start=start, stop=True, skip_group_check=True)

                        def scores(p):
                            hold("swa_q", 2 * (4 * i + p) + 2)
                            for h in range(2):
                                mm(bank[h][:, 0:P], qz[:, h, 0:P], work[:, bass.ds(i * T + SK * T, P)], True)
                                m = mm(bank[h][:, P:P + T], qz[:, h, P:T], work[:, bass.ds(i * T + SK * T, T)], False)
                            m.then_inc(sem("swa_qk"), 1)

                        if p == 0:
                            scores(0)
                        part(0)
                        part(1)
                        part(2)
                        hold("swa_p", n + 1)
                        hold("swa_o", n)
                        for h in range(2):
                            for j, (b, k) in enumerate(((0, 1), (1, 0), (1, 1))):
                                m = pe.transpose(bank[2 + h][:, j * P:(j + 1) * P],
                                                 p4[:, 2 * h + b, k * P:(k + 1) * P], C2("ident"))
                        m.then_inc(sem("swa_t"), 1)
                        if p < 3:
                            scores(p + 1)
                        part(3)
                        hold("swa_pt", 2 * n + 2)
                        hold("swa_v", i + 1)
                        for h in range(2):
                            o = bank[2][64 * h:64 * h + 64, :]
                            pt3 = spt[:, 384 * h:384 * h + 384]
                            mm(o[:, 0:P], vst[:, 0, :], pt3[:, 0:P], True)
                            mm(o[:, P:T], vst[:, 0, :], pt3[:, P:2 * P], False)
                            m = mm(o[:, P:T], vst[:, 1, :], pt3[:, 2 * P:3 * P], False)
                        m.then_inc(sem("swa_pv"), 1)

            def mla_pe():
                hold("nq_part", 1)
                pe.matmul(bank[0][:, 0:T], C2("ones"), stat[0], start=True, stop=True).then_inc(sem("nq_sum"), 1)
                hold("nk_part", 1)
                pe.matmul(bank[0][:, 0:T], C2("ones"), stat[0], start=True, stop=True).then_inc(sem("nk_sum"), 1)
                pe.matmul(bank[2][:, 0:T], C2("rot"), lat[:, 10, :], start=True, stop=True).then_inc(sem("rot"), 1)
                hold("nq_lo", 1)
                for q in range(6):
                    quad_pe(pe, B0["uq"] + 3 * q, 0, None, Q0["uq"] + q, 0, (Q0["uq"] + q) % 2, nb=3)
                pe.wait_ge(sem("quad_read"), Q0["uq"] + 6)
                for k in range(8):
                    hold("rope_s", k + 1)
                    pe.matmul(bank[2][:, 0:T], C2("rot"), tiles(MR + k), start=True, stop=True).then_inc(sem("rot"), 1)
                hold("nk_lo", 1)
                hold("rope", 9)
                c, q = B0["ukv"], Q0["ukv"]

                def mm(o, l, r, start):
                    return pe.matmul(o, l, r, start=start, stop=True, skip_group_check=True)

                def keys_values(n0, i=None):
                    pe.wait_ge(sem("quad_read"), at(q + n0 - 1, 2, i))
                    for b in range(2):
                        block(pe, c + 2 * n0 + b, 4, i, 512, hh[:, 6:10, :], hl[:, 6:10, :], 2 * b, (q + n0) % 2,
                              b == 0, b == 1, parts=((False, 0, 0), (False, 2, T), (True, "v", 512)))

                def scores(n0, i=None):
                    hold("mla_q", at(n0 + 1, 2, i))
                    hold("mla_qr", at(2 * n0 + 2, 4, i))
                    hold("mla_k", at(n0 + 1, 2, i))
                    for h in range(2):
                        for b in range(2):
                            o = bank[h][:, b * T:(b + 1) * T]
                            mm(o, qn[:, h, b * P:(b + 1) * P], kn[n0 % 2][:, h, :], b == 0)
                            m = mm(o, qr[:, h, b * P:(b + 1) * P], krr, False)
                    m.then_inc(sem("mla_qk"), 1)

                def turn(n0, i=None, last=False):
                    if not last:
                        keys_values(n0 + 1, i)
                    hold("mla_p", at(n0 + 1, 2, i))
                    if n0:
                        hold("mla_o", at(n0, 2, i))
                    for h in range(2):
                        for j, (b, k) in enumerate(((0, 0), (1, 0), (1, 1))):
                            m = pe.transpose(bank[2 + h][:, j * P:(j + 1) * P],
                                             mp4[:, 2 * h + b, k * P:(k + 1) * P], C2("ident"))
                    m.then_inc(sem("mla_t"), 1)
                    if not last:
                        scores(n0 + 1, i)
                    hold("mla_pt", at(2 * n0 + 2, 4, i))
                    pe.wait_ge(sem("quad_read"), at(q + n0 + 1, 2, i))
                    for h in range(2):
                        o = bank[2][:, h * T:(h + 1) * T]
                        pt3 = mpt[:, 384 * h:384 * h + 384]
                        v0, v1 = (vv[n0 % 2][:, t, h * P:(h + 1) * P] for t in range(2))
                        mm(o[:, 0:P], v0, pt3[:, 0:P], h == 0)
                        mm(o[:, P:T], v0, pt3[:, P:2 * P], False)
                        m = mm(o[:, P:T], v1, pt3[:, 2 * P:3 * P], False)
                    m.then_inc(sem("mla_pv"), 1)

                keys_values(0)
                scores(0)
                turn(0)
                with pe.Fori(0, 3) as i:
                    for s in range(2):
                        turn(1 + s, i)
                turn(7, last=True)

            def mix2_pe():
                with pe.Fori(0, 2) as i:
                    for s in range(2):
                        quad_pe(pe, B0["out2"] + 8 * s, 16, i, Q0["out2"] + s, 2, (Q0["out2"] + s) % 2,
                                operand=None if s else "m2")
                norm_sum("r1")

            def ffn_pe():
                hold("r1_x", 1)
                norm_sum("n3")
                with pe.Fori(0, 11) as i:
                    for s in range(2):
                        quad_pe(pe, B0["up"] + 8 * s, 16, i, Q0["up"] + s, 2, (Q0["up"] + s) % 2,
                                operand=None if s else "n3")
                c = B0["down"]
                pe.wait_ge(sem("quad_read"), Q0["up"] + 22)

                def turn(k0, i=None, first=False, last=False):
                    for k in (k0, k0 + 1):
                        hold("y_lo", at(k + 1, 2, i))
                        for b, g in enumerate((G[0], G[1], A[0], A[1])):
                            block(pe, c + 4 * k + b, 8, i, 512, yh, yl, 2 * (k % 2), g, first and k == k0,
                                  last and k == k0 + 1)

                turn(0, first=True)
                with pe.Fori(0, 9) as i:
                    turn(2, i)
                turn(20, last=True)
                hold("down_out", 1)
                norm_sum("r2")

            hold("con_loaded", 16)
            norm_sum("n1")
            c, q = B0["fox"], Q0["fox"]
            for s in range(2):
                quad_pe(pe, c + 8 * s, 0, None, q + s, 0, s, token=True, operand="n1")
            with pe.Fori(0, 3) as i:
                for s in range(2):
                    quad_pe(pe, c + 16 + 8 * s, 16, i, q + 2 + s, 2, s)
            quad_pe(pe, B0["waf"], 0, None, Q0["waf"], 0, 0, cols=256, nb=4)
            c, q = B0["rwkv"], Q0["rwkv"]
            hold("fox_z", 1)

            def scores(n, k):
                hold("fox_q", n + 1)
                hold("fox_aug", n + 1)
                hold("fox_s", n)
                for b in range(TT):
                    o = bank[0][:, b * T:(b + 1) * T]
                    pe.matmul(o, fq[:, b * P:(b + 1) * P], k, start=b == 0, stop=False, skip_group_check=True)
                    mm = pe.matmul(o, aug_l[:, b * P:(b + 1) * P], aug_h, start=False, stop=True,
                                   skip_group_check=True)
                mm.then_inc(sem("fox_qk"), 1)

            scores(0, tiles(8))
            with pe.Fori(0, FOX_HEADS // 2) as i:
                for s in range(2):
                    n, g = 2 * i + s, (q + s) % 2

                    def part(b0, b1):
                        for b in range(b0, b1):
                            block(pe, c + 8 * s + b, 16, i, 512, hh, hl, 2 * b, g, b == 0, b == NQ - 1)

                    pe.wait_ge(sem("quad_read"), at(q + s - 1, 2, i))
                    part(0, 3)
                    hold("fox_p", n * 2 + 2)
                    hold("fox_pt", n)
                    for m, (b, k) in enumerate(((0, 0), (1, 0), (1, 1))):
                        mm = pe.transpose(bank[1][:, m * P:(m + 1) * P], pr[:, b, k * P:(k + 1) * P], C1("ident"))
                    mm.then_inc(sem("fox_t"), 1)
                    scores(n + 1, tile_at(9 + s, i, 1, 2))
                    part(3, 5)
                    hold("fox_pt", n + 1)
                    hold("fox_v", n + 1)
                    hold("fox_o", n)
                    o = bank[2]
                    pe.matmul(o[:, 0:P], fv[:, 0, :], ptf[:, 0:P], start=True, stop=True, skip_group_check=True)
                    pe.matmul(o[:, P:T], fv[:, 0, :], ptf[:, P:2 * P], start=False, stop=False, skip_group_check=True)
                    pe.matmul(o[:, P:T], fv[:, 1, :], ptf[:, 2 * P:3 * P], start=False, stop=True,
                              skip_group_check=True).then_inc(sem("fox_pv"), 1)
                    part(5, 8)
            rwkv_pe()
            mix1_pe()
            layer2_pe()


def _blocks(w, cols, token=False):
    k, n = w.shape
    ks = BLK // cols
    b = w.reshape(k // (ks * P), ks, P, n // cols, cols).transpose(3, 0, 2, 1, 4)
    return b.reshape(-1, P, BLK)


def _cols(v, tiles):
    return np.ascontiguousarray(v.reshape(tiles, P).T)


def _layout(a):
    f = np.float32
    wi = a["w_in"][0]
    o = {"q": 0, "k": W1, "v": 2 * W1, "z": 3 * W1, "f": 4 * W1}
    r0 = FOX_COLS
    lora = r0 + 4 * W1
    zero = np.zeros((D, 1), f)
    waf = np.concatenate([wi[:, lora:lora + LORA], wi[:, 4 * W1:FOX_COLS], np.repeat(zero, 24, 1),
                          wi[:, lora + LORA:lora + 2 * LORA], np.repeat(zero, 32, 1)], 1)
    g0 = FOX_COLS + RWKV_COLS
    parts = [_blocks(np.concatenate([wi[:, 2 * W1:3 * W1], wi[:, 0:2 * W1], wi[:, 3 * W1:4 * W1]], 1), 512),
             _blocks(waf, 256), _blocks(wi[:, r0:r0 + 4 * W1], 512)]
    pf, pr_, wo = a["w_proj_fox"][0], a["w_proj_rwkv"][0], a["w_out"][0]
    parts.append(_blocks(wi[:, g0:g0 + 2 * D], 512))
    for q in range(4):
        s = slice(512 * q, 512 * q + 512)
        parts += [_blocks(pf[:, s], 512), _blocks(pr_[:, s], 512)]
    parts.append(_blocks(wo, 512))
    w2 = a["w_in_2"][0]
    lat = QR + KVR
    kr = w2[:, lat:lat + ROPE]
    parts += [_blocks(w2[:, 0:1024], 512), _blocks(w2[:, 1024:lat], 256), _blocks(np.concatenate([kr, kr], 1), 128)]
    s0 = lat + ROPE
    parts.append(_blocks(w2[:, s0:s0 + 2048 + 512], 512))
    parts.append(_blocks(w2[:, s0 + 2560:s0 + 2560 + 2 * D], 512))
    uq = a["w_uq_2"][0].reshape(QR, MLA_HEADS, 192)
    uq = np.concatenate([uq[:, :, :P].reshape(QR, -1), uq[:, :, P:].reshape(QR, -1)], 1)
    parts.append(_blocks(uq, 512))
    parts.append(_blocks(a["w_ukv_2"][0], 512))
    parts.append(_blocks(a["w_o_2"][0], 512))
    up = a["w_up_2"][0]
    for q in range(11):
        parts += [_blocks(up[:, 512 * q:512 * q + 512], 512), _blocks(up[:, D_FF + 512 * q:D_FF + 512 * q + 512], 512)]
    down = a["w_down_2"][0]
    parts.append(down.reshape(22, 2, P, 4, 512).transpose(0, 3, 2, 1, 4).reshape(-1, P, BLK))
    w = np.concatenate(parts, 0)
    assert w.shape == (NBLK, P, BLK), w.shape

    def pad(v):
        return np.concatenate([v.reshape(-1), np.zeros(P - v.size, f)])[:, None]

    mu = a["rwkv_shift_mix"][0]
    v = {
        "g1": _cols(a["norm_gain"], 16), "mu": _cols(mu[:4 * W1], 32), "mu_w": pad(mu[4 * W1:4 * W1 + LORA]),
        "mu_a": pad(mu[4 * W1 + LORA:]), "fbias": pad(a["fox_forget_bias"]), "w0": _cols(a["rwkv_w0"], 8),
        "a0": _cols(a["rwkv_a0"], 8), "k_k": _cols(a["rwkv_k_k"], 8), "k_a": _cols(a["rwkv_k_a"], 8),
        "r_k": _cols(a["rwkv_r_k"], 8), "ln_w": _cols(a["rwkv_ln_w"], 8), "ln_b": _cols(a["rwkv_ln_b"], 8),
        "gf": _cols(a["final_norm_gain"], 16), "c": _cols(a["c_2"], 16), "b_ada": _cols(a["b_ada_2"], 96),
        "g_pre_mix": _cols(a["g_pre_mix_2"], 16), "g_post_mix": _cols(a["g_post_mix_2"], 16),
        "g_q": _cols(a["g_q_lat_2"], 6), "g_kv": _cols(a["g_kv_lat_2"], 4),
        "sinks": np.repeat(a["sinks_2"].reshape(1, -1), P, 0), "g_pre_ffn": _cols(a["g_pre_ffn_2"], 16),
        "g_post_ffn": _cols(a["g_post_ffn_2"], 16),
        "conv_w": np.concatenate([_cols(a["conv_w_2"][0, j], 88) for j in range(3)], 1),
        "conv_b": _cols(a["conv_b_2"], 88),
    }
    c1, c2 = constants()
    tiled = np.ascontiguousarray(a["x"][0].T.reshape(DT, P, T).transpose(1, 0, 2).reshape(P, DT * T))
    return {
        "x": tiled, "w": w, "vec": np.ascontiguousarray(np.concatenate([v[n] for n in VEC], 1)),
        "con1": c1, "con2": c2,
        "lora": np.ascontiguousarray(np.stack([a["rwkv_w2"][0], a["rwkv_a2"][0]], 1).reshape(LORA, 2, WT, P)
                                     .transpose(2, 0, 1, 3).reshape(WT, LORA, 2 * P)[list(range(WT)) + [0]]),
        "rel": np.ascontiguousarray(np.concatenate([a["rel_bias_2"], np.zeros((BUCKETS, 4), f)], 1)),
        "ada": np.concatenate([a["w_ada_2"][0].reshape(DT, P, 12, 1024).transpose(2, 0, 1, 3).reshape(-1, P, 1024),
                               np.zeros((2, P, 1024), f)], 0),
    }


def kernel(**inputs):
    import concourse.bacc as bacc
    from concourse.bass_utils import run_bass_kernel_spmd

    nc = bacc.Bacc("TRN2", target_bir_lowering=False, num_devices=1)
    arrays = _layout({n: np.asarray(v) for n, v in inputs.items()})
    ins = {n: nc.dram_tensor(f"in_{n}", v.shape, F32, kind="ExternalInput").ap() for n, v in arrays.items()}
    out = nc.dram_tensor("out_x", (P, DT * T), F32, kind="ExternalOutput").ap()
    build(nc, ins, out)
    r = run_bass_kernel_spmd(nc, [{f"in_{n}": v for n, v in arrays.items()}], core_ids=[0])
    y = r.results[0]["out_x"]
    return np.ascontiguousarray(y.reshape(P, DT, T).transpose(1, 0, 2).reshape(D, T).T)[None]
```
